# Optimizing a Trainium2 kernel written in Bass

```python
import math
import jax, jax.numpy as jnp
from jax import lax
import numpy as np

D_MODEL = 1024
BATCH = 1
SEQ = 1024
DEPTH = 1

HEAD_DIM = 64
A_Q_HEADS = 8
A_KV_HEADS = 2
A_WIDTH = A_Q_HEADS * HEAD_DIM
A_KV_WIDTH = A_KV_HEADS * HEAD_DIM
WINDOW = 128
BLOCK = 128
B_WIDTH = 256
B_BLOCKS = 4
B_BLOCK_DIM = B_WIDTH // B_BLOCKS
CONV_WIDTH = 4
LRU_C = 8.0
C_HEADS = 4
C_WIDTH = C_HEADS * HEAD_DIM
DECAY_RANK = 32
AICL_RANK = 32
VRES_RANK = 16
C_SHIFT_WIDTH = 3 * C_WIDTH + DECAY_RANK + AICL_RANK
GN_EPS = 64e-5

D_MIX = A_WIDTH + B_WIDTH + C_WIDTH
SPLIT_SIZES = (A_WIDTH, A_KV_WIDTH, A_KV_WIDTH, A_WIDTH,
               B_WIDTH, B_WIDTH,
               C_SHIFT_WIDTH, C_WIDTH)
D_IN = sum(SPLIT_SIZES)
LN_EPS = 1e-5
ALPHA = (2 * DEPTH) ** 0.25
BETA = (8 * DEPTH) ** -0.25


def _layer_norm(x, g, b):
    xf = x.astype(jnp.float32)
    mu = jnp.mean(xf, axis=-1, keepdims=True)
    var = jnp.mean(jnp.square(xf - mu), axis=-1, keepdims=True)
    return (xf - mu) * lax.rsqrt(var + LN_EPS) * g + b

def _swa_sinks(q, k, v, sinks):
    bsz, seq = q.shape[0], q.shape[1]
    nb = seq // BLOCK
    grp = A_Q_HEADS // A_KV_HEADS
    qb = q.astype(jnp.float32).reshape(bsz, nb, BLOCK, A_KV_HEADS, grp, HEAD_DIM) * (HEAD_DIM ** -0.5)

    def band(t):
        t = t.astype(jnp.float32).reshape(bsz, seq, A_KV_HEADS, HEAD_DIM)
        prev = jnp.pad(t, ((0, 0), (BLOCK, 0), (0, 0), (0, 0)))[:, :seq]
        prev = prev.reshape(bsz, nb, BLOCK, A_KV_HEADS, HEAD_DIM)
        cur = t.reshape(bsz, nb, BLOCK, A_KV_HEADS, HEAD_DIM)
        return jnp.concatenate([prev, cur], axis=2)

    kb, vb = band(k), band(v)
    s = jnp.einsum("bnqhgd,bnkhd->bnhgqk", qb, kb)
    qi = jnp.arange(BLOCK)[:, None]
    kj = jnp.arange(2 * BLOCK)[None, :]
    diff = qi + BLOCK - kj
    band_mask = (diff >= 0) & (diff < WINDOW)
    key_pos = jnp.arange(nb)[:, None] * BLOCK - BLOCK + jnp.arange(2 * BLOCK)[None, :]
    mask = band_mask[None] & (key_pos >= 0)[:, None, :]
    s = jnp.where(mask[None, :, None, None], s, -jnp.inf)
    sink = sinks.astype(jnp.float32).reshape(A_KV_HEADS, grp)[None, None, :, :, None, None]
    m = jnp.maximum(jnp.max(s, axis=-1, keepdims=True), sink)
    p = jnp.exp(s - m)
    denom = jnp.sum(p, axis=-1, keepdims=True) + jnp.exp(sink - m)
    o = jnp.einsum("bnhgqk,bnkhd->bnqhgd", p / denom, vb)
    return o.reshape(bsz, seq, A_WIDTH)

def _rg_lru(xb, conv_w, conv_b, wa, ba, wx, bx, lam):
    bsz, seq = xb.shape[0], xb.shape[1]
    xf = xb.astype(jnp.float32)
    xc = lax.conv_general_dilated(
        xf, conv_w.astype(jnp.float32).reshape(CONV_WIDTH, 1, B_WIDTH),
        window_strides=(1,), padding=[(CONV_WIDTH - 1, 0)],
        dimension_numbers=("NWC", "WIO", "NWC"), feature_group_count=B_WIDTH) + conv_b
    xh = xc.reshape(bsz, seq, B_BLOCKS, B_BLOCK_DIM)
    r = jax.nn.sigmoid(jnp.einsum("bsnd,nde->bsne", xh, wa).reshape(bsz, seq, B_WIDTH) + ba)
    i = jax.nn.sigmoid(jnp.einsum("bsnd,nde->bsne", xh, wx).reshape(bsz, seq, B_WIDTH) + bx)
    log_a = -LRU_C * r * jax.nn.softplus(-lam.astype(jnp.float32))
    a = jnp.exp(log_a)
    u = jnp.sqrt(-jnp.expm1(2.0 * log_a)) * (i * xc)

    def combine(e1, e2):
        a1, b1 = e1
        a2, b2 = e2
        return a1 * a2, a2 * b1 + b2

    _, h = lax.associative_scan(combine, (a, u), axis=1)
    return h

def _rwkv7(cs, mu, w0, w2, a0, a2, k_k, k_a, r_k, gn_w, gn_b, vres):
    bsz, seq = cs.shape[0], cs.shape[1]
    cs = cs.astype(jnp.float32)
    prev = jnp.pad(cs, ((0, 0), (1, 0), (0, 0)))[:, :seq]
    xs = cs + (prev - cs) * mu
    r, k, v, wl, al = jnp.split(xs, [C_WIDTH, 2 * C_WIDTH, 3 * C_WIDTH, 3 * C_WIDTH + DECAY_RANK], axis=-1)
    logw = -jax.nn.softplus(-(w0 + jnp.tanh(wl) @ w2)) - 0.5
    decay = jnp.exp(-jnp.exp(logw))
    a = jax.nn.sigmoid(a0 + al @ a2)
    v_own = v
    if vres is not None:
        v_first, v0, v1, v2 = vres
        v = v + (v_first - v) * jax.nn.sigmoid(v0 + (v @ v1) @ v2)

    def heads(t):
        return t.reshape(bsz, seq, C_HEADS, HEAD_DIM)

    kk = heads(k * k_k)
    kk = kk * lax.rsqrt(jnp.sum(jnp.square(kk), axis=-1, keepdims=True) + 1e-12)
    k = k * (1.0 + (a - 1.0) * k_a)
    rh, wh, kh, vh, ah = heads(r), heads(decay), heads(k), heads(v), heads(a)
    bh = kk * ah

    def step(state, inp):
        r_t, w_t, k_t, v_t, kk_t, b_t = inp
        sa = jnp.einsum("bhvk,bhk->bhv", state, -kk_t)
        state = (state * w_t[:, :, None, :] + sa[..., None] * b_t[:, :, None, :]
                 + v_t[..., None] * k_t[:, :, None, :])
        y_t = jnp.einsum("bhvk,bhk->bhv", state, r_t)
        return state, y_t

    tm = lambda t: jnp.swapaxes(t, 0, 1)
    s0 = jnp.zeros((bsz, C_HEADS, HEAD_DIM, HEAD_DIM), jnp.float32)
    _, y = lax.scan(step, s0, (tm(rh), tm(wh), tm(kh), tm(vh), tm(kk), tm(bh)))
    y = tm(y)
    ym = jnp.mean(y, axis=-1, keepdims=True)
    yv = jnp.mean(jnp.square(y - ym), axis=-1, keepdims=True)
    y = (y - ym) * lax.rsqrt(yv + GN_EPS) * gn_w.reshape(C_HEADS, HEAD_DIM) + gn_b.reshape(C_HEADS, HEAD_DIM)
    bonus = jnp.sum(rh * kh * r_k, axis=-1, keepdims=True) * vh
    return (y + bonus).reshape(bsz, seq, C_WIDTH), v_own

def first_inputs(seed: int = 0) -> dict:
    key = jax.random.key(seed)
    ks = jax.random.split(key, 32)
    n = lambda i, shape: jax.random.normal(ks[i], shape, jnp.float32)
    u_lru = jax.random.uniform(ks[11], (DEPTH, B_WIDTH), jnp.float32, 0.9, 0.999)
    a_base = u_lru ** (1.0 / LRU_C)
    w0_base = jnp.linspace(-6.0, -1.0, C_WIDTH, dtype=jnp.float32)[None, :]
    return {
        "x": n(0, (BATCH, SEQ, D_MODEL)),
        "w_in": n(1, (DEPTH, D_MODEL, D_IN)) * D_MODEL ** -0.5,
        "w_out": n(2, (DEPTH, D_MIX, D_MODEL)) * (D_MIX ** -0.5) * BETA,
        "ln_g": 1.0 + 0.02 * n(3, (DEPTH, D_MODEL)),
        "ln_b": 0.02 * n(4, (DEPTH, D_MODEL)),
        "attn_sinks": 0.5 * n(5, (DEPTH, A_Q_HEADS)),
        "conv_w": n(6, (DEPTH, CONV_WIDTH, B_WIDTH)) * CONV_WIDTH ** -0.5,
        "conv_b": 0.02 * n(7, (DEPTH, B_WIDTH)),
        "lru_wa": n(8, (DEPTH, B_BLOCKS, B_BLOCK_DIM, B_BLOCK_DIM)) * B_BLOCK_DIM ** -0.5,
        "lru_ba": 0.02 * n(9, (DEPTH, B_WIDTH)),
        "lru_wx": n(10, (DEPTH, B_BLOCKS, B_BLOCK_DIM, B_BLOCK_DIM)) * B_BLOCK_DIM ** -0.5,
        "lru_bx": 0.02 * n(12, (DEPTH, B_WIDTH)),
        "lru_lambda": jnp.log(a_base) - jnp.log1p(-a_base),
        "rwkv_mu": jax.random.uniform(ks[13], (DEPTH, C_SHIFT_WIDTH), jnp.float32),
        "rwkv_w0": w0_base + 0.1 * n(14, (DEPTH, C_WIDTH)),
        "rwkv_w2": 0.1 * n(15, (DEPTH, DECAY_RANK, C_WIDTH)),
        "rwkv_a0": 0.1 * n(16, (DEPTH, C_WIDTH)),
        "rwkv_a2": 0.1 * n(17, (DEPTH, AICL_RANK, C_WIDTH)),
        "rwkv_kk": 0.85 + 0.02 * n(18, (DEPTH, C_WIDTH)),
        "rwkv_ka": 1.0 + 0.02 * n(19, (DEPTH, C_WIDTH)),
        "rwkv_rk": -0.04 + 0.02 * n(20, (DEPTH, C_HEADS, HEAD_DIM)),
        "rwkv_gn_w": 1.0 + 0.02 * n(21, (DEPTH, C_WIDTH)),
        "rwkv_gn_b": 0.02 * n(22, (DEPTH, C_WIDTH)),
        "rwkv_v0": 1.0 + 0.1 * n(23, (DEPTH - 1, C_WIDTH)),
        "rwkv_v1": n(24, (DEPTH - 1, C_WIDTH, VRES_RANK)) * C_WIDTH ** -0.5,
        "rwkv_v2": 0.1 * n(25, (DEPTH - 1, VRES_RANK, C_WIDTH)),
    }

def first_block(x, w_in, w_out, ln_g, ln_b, attn_sinks, conv_w, conv_b, lru_wa, lru_ba,
              lru_wx, lru_bx, lru_lambda, rwkv_mu, rwkv_w0, rwkv_w2, rwkv_a0, rwkv_a2,
              rwkv_kk, rwkv_ka, rwkv_rk, rwkv_gn_w, rwkv_gn_b, rwkv_v0, rwkv_v1, rwkv_v2):
    split_idx = [int(c) for c in np.cumsum(SPLIT_SIZES)[:-1]]
    v_first = None
    for l in range(DEPTH):
        proj = jnp.einsum("bsd,de->bse", x, w_in[l])
        q, k, v, g_a, x_b, g_b, c_cols, g_c = jnp.split(proj, split_idx, axis=-1)
        y_a = _swa_sinks(q, k, v, attn_sinks[l])
        y_b = _rg_lru(x_b, conv_w[l], conv_b[l], lru_wa[l], lru_ba[l], lru_wx[l], lru_bx[l], lru_lambda[l])
        vres = None if l == 0 else (v_first, rwkv_v0[l - 1], rwkv_v1[l - 1], rwkv_v2[l - 1])
        y_c, v_own = _rwkv7(c_cols, rwkv_mu[l], rwkv_w0[l], rwkv_w2[l], rwkv_a0[l], rwkv_a2[l],
                            rwkv_kk[l], rwkv_ka[l], rwkv_rk[l], rwkv_gn_w[l], rwkv_gn_b[l], vres)
        if l == 0:
            v_first = v_own
        silu = lambda t: jax.nn.silu(t.astype(jnp.float32))
        y = jnp.concatenate([y_a * silu(g_a), y_b * silu(g_b), y_c * silu(g_c)], axis=-1)
        out = jnp.einsum("bse,ed->bsd", y, w_out[l])
        x = _layer_norm(ALPHA * x.astype(jnp.float32) + out, ln_g[l], ln_b[l]).astype(x.dtype)
    return x


_first_inputs = first_inputs


def first_inputs(seed=0):
    import zlib

    import numpy as np

    out = dict(_first_inputs(seed))
    spreads = {}
    factors = {'ln_g': 3.001,
     'ln_b': 2.876,
     'attn_sinks': 8.0,
     'conv_b': 3.874,
     'lru_ba': 8.0,
     'lru_bx': 8.0,
     'rwkv_w2': 8.0,
     'rwkv_a0': 8.0,
     'rwkv_kk': 8.0,
     'rwkv_ka': 8.0,
     'rwkv_rk': 8.0,
     'rwkv_gn_w': 8.0,
     'rwkv_gn_b': 8.0}
    for name, (base, spread) in spreads.items():
        noise = np.random.default_rng([zlib.crc32(name.encode()), seed]).standard_normal(out[name].shape)
        drawn = base * np.exp(spread * noise) if base else spread * noise
        out[name] = __import__('jax').numpy.asarray(drawn.astype(out[name].dtype))
    for name, factor in factors.items():
        out[name] = (out[name] * factor).astype(out[name].dtype)
    return out


_narrow_inputs = first_inputs


def first_inputs(seed=0):

    out = dict(_narrow_inputs(seed))
    wider = {'ln_g': 3.38,
     'ln_b': 3.38,
     'attn_sinks': 9.41,
     'lru_ba': 12.0,
     'lru_bx': 12.0,
     'rwkv_kk': 10.69,
     'rwkv_ka': 3.1,
     'rwkv_gn_w': 4.38,
     'rwkv_gn_b': 4.66}
    for name, times in wider.items():
        mean = out[name].mean()
        out[name] = (mean + times * (out[name] - mean)).astype(out[name].dtype)
    return out


DEPTH_2 = 2

N_A = DEPTH_2 // 2
N_B = DEPTH_2 - N_A
N_META = 16
POOL_WINDOWS = (2, 4, 8, 16)
N_POOL_GROUPS = len(POOL_WINDOWS)
POOL_GROUP_DIM = D_MODEL // N_POOL_GROUPS
MAX_WINDOW = max(POOL_WINDOWS)
N_HEADS = 8
QK_NOPE_DIM = 128
QK_ROPE_DIM = 64
V_HEAD_DIM = 128
Q_LORA_RANK = 384
KV_LORA_RANK = 256
ROPE_THETA = 10000.0
ATTN_SCALE = (QK_NOPE_DIM + QK_ROPE_DIM) ** -0.5
Q_BLOCK = 128
N_EXPERT_GROUPS = 4
EXPERTS_PER_GROUP = 8
N_EXPERTS = N_EXPERT_GROUPS * EXPERTS_PER_GROUP
TOP_K_IN_GROUP = 2
D_EXPERT = 256
MOE_GROUP_ROWS = 256
RMS_EPS = 1e-6
NEG_INF = -1e30


def rmsnorm(x, g):
    xf = x.astype(jnp.float32)
    y = xf * lax.rsqrt(jnp.mean(xf * xf, axis=-1, keepdims=True) + RMS_EPS)
    return (y * g.astype(jnp.float32)).astype(x.dtype)

def rope_tables(length):
    pos = jnp.arange(length, dtype=jnp.float32)
    inv_freq = ROPE_THETA ** (-jnp.arange(0, QK_ROPE_DIM, 2, dtype=jnp.float32) / QK_ROPE_DIM)
    ang = pos[:, None] * inv_freq[None, :]
    return jnp.cos(ang), jnp.sin(ang)

def apply_rope(x, cos, sin):
    xf = x.astype(jnp.float32)
    half = xf.shape[-1] // 2
    x1, x2 = xf[..., :half], xf[..., half:]
    return jnp.concatenate([x1 * cos - x2 * sin, x1 * sin + x2 * cos], axis=-1).astype(x.dtype)

def pool_mixer(h, w_grp, scale):
    L_ = h.shape[1]
    hf = h.astype(jnp.float32)
    cs = jnp.pad(jnp.cumsum(hf, axis=1), ((0, 0), (MAX_WINDOW, 0), (0, 0)))
    t = jnp.arange(L_)
    outs = []
    for g, w in enumerate(POOL_WINDOWS):
        sl = slice(g * POOL_GROUP_DIM, (g + 1) * POOL_GROUP_DIM)
        win_sum = cs[:, MAX_WINDOW:, sl] - cs[:, MAX_WINDOW - w:MAX_WINDOW - w + L_, sl]
        cnt = jnp.minimum(t + 1, w).astype(jnp.float32)[None, :, None]
        pooled = (win_sum / cnt - hf[:, :, sl]).astype(h.dtype)
        outs.append(jnp.einsum('blc,cd->bld', pooled, w_grp[g]))
    return jnp.concatenate(outs, axis=-1) * scale

def shared_latent_kv(h, kv_norm, w_dkv, kv_lat_norm, w_uk, w_uv, cos, sin):
    c = jnp.einsum('bld,dr->blr', rmsnorm(h, kv_norm), w_dkv)
    c_kv = rmsnorm(c[..., :KV_LORA_RANK], kv_lat_norm)
    k_rope = apply_rope(c[..., KV_LORA_RANK:], cos, sin)
    k_nope = jnp.einsum('blr,rhd->blhd', c_kv, w_uk)
    v = jnp.einsum('blr,rhd->blhd', c_kv, w_uv)
    return k_nope, k_rope, v

def causal_block_attention(q_nope, q_rope, k_nope, k_rope, v):
    B_, L_, H_, _ = q_nope.shape
    nb = -(-L_ // Q_BLOCK)
    Lp = nb * Q_BLOCK
    pad = Lp - L_
    padf = lambda a: jnp.pad(a, [(0, 0), (0, pad)] + [(0, 0)] * (a.ndim - 2))
    qn, qr, kn, kr, vv = padf(q_nope), padf(q_rope), padf(k_nope), padf(k_rope), padf(v)
    to_blocks = lambda a: jnp.moveaxis(a.reshape((B_, nb, Q_BLOCK) + a.shape[2:]), 1, 0)
    kpos = jnp.arange(Lp)

    def one_block(args):
        qn_b, qr_b, b_idx = args
        s = (jnp.einsum('bqhd,bkhd->bhqk', qn_b, kn, preferred_element_type=jnp.float32)
             + jnp.einsum('bqhr,bkr->bhqk', qr_b, kr, preferred_element_type=jnp.float32)) * ATTN_SCALE
        qpos = b_idx * Q_BLOCK + jnp.arange(Q_BLOCK)
        s = jnp.where(kpos[None, :] <= qpos[:, None], s, NEG_INF)
        p = jax.nn.softmax(s, axis=-1)
        return jnp.einsum('bhqk,bkhd->bqhd', p.astype(vv.dtype), vv)

    o = lax.map(one_block, (to_blocks(qn), to_blocks(qr), jnp.arange(nb)))
    return jnp.moveaxis(o, 0, 1).reshape(B_, Lp, H_, V_HEAD_DIM)[:, :L_]

def mla_mixer(hn, w_dq, q_norm, w_uq, w_o, k_nope, k_rope, v, cos, sin):
    B_, L_, _ = hn.shape
    cq = rmsnorm(jnp.einsum('bld,dr->blr', hn, w_dq), q_norm)
    q = jnp.einsum('blr,rhd->blhd', cq, w_uq)
    q_nope = q[..., :QK_NOPE_DIM]
    q_rope = apply_rope(q[..., QK_NOPE_DIM:], cos[:, None, :], sin[:, None, :])
    o = causal_block_attention(q_nope, q_rope, k_nope, k_rope, v)
    return jnp.einsum('blf,fd->bld', o.reshape(B_, L_, N_HEADS * V_HEAD_DIM), w_o)

def hierarchical_moe(h, wr_g, br_g, wr_e, br_e, w_gate, w_up, w_down):
    B_, L_, D_ = h.shape
    xt = h.reshape(-1, D_)
    n_tok = xt.shape[0]
    xf = xt.astype(jnp.float32)
    p_g = jax.nn.softmax(xf @ wr_g.astype(jnp.float32) + br_g.astype(jnp.float32), axis=-1)
    g_sel = jnp.argmax(p_g, axis=-1)
    w_g = jnp.max(p_g, axis=-1)
    logit_e = (xf @ wr_e.astype(jnp.float32) + br_e.astype(jnp.float32)).reshape(n_tok, N_EXPERT_GROUPS, EXPERTS_PER_GROUP)
    sel = jnp.take_along_axis(logit_e, g_sel[:, None, None], axis=1)[:, 0]
    top_v, top_i = lax.top_k(sel, TOP_K_IN_GROUP)
    gate = w_g[:, None] * jax.nn.softmax(top_v, axis=-1)
    eid = (g_sel[:, None] * EXPERTS_PER_GROUP + top_i).reshape(-1).astype(jnp.int32)
    tid = jnp.repeat(jnp.arange(n_tok, dtype=jnp.int32), TOP_K_IN_GROUP)
    wt = gate.reshape(-1)
    n_assign = n_tok * TOP_K_IN_GROUP
    order = jnp.argsort(eid)
    e_sorted = eid[order]
    counts = jnp.bincount(eid, length=N_EXPERTS)
    starts = jnp.cumsum(counts) - counts
    padded = (counts + MOE_GROUP_ROWS - 1) // MOE_GROUP_ROWS * MOE_GROUP_ROWS
    pends = jnp.cumsum(padded)
    pstarts = pends - padded
    dest = pstarts[e_sorted] + (jnp.arange(n_assign) - starts[e_sorted])
    n_blocks = -(-(n_assign + N_EXPERTS * (MOE_GROUP_ROWS - 1)) // MOE_GROUP_ROWS)
    n_rows = n_blocks * MOE_GROUP_ROWS
    row_tok = jnp.full((n_rows,), n_tok, jnp.int32).at[dest].set(tid[order])
    row_w = jnp.zeros((n_rows,), h.dtype).at[dest].set(wt[order].astype(h.dtype))
    block_e = jnp.minimum(jnp.searchsorted(pends, jnp.arange(n_blocks) * MOE_GROUP_ROWS, side='right'), N_EXPERTS - 1)
    x_rows = jnp.concatenate([xt, jnp.zeros((1, D_), xt.dtype)], axis=0)[row_tok]
    x_rows = x_rows.reshape(n_blocks, MOE_GROUP_ROWS, D_)

    def expert_block(args):
        e, xb = args
        return (jax.nn.silu(xb @ w_gate[e]) * (xb @ w_up[e])) @ w_down[e]

    y = lax.map(expert_block, (block_e, x_rows)).reshape(n_rows, D_)
    out = jnp.zeros((n_tok + 1, D_), h.dtype).at[row_tok].add(y * row_w[:, None])[:n_tok]
    return out.reshape(B_, L_, D_)

def second_inputs(seed: int = 0) -> dict:
    key = jax.random.key(seed)
    ks = jax.random.split(key, 32)
    f32 = jnp.float32
    nrm = lambda k, shape, fan: jax.random.normal(k, shape, f32) * (fan ** -0.5)
    gain = lambda k, shape: 1.0 + 0.05 * jax.random.normal(k, shape, f32)
    return {
        "x": jax.random.normal(ks[0], (BATCH, SEQ, D_MODEL), f32),
        "meta_tokens": jax.random.normal(ks[1], (N_META, D_MODEL), f32),
        "a_norm": gain(ks[2], (N_A, D_MODEL)),
        "a_w": nrm(ks[3], (N_A, N_POOL_GROUPS, POOL_GROUP_DIM, POOL_GROUP_DIM), POOL_GROUP_DIM),
        "a_scale": gain(ks[4], (N_A, D_MODEL)),
        "b_norm": gain(ks[5], (N_B, D_MODEL)),
        "b_w_dq": nrm(ks[6], (N_B, D_MODEL, Q_LORA_RANK), D_MODEL),
        "b_q_norm": gain(ks[7], (N_B, Q_LORA_RANK)),
        "b_w_uq": nrm(ks[8], (N_B, Q_LORA_RANK, N_HEADS, QK_NOPE_DIM + QK_ROPE_DIM), Q_LORA_RANK),
        "b_w_o": nrm(ks[9], (N_B, N_HEADS * V_HEAD_DIM, D_MODEL), N_HEADS * V_HEAD_DIM),
        "kv_norm": gain(ks[10], (D_MODEL,)),
        "w_dkv": nrm(ks[11], (D_MODEL, KV_LORA_RANK + QK_ROPE_DIM), D_MODEL),
        "kv_lat_norm": gain(ks[12], (KV_LORA_RANK,)),
        "w_uk": nrm(ks[13], (KV_LORA_RANK, N_HEADS, QK_NOPE_DIM), KV_LORA_RANK),
        "w_uv": nrm(ks[14], (KV_LORA_RANK, N_HEADS, V_HEAD_DIM), KV_LORA_RANK),
        "ffn_norm": gain(ks[15], (DEPTH_2, D_MODEL)),
        "router_g": nrm(ks[16], (DEPTH_2, D_MODEL, N_EXPERT_GROUPS), D_MODEL),
        "router_g_bias": 0.01 * jax.random.normal(ks[17], (DEPTH_2, N_EXPERT_GROUPS), f32),
        "router_e": nrm(ks[18], (DEPTH_2, D_MODEL, N_EXPERTS), D_MODEL),
        "router_e_bias": 0.01 * jax.random.normal(ks[19], (DEPTH_2, N_EXPERTS), f32),
        "w_gate": nrm(ks[20], (DEPTH_2, N_EXPERTS, D_MODEL, D_EXPERT), D_MODEL),
        "w_up": nrm(ks[21], (DEPTH_2, N_EXPERTS, D_MODEL, D_EXPERT), D_MODEL),
        "w_down": nrm(ks[22], (DEPTH_2, N_EXPERTS, D_EXPERT, D_MODEL), D_EXPERT),
        "final_norm": gain(ks[23], (D_MODEL,)),
    }

def second_block(x, meta_tokens, a_norm, a_w, a_scale, b_norm, b_w_dq, b_q_norm, b_w_uq, b_w_o,
              kv_norm, w_dkv, kv_lat_norm, w_uk, w_uv, ffn_norm, router_g, router_g_bias,
              router_e, router_e_bias, w_gate, w_up, w_down, final_norm):
    B_, S_, D_ = x.shape
    h = jnp.concatenate([jnp.broadcast_to(meta_tokens[None].astype(x.dtype), (B_, N_META, D_)), x], axis=1)
    L_ = S_ + N_META
    cos, sin = rope_tables(L_)
    k_nope = k_rope = v = None
    for layer in range(DEPTH_2):
        if layer < N_A:
            i = layer
            h = h + pool_mixer(rmsnorm(h, a_norm[i]), a_w[i], a_scale[i])
        else:
            i = layer - N_A
            h = h + mla_mixer(rmsnorm(h, b_norm[i]), b_w_dq[i], b_q_norm[i], b_w_uq[i], b_w_o[i],
                              k_nope, k_rope, v, cos, sin)
        h = h + hierarchical_moe(rmsnorm(h, ffn_norm[layer]), router_g[layer], router_g_bias[layer],
                                 router_e[layer], router_e_bias[layer], w_gate[layer], w_up[layer], w_down[layer])
        if layer == N_A - 1:
            k_nope, k_rope, v = shared_latent_kv(h, kv_norm, w_dkv, kv_lat_norm, w_uk, w_uv, cos, sin)
    return rmsnorm(h, final_norm)[:, N_META:]


def setup_inputs(seed=0):
    out = dict(first_inputs(seed))
    for name, value in second_inputs(seed + 1).items():
        if name != "x":
            out[name + "_2"] = value
    return out


def reference(
    x, w_in, w_out, ln_g, ln_b, attn_sinks, conv_w, conv_b, lru_wa, lru_ba, lru_wx, lru_bx,
    lru_lambda, rwkv_mu, rwkv_w0, rwkv_w2, rwkv_a0, rwkv_a2, rwkv_kk, rwkv_ka, rwkv_rk,
    rwkv_gn_w, rwkv_gn_b, rwkv_v0, rwkv_v1, rwkv_v2, meta_tokens_2, a_norm_2, a_w_2, a_scale_2,
    b_norm_2, b_w_dq_2, b_q_norm_2, b_w_uq_2, b_w_o_2, kv_norm_2, w_dkv_2, kv_lat_norm_2,
    w_uk_2, w_uv_2, ffn_norm_2, router_g_2, router_g_bias_2, router_e_2, router_e_bias_2,
    w_gate_2, w_up_2, w_down_2, final_norm_2,
):
    x = first_block(
        x, w_in, w_out, ln_g, ln_b, attn_sinks, conv_w, conv_b, lru_wa, lru_ba, lru_wx, lru_bx,
        lru_lambda, rwkv_mu, rwkv_w0, rwkv_w2, rwkv_a0, rwkv_a2, rwkv_kk, rwkv_ka, rwkv_rk,
        rwkv_gn_w, rwkv_gn_b, rwkv_v0, rwkv_v1, rwkv_v2,
    )
    return second_block(
        x, meta_tokens_2, a_norm_2, a_w_2, a_scale_2, b_norm_2, b_w_dq_2, b_q_norm_2, b_w_uq_2,
        b_w_o_2, kv_norm_2, w_dkv_2, kv_lat_norm_2, w_uk_2, w_uv_2, ffn_norm_2, router_g_2,
        router_g_bias_2, router_e_2, router_e_bias_2, w_gate_2, w_up_2, w_down_2, final_norm_2,
    )


_drawn_inputs = setup_inputs


def setup_inputs(seed=0):
    import zlib

    import numpy as np

    out = dict(_drawn_inputs(seed))
    spreads = {}
    factors = {'attn_sinks': 3.326,
     'meta_tokens_2': 3.48,
     'a_norm_2': 3.158,
     'a_scale_2': 3.119,
     'b_norm_2': 8.0,
     'b_q_norm_2': 8.0,
     'kv_norm_2': 8.0,
     'kv_lat_norm_2': 8.0,
     'router_g_bias_2': 22.047,
     'router_e_bias_2': 6.861}
    for name, (base, spread) in spreads.items():
        noise = np.random.default_rng([zlib.crc32(name.encode()), seed]).standard_normal(out[name].shape)
        drawn = base * np.exp(spread * noise) if base else spread * noise
        out[name] = __import__('jax').numpy.asarray(drawn.astype(out[name].dtype))
    for name, factor in factors.items():
        out[name] = (out[name] * factor).astype(out[name].dtype)
    return out
```

```python
from contextlib import ExitStack

import numpy as np

import concourse.bass as bass
from concourse import mybir

F32 = mybir.dt.float32
BF16 = mybir.dt.bfloat16
I32 = mybir.dt.int32
U32 = mybir.dt.uint32
ALU = mybir.AluOpType
ACT = mybir.ActivationFunctionType
AX = mybir.AxisListType

P = 128
D = 1024
KD = D // P
T = 1024
NT = T // P
HD = 64
AH, AKV = 8, 2
C_LRU = 8.0
LN_EPS, GN_EPS, RMS_EPS = 1e-5, 64e-5, 1e-6
ALPHA = 2.0 ** 0.25
EXP_HALF = float(np.exp(-0.5))
CH = 64

N_META = 16
L = T + N_META
NS = NT + 1
WINDOWS = (2, 4, 8, 16)
PADW = max(WINDOWS)
MH, NOPE, ROPE, VH = 8, 128, 64, 128
QL, KVL = 384, 256
SCALE = (NOPE + ROPE) ** -0.5
NEG = -1e30
NG, EPG = 4, 8
NE = NG * EPG
DE = 256
NOV = (2 * L) // P
NBLK = NE + NOV
SLOTS = NBLK * P

SLOT = [(N_META + P * s, P) for s in range(NT)] + [(0, N_META)]

GROUPS = [("q", 0, 512), ("kv", 512, 256), ("ga", 768, 512), ("lru", 1280, 512),
          ("rk", 1792, 512), ("vwa", 2304, 320), ("gc", 2624, 256)]

CHAN = [("conv_w", 8), ("conv_b", 2), ("lru_ba", 2), ("lru_bx", 2), ("lam", 2), ("mu", 6), ("mu_wa", 1),
        ("w0", 2), ("a0", 2), ("k_k", 2), ("k_a", 2), ("r_k", 2), ("gn_w", 2), ("gn_b", 2),
        ("a_norm", 8), ("kv_norm", 8), ("b_norm", 8), ("q_norm", 3), ("kv_lat", 2)]
CHAN_AT, _n = {}, 0
for _name, _w in CHAN:
    CHAN_AT[_name] = _n
    _n += _w
N_CHAN = _n
DUMPS = {}
ROWS = ["ln_g", "ln_b", "a_scale", "ffn0", "ffn1", "final"]


class Mark:

    def __init__(self, sem, value):
        self.sem, self.value = sem, value


class Lane:

    def __init__(self, engine, new_sem, name):
        self.e, self.new_sem, self.name = engine, new_sem, name
        self.queue, self.waited = [], {}
        self.sem, self.count = None, 0

    def stage(self, name):
        if self.count or self.sem is None:
            self.sem = self.new_sem(f"{self.name}_{name}")
        self.count = 0

    def last(self):
        return Mark(self.sem, self.count) if self.count else None

    def wait(self, marks):
        for m in marks:
            if m is None:
                continue
            if isinstance(m, (list, tuple)):
                self.wait(m)
            elif self.waited.get(m.sem, 0) < m.value:
                self.waited[m.sem] = m.value
                self.queue.append(lambda m=m: self.e.wait_ge(m.sem, m.value))

    def do(self, make, *after):
        self.wait(after)
        sem = self.sem
        self.queue.append(lambda: make().then_inc(sem, 1))
        self.count += 1
        return Mark(self.sem, self.count)

    def raw(self, make, *after):
        self.wait(after)
        self.queue.append(make)

    def dma(self, sem, out, in_, *after):
        self.wait(after)
        self.queue.append(lambda: self.e.dma_start(out, in_).then_inc(sem.sem, 16))
        return sem.next()

    def play(self, queue=None):
        for make in (self.queue if queue is None else queue):
            make()


class DmaSem:

    def __init__(self, sem):
        self.sem, self.value = sem, 0

    def next(self):
        self.value += 16
        return Mark(self.sem, self.value)


class Vec(Lane):

    def tt(self, out, a, b, op, *after):
        return self.do(lambda: self.e.tensor_tensor(out, a, b, op), *after)

    def ts(self, out, a, s1, s2, op0, op1, *after):
        if op1 is None:
            return self.do(lambda: self.e.tensor_scalar(out, a, s1, None, op0), *after)
        return self.do(lambda: self.e.tensor_scalar(out, a, s1, s2, op0, op1), *after)

    def stt(self, out, a, s, b, op0, op1, *after):
        return self.do(lambda: self.e.scalar_tensor_tensor(out=out, in0=a, scalar=s, in1=b, op0=op0, op1=op1), *after)

    def copy(self, out, a, *after):
        return self.do(lambda: self.e.tensor_copy(out, a), *after)

    def red(self, out, a, op, *after):
        return self.do(lambda: self.e.tensor_reduce(out, a, AX.X, op), *after)

    def recip(self, out, a, *after):
        return self.do(lambda: self.e.reciprocal(out, a), *after)

    def set(self, out, value, *after):
        return self.do(lambda: self.e.memset(out, value), *after)


class Act(Lane):

    def act(self, out, a, func, *after, bias=0.0, scale=1.0, accum=None):
        if accum is not None:
            return self.do(lambda: self.e.activation(out, a, func, bias=bias, scale=scale, accum_out=accum), *after)
        return self.do(lambda: self.e.activation(out, a, func, bias=bias, scale=scale), *after)

    def copy(self, out, a, *after, scale=1.0):
        return self.do(lambda: self.e.activation(out, a, ACT.Copy, bias=0.0, scale=scale), *after)


class Ten(Lane):

    def mms(self, products, *after):
        self.wait(after)
        sem = self.sem

        def make():
            for i, (out, lhsT, rhs, start, stop) in enumerate(products):
                if start is None:
                    ins = self.e.transpose(out, lhsT, rhs)
                else:
                    ins = self.e.matmul(out, lhsT, rhs, start=start, stop=stop, skip_group_check=True)
                if i == len(products) - 1:
                    ins.then_inc(sem, 1)
        self.queue.append(make)
        self.count += 1
        return Mark(self.sem, self.count)


class Buf:

    def __init__(self, ap, sem=None):
        self.ap, self.free, self.sem = ap, [], sem


class Ring:
    def __init__(self, bufs):
        self.bufs, self.at = bufs, 0

    def take(self):
        b = self.bufs[self.at % len(self.bufs)]
        self.at += 1
        return b


def bc_mid(ap, n):
    return ap.unsqueeze(1).to_broadcast([ap.shape[0], n, ap.shape[1]])


def bc_last(ap, n):
    return ap.unsqueeze(2).to_broadcast([ap.shape[0], ap.shape[1], n])


def build(nc, io, dumps):
    ctx = ExitStack()
    with ctx:
        def new_sem(name):
            return ctx.enter_context(nc.semaphore(name))

        def dsem(name):
            return DmaSem(new_sem("dma_" + name))

        PE = Ten(nc.tensor, new_sem, "pe")
        V = Vec(nc.vector, new_sem, "dve")
        G = Vec(nc.gpsimd, new_sem, "pool")
        S = Act(nc.scalar, new_sem, "act")
        SP = Lane(nc.sync, new_sem, "sp")
        lanes = [PE, V, G, S, SP]
        compute = [PE, V, G, S]

        def stage(name):
            for lane in compute:
                lane.stage(name)

        ARENA = 53000
        arena = ctx.enter_context(nc.sbuf_tensor("arena", [P, ARENA], F32))
        psum = ctx.enter_context(nc.psum_tensor("psum", [P, 8 * 512], F32))
        top = [0]

        def take(*dims):
            n = int(np.prod(dims))
            o = top[0]
            top[0] += n + (n % 2)
            assert top[0] <= ARENA, (top[0], dims)
            v = arena[:, o:o + n]
            if len(dims) == 2:
                v = v.rearrange("p (a b) -> p a b", a=dims[0])
            if len(dims) == 3:
                v = v.rearrange("p (a b c) -> p a b c", a=dims[0], b=dims[1])
            return v

        banks = [psum[:, 512 * i:512 * (i + 1)] for i in range(8)]
        psum_ring = Ring([Buf(b) for b in banks])
        marks_out = []
        xn_dram = nc.dram_tensor("xn_rows", (L, D), F32, kind="Internal").ap()
        y_dram = nc.dram_tensor("expert_rows", (SLOTS, D), F32, kind="Internal").ap()
        slots_dram = nc.dram_tensor("slot_tokens", (SLOTS, 1), I32, kind="Internal").ap()

        def barrier():
            ms = [lane.last() for lane in compute] + [Mark(d.sem, d.value) for d in all_dma if d.value]
            for lane in lanes:
                lane.wait(ms)
            for b in psum_ring.bufs:
                b.free = []

        all_dma = []

        by_name = {}

        def dma_sem(name):
            if name not in by_name:
                by_name[name] = dsem(name)
                all_dma.append(by_name[name])
            return by_name[name]

        def dump(name, ap, *after):
            if dumps is not None and name in dumps:
                after = after or tuple(lane.last() for lane in compute)
                marks_out.append(SP.dma(dma_sem("dump_" + name), dumps[name], ap, *after))

        stage("const")
        ident = take(P)
        chan = take(N_CHAN)
        one_col, zero_col = take(1), take(1)
        eps_ln, eps_gn, eps_rms, eps_kk = take(1), take(1), take(1), take(1)
        ones = take(P)
        pair_ones = take(P)
        G.set(ident, 0.0)
        G.set(ones, 1.0)
        G.set(pair_ones, 1.0)
        G.set(one_col, 1.0)
        G.set(zero_col, 0.0)
        G.set(eps_ln, LN_EPS)
        G.set(eps_gn, GN_EPS)
        G.set(eps_rms, RMS_EPS)
        m = G.set(eps_kk, 1e-12)

        def keep(out, in_, pattern, base, mult, op, fill, *after):
            return G.do(lambda: G.e.affine_select(out=out, in_=in_, pattern=pattern, compare_op=op, fill=fill,
                                                  base=base, channel_multiplier=mult), *after)

        m = keep(ident, ident, [[-1, P]], 0, 1, ALU.not_equal, 1.0, m)

        def same_block(t, n, *after):
            v = t.rearrange("p (b c) -> p b c", c=n)
            a = keep(v, v, [[-n, P // n], [0, n]], 0, 1, ALU.is_ge, 0.0, *after)
            return keep(v, v, [[n, P // n], [0, n]], n - 1, -1, ALU.is_ge, 0.0, a)

        m_const = same_block(pair_ones, HD, m)
        d_chan = dma_sem("chan")
        m_chan = SP.dma(d_chan, chan, io["chan"])

        def col(name, i=0, rows=P):
            c = CHAN_AT[name] + i
            return chan[0:rows, c:c + 1]

        zero_rows = arena[:, ARENA - D:ARENA]
        m = G.set(zero_rows, 0.0)
        fill = dma_sem("y_fill")
        for b in range(NE, NBLK):
            m_yfill = SP.dma(fill, y_dram[P * b:P * (b + 1), :], zero_rows, m)

        h_at = top[0]
        h = take(NS, D)
        top[0] = h_at
        w_bufs = Ring([Buf(take(KD, 512), dma_sem(f"w_in{i}")) for i in range(2)])
        top[0] = h_at + NS * D
        xT = take(KD, T)
        yT = take(KD, T)
        base_b1 = top[0]

        stage("xT")
        x_bufs = Ring([Buf(take(D), dma_sem(f"x{i}")) for i in range(3)])
        for i in range(NT):
            xb = x_bufs.take()
            m = SP.dma(xb.sem, xb.ap, io["x"][P * i:P * (i + 1), :], xb.free)
            if i == 0:
                w_q = w_bufs.take()
                m_wq = SP.dma(w_q.sem, w_q.ap, io["w_in_q"])
            rd = []
            for half in range(2):
                bk = psum_ring.take()
                pv = bk.ap.rearrange("p (a b) -> p a b", a=4)
                mt = PE.mms([(pv[:, k, :], xb.ap[:, P * (4 * half + k):P * (4 * half + k + 1)], ident, None, None)
                             for k in range(4)], m, m_const, bk.free)
                dst = xT[:, 4 * half:4 * half + 4, P * i:P * (i + 1)]
                bk.free = [(V.copy if half else S.copy)(dst, pv, mt)]
                rd.append(mt)
            xb.free = rd
        m_xT = [V.last(), S.last()]
        top[0] = base_b1

        def load_group(name, width):
            b = w_bufs.take()
            wv = b.ap.rearrange("p a b -> p (a b)")[:, 0:KD * width].rearrange("p (a b) -> p a b", a=KD)
            mk = SP.dma(b.sem, wv, io["w_in_" + name], b.free)
            return b, wv, mk

        def project(w, c0, width, m_w, evac):
            mt = None
            for half in range(2):
                bk = psum_ring.take()
                mt = PE.mms([(bk.ap[0:width, :], w[:, k, c0:c0 + width], xT[:, k, 512 * half:512 * half + 512],
                              k == 0, k == KD - 1) for k in range(KD)], m_w, m_xT, bk.free)
                bk.free = evac(half, bk.ap[0:width, :], mt)
            return mt

        def half_cols(half):
            return slice(512 * half, 512 * half + 512)

        stage("qkv")
        qT = take(4, T)
        kd = take(AKV, T)
        v_tok = take(NT, P)
        sig = Ring([Buf(take(512)) for _ in range(3)])
        for mt_i in range(4):
            mt = project(w_q.ap, P * mt_i, P, m_wq,
                         lambda hf, ps, mk, mt_i=mt_i: [S.copy(qT[:, mt_i, half_cols(hf)], ps, mk, scale=HD ** -0.5)])
        w_q.free = [mt]
        wb, w, m_w = load_group("kv", 256)

        def evac_k(hf, ps, mk):
            for kv in range(AKV):
                for dst in range(2):
                    r = V.copy(kd[64 * dst:64 * dst + 64, kv, half_cols(hf)], ps[64 * kv:64 * kv + 64, :], mk)
            return [r]
        project(w, 0, P, m_w, evac_k)
        for g in range(2):
            bk = psum_ring.take()
            pv = bk.ap.rearrange("p (a b) -> p a b", a=4)
            prods = []
            for j in range(4):
                i = 4 * g + j
                prods += [(pv[:, j, :], xT[:, k, P * i:P * (i + 1)], w[:, k, P:2 * P], k == 0, k == KD - 1)
                          for k in range(KD)]
            mt = PE.mms(prods, m_w, m_xT, bk.free)
            bk.free = [S.copy(v_tok[:, 4 * g:4 * g + 4, :], pv, mt)]
        wb.free = [mt]

        def gate(y_at):
            def evac(hf, ps, mk):
                sb = sig.take()
                a = S.act(sb.ap, ps, ACT.Sigmoid, mk, sb.free)
                r = V.tt(yT[:, y_at, half_cols(hf)], ps, sb.ap, ALU.mult, a)
                sb.free = [r]
                return [r]
            return evac

        wb, w, m_w = load_group("ga", 512)
        for j in range(4):
            mt = project(w, P * j, P, m_w, gate(j))
        wb.free = [mt]
        m_q, m_kvg = S.last(), V.last()

        stage("swa")
        wl, wlw, m_wl = load_group("lru", 512)
        band = take(2, P)
        mk_ = G.set(band, 0.0)
        mk_ = keep(band[:, 0, :], band[:, 0, :], [[1, P]], 0, -1, ALU.is_gt, NEG, mk_)
        m_band = keep(band[:, 1, :], band[:, 1, :], [[-1, P]], 0, 1, ALU.is_ge, NEG, mk_)
        sink_row, sink = take(AH), take(AH)
        m_s = SP.dma(dma_sem("sinks"), sink_row, io["sinks"].to_broadcast([P, AH]))
        ORDER = [0, 2, 1, 3, 4, 6, 5, 7]
        for g in range(2):
            V.copy(sink[:, 4 * g:4 * g + 4].rearrange("p (c b) -> p b c", c=2),
                   sink_row[:, 4 * g:4 * g + 4].rearrange("p (b c) -> p b c", b=2), m_s)
        m_sink = V.last()
        Pm = [take(AH, 2 * P) for _ in range(2)]
        PT = [take(2 * AH, P) for _ in range(2)]
        st = [[take(AH) for _ in range(6)] for _ in range(2)]
        pm_free, pt_free = [[], []], [[], []]
        for n in range(NT):
            pm, pt, (mx, nm, rs, es, den, rden) = Pm[n % 2], PT[n % 2], st[n % 2]
            c0 = 0 if n else P
            k0 = P * (n - 1) + c0
            wd = 2 * P - c0
            masked = []
            for b in range(4):
                bk = psum_ring.take()
                pv = bk.ap.rearrange("p (a b) -> p a b", a=2)
                prods = []
                for j in range(2):
                    hh = ORDER[2 * b + j]
                    pr = slice(64 * (hh % 2), 64 * (hh % 2) + 64)
                    prods.append((pv[:, j, c0:], qT[pr, hh // 2, P * n:P * (n + 1)], kd[pr, hh // 4, k0:k0 + wd], True, True))
                mt = PE.mms(prods, m_q, m_kvg, bk.free)
                bk.free = [V.tt(pm[:, 2 * b:2 * b + 2, c0:], pv[:, :, c0:],
                                bc_mid(band.rearrange("p a b -> p (a b)")[:, c0:], 2), ALU.add,
                                mt, m_band, pm_free[n % 2])]
            a = V.red(mx, pm[:, :, c0:], ALU.max, V.last())
            a = V.tt(mx, mx, sink, ALU.max, a, m_sink)
            a = V.ts(nm, mx, -1.0, None, ALU.mult, None, a)
            e_in = V.tt(es, sink, nm, ALU.add, a)
            for j in range(AH):
                e = S.act(pm[:, j, c0:], pm[:, j, c0:], ACT.Exp, a, bias=nm[:, j:j + 1], accum=rs[:, j:j + 1])
            e = S.act(es, es, ACT.Exp, e_in)
            a = V.tt(den, rs, es, ALU.add, e)
            a = V.recip(rden, den, a)
            a = V.tt(pm[:, :, c0:], pm[:, :, c0:], bc_last(rden, wd), ALU.mult, a)
            parts = [0, 1] if n else [1]
            tr = []
            for b in range(4):
                bk = psum_ring.take()
                pv = bk.ap.rearrange("p (a b) -> p a b", a=4)
                prods = []
                for j in range(2):
                    for u in parts:
                        prods.append((pv[:, 2 * j + u, :], pm[:, 2 * b + j, P * u:P * (u + 1)], ident, None, None))
                mt = PE.mms(prods, a, bk.free)
                if n:
                    src, dst = pv, pt[:, 4 * b:4 * b + 4, :]
                else:
                    src, dst = pv[:, 1::2, :], pt[:, 4 * b + 1:4 * b + 4:2, :]
                bk.free = [(S.copy if b % 2 else V.copy)(dst, src, mt, pt_free[n % 2])]
                tr.append(bk.free[0])
            pm_free[n % 2] = [mt]
            bk = psum_ring.take()
            pv = bk.ap.rearrange("p (a b) -> p a b", a=4)
            prods = []
            for j, hh in enumerate(ORDER):
                pr = slice(64 * (hh % 2), 64 * (hh % 2) + 64)
                for u in parts:
                    prods.append((pv[pr, hh // 2, :], v_tok[:, n - 1 + u, 64 * (hh // 4):64 * (hh // 4) + 64],
                                  pt[:, 2 * j + u, :], u == parts[0], u == 1))
            mt = PE.mms(prods, tr, bk.free)
            pt_free[n % 2] = [mt]
            bk.free = [V.tt(yT[:, 0:4, P * n:P * (n + 1)], pv, yT[:, 0:4, P * n:P * (n + 1)], ALU.mult, mt)]
        dump("ya", yT[:, 0:4, :])

        barrier()
        top[0] = base_b1
        stage("lru")
        sig = Ring([Buf(take(512)) for _ in range(3)])
        xb = take(2, T + 3)
        xc, ra, ib, q_, u_ = take(2, T), take(2, T), take(2, T), take(2, T), take(2, T)
        wa_d, wx_d = take(2, P), take(2, P)
        z = V.set(xb[:, :, 0:3], 0.0)
        zz = V.set(wa_d, 0.0)
        zz = V.set(wx_d, 0.0)
        d_l = dma_sem("lru_w")
        for dst, name in ((wa_d, "lru_wa"), (wx_d, "lru_wx")):
            for b in range(4):
                pr = slice(64 * (b % 2), 64 * (b % 2) + 64)
                m_lw = SP.dma(d_l, dst[pr, b // 2, 64 * (b % 2):64 * (b % 2) + 64], io[name][b], zz)
        for j in range(2):
            project(wlw, P * j, P, m_wl,
                    lambda hf, ps, mk, j=j: [S.copy(xb[:, j, 3 + 512 * hf:3 + 512 * hf + 512], ps, mk)])
        m_xb = S.last()
        for j in range(2):
            mt = project(wlw, 256 + P * j, P, m_wl, gate(4 + j))
        wl.free = [mt]
        wrk, wrkw, m_wrk = load_group("rk", 512)
        sp = [take(2) for _ in range(8)]
        lam = chan[:, CHAN_AT["lam"]:CHAN_AT["lam"] + 2]
        neg, ab, e_, s_, s2, ac, cl, ncl = sp
        a = V.ts(neg, lam, -1.0, None, ALU.mult, None, m_chan)
        a = V.tt(ab, lam, neg, ALU.max, a)
        a2 = S.act(e_, ab, ACT.Exp, a, scale=-1.0)
        a = V.ts(s_, e_, 2.0, None, ALU.add, None, a2)
        a = V.recip(s_, s_, a)
        a = V.tt(s_, s_, e_, ALU.mult, a)
        a = V.tt(s2, s_, s_, ALU.mult, a)
        a = V.ts(ac, s2, 1.0 / 19, 1.0 / 17, ALU.mult, ALU.add, a)
        for c in (15, 13, 11, 9, 7, 5, 3, 1):
            a = V.tt(ac, ac, s2, ALU.mult, a)
            a = V.ts(ac, ac, 1.0 / c, None, ALU.add, None, a)
        a = V.tt(ac, ac, s_, ALU.mult, a)
        a = V.ts(ac, ac, 2.0, None, ALU.mult, None, a)
        a = V.ts(neg, neg, 0.0, None, ALU.max, None, a)
        a = V.tt(ac, ac, neg, ALU.add, a)
        a = V.ts(cl, ac, -C_LRU, None, ALU.mult, None, a)
        m_cl = V.ts(ncl, ac, C_LRU, None, ALU.mult, None, a)
        for j in range(2):
            a = V.ts(xc[:, j, :], xb[:, j, 0:T], col("conv_w", 4 * j), col("conv_b", j), ALU.mult, ALU.add, m_xb, z)
            for t in range(1, 4):
                a = V.stt(xc[:, j, :], xb[:, j, t:t + T], col("conv_w", 4 * j + t), xc[:, j, :], ALU.mult, ALU.add, a)
            for wt, dst, bias in ((wa_d, ra, "lru_ba"), (wx_d, ib, "lru_bx")):
                for hf in range(2):
                    bk = psum_ring.take()
                    mt = PE.mms([(bk.ap, wt[:, j, :], xc[:, j, half_cols(hf)], True, True)], a, m_lw, bk.free)
                    bk.free = [S.act(dst[:, j, half_cols(hf)], bk.ap, ACT.Sigmoid, mt, bias=col(bias, j))]
        m_r = S.last()
        for j in range(2):
            th = S.act(q_[:, j, :], ra[:, j, :], ACT.Tanh, m_r, m_cl, scale=ncl[:, j:j + 1])
            ea = S.act(ra[:, j, :], ra[:, j, :], ACT.Exp, th, scale=cl[:, j:j + 1])
            a = V.tt(u_[:, j, :], ra[:, j, :], ra[:, j, :], ALU.mult, ea)
            a = V.stt(q_[:, j, :], u_[:, j, :], 1.0, q_[:, j, :], ALU.add, ALU.mult, a, th)
        for j in range(2):
            a = S.act(q_[:, j, :], q_[:, j, :], ACT.Sqrt, V.last())
            a = V.tt(ib[:, j, :], ib[:, j, :], xc[:, j, :], ALU.mult, m_r)
            a = V.tt(u_[:, j, :], ib[:, j, :], q_[:, j, :], ALU.mult, a, S.last())
            a = V.do(lambda j=j: nc.vector.tensor_tensor_scan(xc[:, j, :], ra[:, j, :], u_[:, j, :], 0.0,
                                                              ALU.mult, ALU.add), a)
            a = V.tt(yT[:, 4 + j, :], yT[:, 4 + j, :], xc[:, j, :], ALU.mult, a)
        dump("yb", yT[:, 4:6, :])

        barrier()
        top[0] = base_b1
        stage("rwkv_in")
        rkv = take(6, T + 2)
        R = [rkv[:, j, 1:T + 1] for j in range(6)]
        wa = take(T + 2)
        sig = Ring([Buf(take(512)) for _ in range(3)])
        wvw, wvww, m_wv = load_group("vwa", 320)
        z = V.set(rkv[:, :, 0:1], 0.0)
        z = V.set(wa[0:64, 0:1], 0.0)
        for j in range(4):
            mt = project(wrkw, P * j, P, m_wrk,
                         lambda hf, ps, mk, j=j: [S.copy(rkv[:, j, 1 + 512 * hf:513 + 512 * hf], ps, mk)])
        wrk.free = [mt]
        wg, wgw, m_wg = load_group("gc", 256)
        for j in range(2):
            project(wvww, P * j, P, m_wv,
                    lambda hf, ps, mk, j=j: [S.copy(rkv[:, 4 + j, 1 + 512 * hf:513 + 512 * hf], ps, mk)])
        project(wvww, 256, 64, m_wv, lambda hf, ps, mk: [S.copy(wa[0:64, 1 + 512 * hf:513 + 512 * hf], ps, mk)])
        for j in range(2):
            project(wgw, P * j, P, m_wg, gate(6 + j))
        barrier()
        stage("rwkv_prep")
        low = [h_at]

        def take_low(*dims):
            n = int(np.prod(dims))
            o = low[0]
            low[0] += n + (n % 2)
            assert low[0] <= base_b1 - KD * T
            v = arena[:, o:o + n]
            return v.rearrange("p (a b) -> p a b", a=dims[0]) if len(dims) == 2 else v

        sgm, av, Lc, Ep, Em, kk = (take_low(2, T) for _ in range(6))
        tmp = [take_low(T) for _ in range(2)]
        w2a2 = take_low(256)
        reset = take_low(T)
        m_w2 = SP.dma(dma_sem("w2a2"), w2a2[0:64, :], io["w2a2"])
        rz = G.set(reset, 1.0)
        m_reset = G.set(reset.rearrange("p (c s) -> p c s", s=CH)[:, :, 0:1], 0.0, rz)
        for j in range(6):
            t_ = tmp[j % 2]
            a = V.tt(t_, rkv[:, j, 0:T], R[j], ALU.subtract, V.last())
            a = V.stt(R[j], t_, col("mu", j), R[j], ALU.mult, ALU.add, a)
        a = V.tt(tmp[0][0:64, :], wa[0:64, 0:T], wa[0:64, 1:T + 1], ALU.subtract, a)
        m_wa = V.stt(wa[0:64, 1:T + 1], tmp[0][0:64, :], col("mu_wa", 0, 64), wa[0:64, 1:T + 1], ALU.mult, ALU.add, a)
        m_th = S.act(wa[0:32, 1:T + 1], wa[0:32, 1:T + 1], ACT.Tanh, m_wa)
        for j in range(2):
            for dst, rows, bias in ((sgm, slice(0, 32), "w0"), (av, slice(32, 64), "a0")):
                for hf in range(2):
                    bk = psum_ring.take()
                    mt = PE.mms([(bk.ap, w2a2[rows, P * j:P * (j + 1)], wa[rows, 1 + 512 * hf:513 + 512 * hf], True, True)],
                                m_th, m_w2, bk.free)
                    bk.free = [S.act(dst[:, j, half_cols(hf)], bk.ap, ACT.Sigmoid, mt, bias=col(bias, j))]
        m_sg = S.last()
        omka = take_low(2)
        m_om = V.ts(omka, chan[:, CHAN_AT["k_a"]:CHAN_AT["k_a"] + 2], -1.0, 1.0, ALU.mult, ALU.add)
        bonus = take(2, T)
        for j in range(2):
            a = V.do(lambda j=j: nc.vector.tensor_tensor_scan(Lc[:, j, :], reset, sgm[:, j, :], 0.0, ALU.mult, ALU.add),
                     m_sg, m_reset)
            a_x = V.tt(sgm[:, j, :], Lc[:, j, :], sgm[:, j, :], ALU.subtract, a)
            S.act(Ep[:, j, :], Lc[:, j, :], ACT.Exp, a, scale=-EXP_HALF)
            S.act(Em[:, j, :], Lc[:, j, :], ACT.Exp, a, scale=EXP_HALF)
            m_ex = S.act(sgm[:, j, :], sgm[:, j, :], ACT.Exp, a_x, scale=-EXP_HALF)
            a = V.ts(kk[:, j, :], R[2 + j], col("k_k", j), None, ALU.mult, None, V.last())
            sq = S.act(tmp[0], kk[:, j, :], ACT.Square, a, PE.last())
            for hf in range(2):
                bk = psum_ring.take()
                mt = PE.mms([(bk.ap, pair_ones, tmp[0][:, half_cols(hf)], True, True)], sq, bk.free)
                bk.free = [S.act(tmp[1][:, half_cols(hf)], bk.ap, ACT.Sqrt, mt, V.last(), bias=eps_kk)]
            a = V.recip(tmp[1], tmp[1], S.last())
            a = V.tt(kk[:, j, :], kk[:, j, :], tmp[1], ALU.mult, a)
            a = V.ts(tmp[1], av[:, j, :], col("k_a", j), omka[:, j:j + 1], ALU.mult, ALU.add, a, m_om)
            a = V.tt(R[2 + j], R[2 + j], tmp[1], ALU.mult, a)
            a = V.stt(tmp[0], R[j], col("r_k", j), R[2 + j], ALU.mult, ALU.mult, a, PE.last())
            for hf in range(2):
                bk = psum_ring.take()
                mt = PE.mms([(bk.ap, pair_ones, tmp[0][:, half_cols(hf)], True, True)], a, bk.free)
                bk.free = [V.tt(bonus[:, j, half_cols(hf)], bk.ap, R[4 + j][:, half_cols(hf)], ALU.mult, mt)]
            a = V.tt(av[:, j, :], av[:, j, :], kk[:, j, :], ALU.mult, V.last(), m_ex)
            a = V.tt(av[:, j, :], av[:, j, :], Em[:, j, :], ALU.mult, a)
            V.tt(R[2 + j], R[2 + j], Em[:, j, :], ALU.mult)
            V.tt(kk[:, j, :], kk[:, j, :], sgm[:, j, :], ALU.mult)
            V.tt(R[j], R[j], Ep[:, j, :], ALU.mult)
        Bf = [av[:, j, :] for j in range(2)]
        Af = [kk[:, j, :] for j in range(2)]
        dump("bonus", bonus)
        dump("Bf", av)

        barrier()
        stage("rwkv")
        Kf, Rf, Vf = [R[2], R[3]], [R[0], R[1]], [R[4], R[5]]
        yb = Lc
        free_low = sgm.rearrange("p a b -> p (a b)"), Em.rearrange("p a b -> p (a b)")
        hi = [top[0]]
        tri = [take(P) for _ in range(5)]
        mN, mNT, mC32, mC64, mUp = tri
        m_a = G.set(mN, -1.0)
        m_a = keep(mN, mN, [[-1, P]], 0, 1, ALU.is_gt, 0.0, m_a)
        m_a = same_block(mN, 16, m_a)
        m_a = G.set(mNT, -1.0, m_a)
        m_a = keep(mNT, mNT, [[1, P]], 0, -1, ALU.is_gt, 0.0, m_a)
        m_a = same_block(mNT, 16, m_a)

        def off_block(t, n, *after):
            hn = n // 2
            a = G.set(t, 1.0, *after)
            v = t.rearrange("p (b u c) -> p b u c", u=2, c=hn)
            a = G.set(v[:, :, 0, :], 0.0, a)
            a = keep(v, v, [[-n, P // n], [0, 2], [0, hn]], 0, 1, ALU.is_ge, 0.0, a)
            return keep(v, v, [[n, P // n], [0, 2], [0, hn]], hn - 1, -1, ALU.is_ge, 0.0, a)

        m_a = off_block(mC32, 32, m_a)
        m_a = off_block(mC64, 64, m_a)
        m_a = G.set(mUp, 1.0, m_a)
        m_a = keep(mUp, mUp, [[1, P]], 0, -1, ALU.is_ge, 0.0, m_a)
        m_a = same_block(mUp, CH, m_a)
        mUpS = take(P)
        m_a = G.set(mUpS, 1.0, m_a)
        m_a = keep(mUpS, mUpS, [[1, P]], 0, -1, ALU.is_gt, 0.0, m_a)
        m_mask = same_block(mUpS, CH, m_a)

        NST = 2 * NT + 1
        STt = take(NST, P).rearrange("p c (a v) -> p c a v", a=2)
        m_state = V.set(STt[:, 0], 0.0)
        tok = [take(8, P) for _ in range(2)]
        big = [take(4, P) for _ in range(9)]
        low_at = [0, 0]

        def take_free(w):
            for i in range(2):
                if low_at[i] + w <= 2 * T:
                    o = low_at[i]
                    low_at[i] += w
                    return free_low[i][:, o:o + w]
            raise AssertionError

        def four(ap):
            return ap.rearrange("p (a b) -> p a b", a=4)
        N_, NT_, CT32, CT64, AKT, RBT, RKT, PA, PB = big
        PTA, PTB, XTa, XTb, X_, Q_ = (four(take_free(4 * P)) for _ in range(6))
        GT = take(2, P)
        AKV_ = four(take_free(4 * HD))
        U0n = four(take_free(4 * HD))
        SA = four(take_free(4 * HD))
        stg = take(2, HD)

        def heads(ap, par):
            return ap.rearrange("p (j r) c -> p j r c", r=2)[:, :, par, :]

        def mm4(lhs, rhs, *after):
            bk = psum_ring.take()
            pv = four(bk.ap)
            mt = PE.mms([(pv[:, i, :], lhs[:, i, :], rhs[:, i, :], True, True) for i in range(4)], bk.free, *after)
            return bk, pv, mt

        prev_tile = []
        for i in range(NT):
            cols = slice(P * i, P * (i + 1))
            tk = tok[i % 2]
            last_all = [V.last(), S.last(), PE.last(), m_mask] if i else [m_mask]
            for half, srcs in enumerate(((Bf[0], Bf[1], Kf[0], Kf[1]), (Af[0], Af[1], Vf[0], Vf[1]))):
                bk = psum_ring.take()
                mt = PE.mms([(four(bk.ap)[:, j, :], s_[:, cols], ident, None, None) for j, s_ in enumerate(srcs)],
                            bk.free, prev_tile)
                bk.free = [S.copy(tk[:, 4 * half:4 * half + 4, :], four(bk.ap), mt, last_all)]
            m_tok = S.last()

            def htok(kind, hh, tk=tk):
                return tk[:, 2 * kind + hh // 2, 64 * (hh % 2):64 * (hh % 2) + 64]
            for par in range(2):
                pr = slice(64 * par, 64 * par + 64)
                A_, B_, K_, R_ = ([f[j][pr, cols] for j in range(2)] for f in (Af, Bf, Kf, Rf))
                bk = psum_ring.take()
                pv = four(bk.ap)
                mt = PE.mms([(pv[:, j, :], A_[j], B_[j], True, True) for j in range(2)] +
                            [(pv[:, 2 + j, :], B_[j], A_[j], True, True) for j in range(2)], bk.free)
                V.tt(heads(N_, par), pv[:, 0:2, :], bc_mid(mN, 2), ALU.mult, mt, last_all)
                V.tt(heads(NT_, par), pv[:, 2:4, :], bc_mid(mNT, 2), ALU.mult)
                V.tt(heads(CT32, par), pv[:, 2:4, :], bc_mid(mC32, 2), ALU.mult)
                bk.free = [V.tt(heads(CT64, par), pv[:, 2:4, :], bc_mid(mC64, 2), ALU.mult)]
                bk = psum_ring.take()
                pv = four(bk.ap)
                mt = PE.mms([(pv[:, j, :], K_[j], A_[j], True, True) for j in range(2)] +
                            [(pv[:, 2 + j, :], B_[j], R_[j], True, True) for j in range(2)], bk.free)
                V.tt(heads(AKT, par), pv[:, 0:2, :], bc_mid(mUpS, 2), ALU.mult, mt)
                bk.free = [V.tt(heads(RBT, par), pv[:, 2:4, :], bc_mid(mUp, 2), ALU.mult)]
                bk = psum_ring.take()
                pv = four(bk.ap)
                mt = PE.mms([(pv[:, j, :], K_[j], R_[j], True, True) for j in range(2)], bk.free)
                bk.free = [V.tt(heads(RKT, par), pv[:, 0:2, :], bc_mid(mUp, 2), ALU.mult, mt)]
            m_m = V.last()
            m_x = V.tt(XTa, NT_, bc_mid(ident, 4), ALU.add, m_m)
            bk, pv, mt = mm4(NT_, N_, m_m)
            bk.free = [S.copy(PA, pv, mt)]
            bk, pv, mt = mm4(N_, NT_)
            bk.free = [V.copy(PTA, pv, mt)]
            m2 = [S.last(), V.last()]
            bk, pv, mt = mm4(PA, XTa, m2, m_x)
            bk.free = [V.tt(XTb, XTa, pv, ALU.add, mt)]
            m_x = V.last()
            bk, pv, mt = mm4(PTA, PA)
            bk.free = [S.copy(PB, pv, mt)]
            bk, pv, mt = mm4(PA, PTA)
            bk.free = [V.copy(PTB, pv, mt)]
            m4 = [S.last(), V.last()]
            bk, pv, mt = mm4(PB, XTb, m4, m_x)
            bk.free = [V.tt(XTa, XTb, pv, ALU.add, mt)]
            m_x = V.last()
            bk, pv, mt = mm4(PTB, PB)
            bk.free = [S.copy(PA, pv, mt)]
            bk, pv, mt = mm4(PA, XTa, S.last(), m_x)
            bk.free = [V.tt(XTb, XTa, pv, ALU.add, mt)]
            m_x = V.last()
            bk = psum_ring.take()
            mt = PE.mms([(four(bk.ap)[:, j, :], XTb[:, j, :], ident, None, None) for j in range(4)], m_x, bk.free)
            bk.free = [S.copy(X_, four(bk.ap), mt)]
            bk, pv, mt = mm4(CT32, X_, S.last())
            bk.free = [S.copy(Q_, pv, mt)]
            m_q_ = S.last()
            bk, pv, mt = mm4(Q_, XTb, m_q_)
            bk.free = [V.tt(XTa, XTb, pv, ALU.subtract, mt)]
            m_x = V.last()
            bk, pv, mt = mm4(XTb, Q_)
            bk.free = [V.tt(PB, X_, pv, ALU.subtract, mt)]
            bk, pv, mt = mm4(CT64, PB, V.last())
            bk.free = [S.copy(Q_, pv, mt)]
            bk, pv, mt = mm4(Q_, XTa, S.last(), m_x)
            bk.free = [V.tt(XTb, XTa, pv, ALU.subtract, mt)]
            m_x = V.last()
            bk = psum_ring.take()
            gp = bk.ap[:, 0:2 * P].rearrange("p (a b) -> p a b", a=2)
            mt = PE.mms([(gp[64 * (hh % 2):64 * (hh % 2) + 64, hh // 2, :], htok(2, hh), XTb[:, hh, :], True, True)
                         for hh in range(4)], m_x, m_tok, bk.free)
            bk.free = [S.copy(GT, gp, mt)]
            bk = psum_ring.take()
            up = bk.ap[:, 0:4 * HD].rearrange("p (a b) -> p a b", a=4)
            mt = PE.mms([(up[:, hh, :], AKT[:, hh, :], htok(3, hh), True, True) for hh in range(4)], bk.free)
            bk.free = [S.copy(AKV_, up, mt)]
            bk = psum_ring.take()
            up = bk.ap[:, 0:4 * HD].rearrange("p (a b) -> p a b", a=4)
            mt = PE.mms([(up[:, hh, :], XTb[:, hh, :], AKV_[:, hh, :], True, True) for hh in range(4)], S.last(), bk.free)
            bk.free = [S.copy(U0n, up, mt, scale=-1.0)]
            m_u = S.last()
            for c in range(2):
                ci = 2 * i + c
                cr = slice(64 * c, 64 * c + 64)
                for par in range(2):
                    pr = slice(64 * par, 64 * par + 64)
                    bk = psum_ring.take()
                    sv = bk.ap[:, 0:2 * HD].rearrange("p (a b) -> p a b", a=2)
                    mt = PE.mms([(sv[cr, j, :], GT[pr, j, cr], STt[pr, ci, j, :], True, True) for j in range(2)],
                                m_state, m_u, bk.free)
                    bk.free = [V.tt(heads(SA, par)[cr], heads(U0n, par)[cr], sv[cr], ALU.subtract, mt, m_u)]
                bk = psum_ring.take()
                dv = bk.ap[:, 0:2 * HD].rearrange("p (a b) -> p a b", a=2)
                prods = []
                for hh in range(4):
                    o = dv[64 * (hh % 2):64 * (hh % 2) + 64, hh // 2, :]
                    prods += [(o, htok(1, hh)[cr], htok(3, hh)[cr], True, False),
                              (o, htok(0, hh)[cr], SA[cr, hh, :], False, True)]
                mt = PE.mms(prods, V.last(), bk.free)
                a = V.tt(stg, STt[:, ci], dv, ALU.add, mt)
                bk.free = [a]
                last_col = P * i + 64 * c + 63
                for j in range(2):
                    m_state = V.ts(STt[:, ci + 1, j, :], stg[:, j, :], Ep[:, j, last_col:last_col + 1], None, ALU.mult, None, a)
            for par in range(2):
                pr = slice(64 * par, 64 * par + 64)
                bk = psum_ring.take()
                yv = bk.ap[:, 0:2 * P].rearrange("p (a b) -> p a b", a=2)
                prods = []
                for j in range(2):
                    hh = 2 * j + par
                    prods += [(yv[pr, j, :], SA[:, hh, :], RBT[:, hh, :], True, False),
                              (yv[pr, j, :], htok(3, hh), RKT[:, hh, :], False, False)]
                    for c in range(2):
                        prods.append((yv[pr, j, 64 * c:64 * c + 64], STt[pr, 2 * i + c, j, :],
                                      Rf[j][pr, P * i + 64 * c:P * i + 64 * c + 64], False, c == 1))
                mt = PE.mms(prods, m_state, bk.free)
                bk.free = [S.copy(yb[pr, :, cols], yv[pr], mt)]
        dump("yr", yb)

        barrier()
        stage("gn")
        sqb, vb = free_low[0], free_low[1]
        wo1 = arena[:, hi[0]:hi[0] + KD * D].rearrange("p (a b) -> p a b", a=KD)
        m_wo = SP.dma(dma_sem("w_out"), wo1, io["w_out"])
        for j in range(2):
            for hf in range(2):
                hc = half_cols(hf)
                bk = psum_ring.take()
                mt = PE.mms([(bk.ap, pair_ones, yb[:, j, hc], True, True)], bk.free)
                bk.free = [V.stt(yb[:, j, hc], bk.ap, -1.0 / HD, yb[:, j, hc], ALU.mult, ALU.add, mt)]
                sq = S.act(sqb[:, T * j + 512 * hf:T * j + 512 * hf + 512], yb[:, j, hc], ACT.Square, V.last())
                bk = psum_ring.take()
                mt = PE.mms([(bk.ap, pair_ones, sqb[:, T * j + 512 * hf:T * j + 512 * hf + 512], True, True)], sq, bk.free)
                vv = vb[:, T * j + 512 * hf:T * j + 512 * hf + 512]
                bk.free = [S.act(vv, bk.ap, ACT.Sqrt, mt, bias=eps_gn, scale=1.0 / HD)]
                a = V.recip(vv, vv, S.last())
                a = V.tt(yb[:, j, hc], yb[:, j, hc], vv, ALU.mult, a)
                a = V.ts(yb[:, j, hc], yb[:, j, hc], col("gn_w", j), col("gn_b", j), ALU.mult, ALU.add, a)
                a = V.tt(yb[:, j, hc], yb[:, j, hc], bonus[:, j, hc], ALU.add, a)
                V.tt(yT[:, 6 + j, hc], yT[:, 6 + j, hc], yb[:, j, hc], ALU.mult, a)
        dump("yc", yT[:, 6:8, :])

        barrier()
        stage("out1")
        top[0] = hi[0] + KD * T
        lng, lnb = take(D), take(D)
        xr = Ring([Buf(take(D), dma_sem(f"xr{i}")) for i in range(2)])
        stats = take(12)
        mv = take(2)
        d_ln = dma_sem("ln")
        SP.dma(d_ln, lng, io["rows"][0:1, :].to_broadcast([P, D]))
        m_ln = SP.dma(d_ln, lnb, io["rows"][1:2, :].to_broadcast([P, D]))
        for i in range(NT):
            xb_ = xr.take()
            m = SP.dma(xb_.sem, xb_.ap, io["x"][P * i:P * (i + 1), :], xb_.free)
            a_ = []
            for hf in range(2):
                bk = psum_ring.take()
                mt = PE.mms([(bk.ap, yT[:, k, P * i:P * (i + 1)], wo1[:, k, half_cols(hf)], k == 0, k == KD - 1)
                             for k in range(KD)], m_wo, bk.free)
                bk.free = [V.stt(h[:, i, half_cols(hf)], xb_.ap[:, half_cols(hf)], ALPHA, bk.ap, ALU.mult, ALU.add, mt, m)]
                a_.append(V.do(lambda i=i, hf=hf: nc.vector.bn_stats(stats[:, 6 * hf:6 * hf + 6], h[:, i, half_cols(hf)]),
                               bk.free[0]))
            xb_.free = [V.last()]
            a = V.do(lambda: nc.vector.bn_aggr(mv, stats), a_)
            s = S.act(mv[:, 1:2], mv[:, 1:2], ACT.Sqrt, a, bias=eps_ln)
            a = V.recip(mv[:, 1:2], mv[:, 1:2], s)
            a = V.ts(h[:, i, :], h[:, i, :], mv[:, 0:1], mv[:, 1:2], ALU.subtract, ALU.mult, a)
            a = G.tt(h[:, i, :], h[:, i, :], lng, ALU.mult, a, m_ln)
            a = G.tt(h[:, i, :], h[:, i, :], lnb, ALU.add, a)
        z = V.set(h[:, NT, :], 0.0)
        SP.dma(dma_sem("meta"), h[0:N_META, NT, :], io["meta"], z)
        barrier()
        dump("h1", h)
        base_b2 = h_at + NS * D

        def rms(dst_rstd, junk, *after):
            for s in range(NS):
                a = S.act(junk, h[:, s, :], ACT.Square, after, S.last(), accum=dst_rstd[:, s:s + 1])
            a = S.act(dst_rstd, dst_rstd, ACT.Sqrt, a, bias=eps_rms, scale=1.0 / D)
            return V.recip(dst_rstd, dst_rstd, a)

        barrier()
        stage("pool")
        top[0] = base_b2
        hn = take(KD, PADW + L)
        xn = take(3, D)
        rstd, junk = take(NS), take(D)
        sa, sb_ = take(PADW + L), take(PADW + L)
        pooled = take(KD, L)
        a_w = take(KD, 256)
        arow = take(D)
        inv = take(4, PADW)
        edge = take(PADW)
        d_pw = dma_sem("pool_w")
        SP.dma(d_pw, a_w, io["a_w"])
        m_aw = SP.dma(d_pw, arow, io["rows"][2:3, :].to_broadcast([P, D]))
        cnt_i = take(PADW)
        a = G.do(lambda: G.e.iota(cnt_i.bitcast(I32), [[1, PADW]], base=1, channel_multiplier=0))
        a = V.copy(edge, cnt_i.bitcast(I32), a)
        for g, w in enumerate(WINDOWS):
            c = V.ts(inv[:, g, :], edge, float(w), None, ALU.min, None, a)
        m_inv = V.recip(inv, inv, c)
        z = V.set(hn[:, :, 0:PADW], 0.0)
        V.set(sa[:, 0:PADW], 0.0)
        m_z = V.set(sb_[:, 0:PADW], 0.0)
        m_r = rms(rstd, junk)
        xn_free = [[], [], []]
        for s, (pos, n) in enumerate(SLOT):
            xs = xn[:, s % 3, :]
            a = V.ts(xs, h[:, s, :], rstd[:, s:s + 1], None, ALU.mult, None, m_r, xn_free[s % 3])
            for half in range(2):
                bk = psum_ring.take()
                pv = bk.ap.rearrange("p (a b) -> p a b", a=4)
                mt = PE.mms([(pv[:, k, 0:n], xs[0:n, P * (4 * half + k):P * (4 * half + k + 1)], ident[0:n, 0:n], None, None)
                             for k in range(4)], a, bk.free)
                for k in range(4):
                    kk_ = 4 * half + k
                    bk.free = [S.copy(hn[:, kk_, PADW + pos:PADW + pos + n], pv[:, k, 0:n], mt, m_chan,
                                      scale=col("a_norm", kk_))]
            xn_free[s % 3] = [mt]
        m_hn = S.last()
        for k in range(KD):
            g = k // 2
            w = WINDOWS[g]
            src, a, sh = hn[:, k, :], [m_hn, m_z, V.last()], 1
            bufs2 = [sa, sb_]
            while sh < w:
                dst = bufs2[0]
                a = V.tt(dst[:, PADW:], src[:, PADW:], src[:, PADW - sh:PADW + L - sh], ALU.add, a)
                src, sh = dst, 2 * sh
                bufs2.reverse()
            b = V.tt(edge, src[:, PADW:2 * PADW], inv[:, g, :], ALU.mult, a, m_inv)
            V.stt(pooled[:, k, PADW:], src[:, 2 * PADW:], 1.0 / w, hn[:, k, 2 * PADW:], ALU.mult, ALU.subtract)
            V.tt(pooled[:, k, 0:PADW], edge, hn[:, k, PADW:2 * PADW], ALU.subtract, b)
        m_p = V.last()
        for s, (pos, n) in enumerate(SLOT):
            for half in range(2):
                bk = psum_ring.take()
                mt = PE.mms([(bk.ap[0:n, 256 * g:256 * g + 256], pooled[:, 4 * half + 2 * g + u, pos:pos + n],
                              a_w[:, 4 * half + 2 * g + u, :], u == 0, u == 1) for g in range(2) for u in range(2)],
                            m_p, m_aw, bk.free)
                hc = half_cols(half)
                a = V.tt(junk[0:n, hc], bk.ap[0:n, :], arow[0:n, hc], ALU.mult, mt, m_aw, V.last())
                bk.free = [a]
                V.tt(h[0:n, s, hc], h[0:n, s, hc], junk[0:n, hc], ALU.add, a)
        dump("h2", h)

        def moe(layer):
            barrier()
            stage(f"route{layer}")
            top[0] = base_b2
            WF = KD * 2 * DE + 2 * D
            w_ring = Ring([Buf(take(WF), dma_sem(f"we{i}")) for i in range(3)])

            def load_expert(e):
                b = w_ring.take()
                mk = SP.dma(b.sem, b.ap, io["w_exp"][layer * NE + e], b.free)
                return b, mk
            loaded = [load_expert(e) for e in range(3)]
            idx = take(NBLK)
            dest = take(NS, 2)
            gates = take(NS, 2)
            counts = take(32)
            base_route = top[0]
            xg = take(NS, D)
            xgT = take(KD, NS * P)
            rstd, junk = take(NS), xgT.rearrange("p a b -> p (a b)")[:, 0:D]
            grow = take(D)
            wr, br = take(KD, NG + NE), take(NG + NE)
            d_r = dma_sem("router")
            SP.dma(d_r, grow, io["rows"][3 + layer:4 + layer, :].to_broadcast([P, D]))
            SP.dma(d_r, wr, io["w_router"][layer])
            m_rw = SP.dma(d_r, br, io["b_router"][layer:layer + 1, :].to_broadcast([P, NG + NE]))
            io4, io32, io48, tokid = take(NG), take(NE), take(NOV), take(NS)
            base_e, valid, upper = take(NE), take(NS), take(P)
            zeros = take(NBLK)
            ci = take(64)
            a1 = G.do(lambda: G.e.iota(ci.bitcast(I32)[:, 0:NE], [[1, NE]], base=0, channel_multiplier=0))
            a2 = G.do(lambda: G.e.iota(tokid.bitcast(I32), [[P, NS]], base=0, channel_multiplier=1))
            G.set(valid, 1.0)
            a3 = G.set(valid[:, NT:NS], 0.0, G.last())
            G.set(valid[0:N_META, NT:NS], 1.0, a3)
            m_zero = G.set(zeros, 0.0)
            a3 = G.set(upper, 1.0)
            m_up = keep(upper, upper, [[1, P]], 0, -1, ALU.is_gt, 0.0, a3)
            V.copy(io32, ci.bitcast(I32)[:, 0:NE], a1)
            V.copy(io4, ci.bitcast(I32)[:, 0:NG])
            V.copy(io48, ci.bitcast(I32)[:, 0:NOV])
            m_io = V.ts(base_e, io32, float(P), None, ALU.mult, None, V.last())
            m_fill = SP.dma(dma_sem("fill"), slots_dram.rearrange("(p c) o -> p (c o)", p=P),
                            zeros.bitcast(I32), m_zero)
            m_r = rms(rstd, junk)
            d_x = dma_sem("xn")
            for s, (pos, n) in enumerate(SLOT):
                a = V.stt(xg[:, s, :], h[:, s, :], rstd[:, s:s + 1], grow, ALU.mult, ALU.mult, m_r, m_rw)
                m_xn = SP.dma(d_x, xn_dram[P * s:P * s + n, :], xg[0:n, s, :], a)
                for half in range(2):
                    bk = psum_ring.take()
                    pv = four(bk.ap)
                    mt = PE.mms([(pv[:, k, :], xg[:, s, P * (4 * half + k):P * (4 * half + k + 1)], ident, None, None)
                                 for k in range(4)], a, bk.free)
                    bk.free = [(S if half else V).copy(xgT[:, 4 * half:4 * half + 4, P * s:P * (s + 1)], pv, mt, m_r)]
            m_t = [V.last(), S.last()]
            marks_out.append(m_xn)
            bk = psum_ring.take()
            NR = NG + NE
            pv = bk.ap[:, 0:NS * NR].rearrange("p (a b) -> p a b", a=NS)
            mt = PE.mms([(pv[:, s, :], xgT[:, k, P * s:P * (s + 1)], wr[:, k, :], k == 0, k == KD - 1)
                         for s in range(NS) for k in range(KD)], m_t, m_rw, bk.free)
            lg = take(NS, NR)
            a = V.tt(lg, pv, bc_mid(br, NS), ALU.add, mt, m_rw)
            bk.free = [a]
            gp, m8, i8 = take(NS, 8), take(NS, 8), take(NS, 8)
            b = V.set(gp, NEG)
            b = V.copy(gp[:, :, 0:NG], lg[:, :, 0:NG], a, b)
            for s in range(NS):
                c = V.do(lambda s=s: nc.vector.max(m8[:, s, :], gp[:, s, :]), b)
                V.do(lambda s=s: nc.vector.max_index(i8[:, s, :].bitcast(U32), m8[:, s, :], gp[:, s, :]), c)
            a = V.last()
            eg, wg, gi = take(NS, NG), take(NS), take(NS)
            c = V.tt(eg, lg[:, :, 0:NG], m8[:, :, 0:1].to_broadcast([P, NS, NG]), ALU.subtract, a)
            c = S.act(eg, eg, ACT.Exp, c)
            c = V.red(wg, eg, ALU.add, c)
            c = V.recip(wg, wg, c)
            c = V.copy(gi, i8[:, :, 0:1].rearrange("p a b -> p (a b)").bitcast(U32), c)
            pen = take(NS, NG)
            c = V.tt(pen, bc_mid(io4, NS), bc_last(gi, NG), ALU.is_equal, c, m_io)
            c = V.ts(pen, pen, -NEG, NEG, ALU.mult, ALU.add, c)
            me = take(NS, NE)
            c = V.tt(me.rearrange("p s (g e) -> p s g e", g=NG), lg[:, :, NG:].rearrange("p s (g e) -> p s g e", g=NG),
                     pen.unsqueeze(3).to_broadcast([P, NS, NG, EPG]), ALU.add, c)
            for s in range(NS):
                b = V.do(lambda s=s: nc.vector.max(m8[:, s, :], me[:, s, :]), c)
                V.do(lambda s=s: nc.vector.max_index(i8[:, s, :].bitcast(U32), m8[:, s, :], me[:, s, :]), b)
            a = V.last()
            e1, rr, ei = take(NS), take(NS), take(NS, 2)
            v0, v1 = (m8[:, :, j:j + 1].rearrange("p a b -> p (a b)") for j in range(2))
            c = V.tt(e1, v1, v0, ALU.subtract, a)
            c = S.act(e1, e1, ACT.Exp, c)
            c = V.ts(rr, e1, 1.0, None, ALU.add, None, c)
            c = V.recip(rr, rr, c)
            c = V.tt(rr, rr, wg, ALU.mult, c)
            V.copy(gates[:, :, 0:1], rr.unsqueeze(2), c)
            V.tt(gates[:, :, 1:2], rr.unsqueeze(2), e1.unsqueeze(2), ALU.mult)
            c = V.copy(ei, i8[:, :, 0:2].bitcast(U32))
            oh, both = [take(NS, NE) for _ in range(2)], take(NS, NE)
            for j in range(2):
                b = V.tt(oh[j], bc_mid(io32, NS), ei[:, :, j:j + 1].to_broadcast([P, NS, NE]), ALU.is_equal, c)
                b = V.tt(oh[j], oh[j], bc_last(valid, NE), ALU.mult, b, G.last())
            m_oh = V.tt(both, oh[0], oh[1], ALU.add, b)
            bk = psum_ring.take()
            pv = bk.ap[:, 0:NS * NE].rearrange("p (a b) -> p a b", a=NS)
            prods = []
            for s in range(NS):
                prods += [(pv[:, s, :], ones, both[:, j, :], j == 0, False) for j in range(s)]
                prods.append((pv[:, s, :], upper, both[:, s, :], s == 0, True))
            mt = PE.mms(prods, m_oh, m_up, bk.free)
            rank = take(NS, NE)
            bk.free = [V.copy(rank, pv, mt)]
            bk = psum_ring.take()
            mt = PE.mms([(bk.ap[:, 0:NE], ones, both[:, j, :], j == 0, j == NS - 1) for j in range(NS)], bk.free)
            cnt, nb, cum, dif = (take(NE) for _ in range(4))
            a = V.copy(cnt, bk.ap[:, 0:NE], mt)
            bk.free = [a]
            a = V.ts(nb, cnt, float(P), None, ALU.is_gt, None, a)
            for j in range(2, (L - 1) // P + 1):
                a = V.stt(nb, cnt, float(P * j), nb, ALU.is_gt, ALU.add, a)
            a = V.do(lambda: nc.vector.tensor_tensor_scan(cum, ones[:, 0:NE], nb, 0.0, ALU.mult, ALU.add), a)
            m_cum = a
            a = V.tt(dif, cum, nb, ALU.subtract, a)
            a = V.ts(dif, dif, float(P), float((NE - 1) * P), ALU.mult, ALU.add, a)
            a = V.tt(dif, dif, base_e, ALU.subtract, a)
            over, slot = take(NS, NE), take(NS, NE)
            b = V.ts(over, rank, float(P), None, ALU.is_ge, None, a)
            b = V.tt(over, over, bc_mid(dif, NS), ALU.mult, b)
            c = V.tt(slot, rank, bc_mid(base_e, NS), ALU.add, b)
            c = V.tt(slot, slot, over, ALU.add, c)
            df = take(NS, 2)
            for j in range(2):
                b = V.tt(oh[j], oh[j], slot, ALU.mult, c)
                V.red(df[:, :, j:j + 1], oh[j], ALU.add, b)
            m_dest = V.copy(dest.bitcast(I32), df, V.last())
            ovx, ovs = take(NOV, NE), take(NOV)
            a = V.tt(ovx[0:1], bc_last(io48[0:1], NE), bc_mid(cum[0:1], NOV), ALU.is_ge, m_cum)
            a = V.red(ovs[0:1], ovx[0:1], ALU.add, a)
            a = V.ts(ovs[0:1], ovs[0:1], float(NE - 1), None, ALU.min, None, a)
            V.copy(counts.bitcast(I32)[0:1, 1:1 + NOV], ovs[0:1], a)
            m_cnt = V.copy(counts.bitcast(I32)[0:1, 0:1], cum[0:1, NE - 1:NE])
            d_sc = dma_sem("scatter")
            for s, (pos, n) in enumerate(SLOT):
                for j in range(2):
                    G.wait([m_dest, m_fill, a2])
                    G.queue.append(lambda s=s, j=j, n=n: G.e.indirect_dma_start(
                        out=slots_dram[:, :], out_offset=bass.IndirectOffsetOnAxis(dest.bitcast(I32)[0:n, s, j:j + 1], 0),
                        in_=tokid.bitcast(I32)[0:n, s:s + 1], in_offset=None).then_inc(d_sc.sem, 16))
                    m_sc = d_sc.next()
            rows = take(P)
            a = SP.dma(dma_sem("slots"), rows.bitcast(I32)[0:NBLK, :],
                       slots_dram.rearrange("(b p) o -> b (p o)", p=P), m_sc)
            rowf = take(P)
            a = V.copy(rowf[0:NBLK, :], rows.bitcast(I32)[0:NBLK, :], a)
            bk = psum_ring.take()
            mt = PE.mms([(bk.ap[:, 0:NBLK], rowf[0:NBLK, :], ident[0:NBLK, 0:NBLK], None, None)], a, bk.free)
            bk.free = [V.copy(idx.bitcast(I32), bk.ap[:, 0:NBLK], mt)]
            m_idx = V.last()
            if layer == 0:
                dump("lg", lg)
                dump("slot", slot)
                dump("gates", gates)

            barrier()
            stage(f"experts{layer}")
            top[0] = base_route
            xe_ring = Ring([Buf(take(D), dma_sem(f"xe{i}")) for i in range(3)])
            xt_ring = Ring([Buf(take(KD, P)) for _ in range(2)])
            g_ring = Ring([Buf(take(DE)) for _ in range(2)])
            h_ring = Ring([Buf(take(DE)) for _ in range(2)])
            ht_ring = Ring([Buf(take(2, P)) for _ in range(2)])
            y_ring = Ring([Buf(take(D), dma_sem(f"y{i}")) for i in range(3)])

            def gather(block):
                xe = xe_ring.take()
                G.wait([m_idx, m_xn, xe.free])
                sem, ap = xe.sem, xe.ap
                G.queue.append(lambda: G.e.indirect_dma_start(
                    out=ap, out_offset=None, in_=xn_dram[:, :],
                    in_offset=bass.IndirectOffsetOnAxis(idx.bitcast(I32)[:, block:block + 1], 0)).then_inc(sem.sem, 16))
                return xe, sem.next()

            def gate_up(xe, m_xe, w, m_w):
                xt = xt_ring.take()
                cp = []
                for half in range(2):
                    bk = psum_ring.take()
                    mt = PE.mms([(four(bk.ap)[:, k, :], xe.ap[:, P * (4 * half + k):P * (4 * half + k + 1)], ident, None, None)
                                 for k in range(4)], m_xe, bk.free)
                    bk.free = [(S if half else V).copy(xt.ap[:, 4 * half:4 * half + 4, :], four(bk.ap), mt, xt.free)]
                    cp.append(bk.free[0])
                xe.free = [mt]
                wv = w.ap[:, 0:KD * 2 * DE].rearrange("p (a b) -> p a b", a=KD)
                bk = psum_ring.take()
                mt = PE.mms([(bk.ap, xt.ap[:, k, :], wv[:, k, :], k == 0, k == KD - 1) for k in range(KD)], cp, m_w, bk.free)
                xt.free = [mt]
                g, hb = g_ring.take(), h_ring.take()
                a = S.act(g.ap, bk.ap[:, 0:DE], ACT.Sigmoid, mt, g.free)
                a = V.tt(g.ap, bk.ap[:, 0:DE], g.ap, ALU.mult, a)
                a = V.tt(hb.ap, bk.ap[:, DE:2 * DE], g.ap, ALU.mult, a, hb.free)
                bk.free, g.free = [a], [a]
                return hb, a

            def down(hb, m_h, w, block):
                bk = psum_ring.take()
                mt = PE.mms([(four(bk.ap)[:, k, :], hb.ap[:, P * k:P * (k + 1)], ident, None, None) for k in range(2)],
                            m_h, bk.free)
                hb.free = [mt]
                ht = ht_ring.take()
                a = S.copy(ht.ap, four(bk.ap)[:, 0:2, :], mt, ht.free)
                bk.free = [a]
                wv = w.ap[:, KD * 2 * DE:].rearrange("p (a b) -> p a b", a=2)
                y = y_ring.take()
                cp = []
                for half in range(2):
                    bk = psum_ring.take()
                    mt = PE.mms([(bk.ap, ht.ap[:, k, :], wv[:, k, half_cols(half)], k == 0, k == 1) for k in range(2)], a, bk.free)
                    bk.free = [(S if half else V).copy(y.ap[:, half_cols(half)], bk.ap, mt, y.free)]
                    cp.append(bk.free[0])
                ht.free = [mt]
                w.free = [mt]
                y.free = [SP.dma(y.sem, y_dram[P * block:P * (block + 1), :], y.ap, cp)]
                return y.free[0]

            gathered = [gather(0), gather(1)]
            pending = None
            for e in range(NE):
                w, m_w = loaded[e]
                xe, m_xe = gathered[e]
                hb, m_h = gate_up(xe, m_xe, w, m_w)
                if e + 2 < NE:
                    gathered.append(gather(e + 2))
                if pending:
                    down(*pending)
                    if e + 2 < NE:
                        loaded.append(load_expert(e + 2))
                pending = (hb, m_h, w, e)
            down(*pending)
            m_y = [b.free for b in y_ring.bufs]

            barrier()
            loads = {}

            def enter(lane):
                lane.queue.append(lambda: loads.__setitem__(lane, lane.e.value_load(counts.bitcast(I32)[0:1, 0:1],
                                                                                   min_val=0, max_val=NOV)))
            for lane in lanes:
                lane.wait([m_cnt])
                enter(lane)
            stage(f"over{layer}")
            for kind, r in (("rows", xe_ring), ("y", y_ring), ("w", w_ring)):
                del r.bufs[1:]
                r.bufs[0].sem, r.bufs[0].free = dsem(f"over{layer}_{kind}"), []
            for r in (xt_ring, g_ring, h_ring, ht_ring):
                for b in r.bufs:
                    b.free = []
            outer = {lane: (lane.queue, dict(lane.waited)) for lane in lanes}
            for blk in range(NOV):
                for lane in lanes:
                    lane.queue = []
                wb_ = w_ring.take()
                SP.wait(wb_.free)
                sem = wb_.sem

                def load_w(blk=blk, wb_=wb_, sem=sem):
                    ex = SP.e.value_load(counts.bitcast(I32)[0:1, 1 + blk:2 + blk], min_val=0, max_val=NE - 1)
                    SP.e.dma_start(wb_.ap, io["w_exp"][bass.ds(ex + layer * NE, 1)].rearrange("a p n -> (a p) n")).then_inc(sem.sem, 16)
                SP.queue.append(load_w)
                m_w = sem.next()
                xe, m_xe = gather(NE + blk)
                hb, m_h = gate_up(xe, m_xe, wb_, m_w)
                m_yo = down(hb, m_h, wb_, NE + blk)
                S.wait([m_yo])
                for lane in lanes:
                    sub = lane.queue
                    lane.queue = outer[lane][0]

                    def branch(lane=lane, sub=sub, blk=blk):
                        with lane.e.If(loads[lane] > blk):
                            lane.play(sub)
                    lane.queue.append(branch)
            for lane in lanes:
                lane.waited = outer[lane][1]
            stage(f"joined{layer}")
            scr = take(16)
            joined = [V.set(scr[:, 0:2], 0.0), G.set(scr[:, 2:4], 0.0), S.copy(scr[:, 4:6], ident[:, 0:2]),
                      PE.mms([(banks[0][:, 0:2], ident, ident[:, 0:2], True, True)])]
            for lane in lanes:
                lane.wait(joined)
            for b in psum_ring.bufs:
                b.free = []

            c_ring = Ring([Buf(take(D), dma_sem(f"c{i}")) for i in range(4)])
            for s, (pos, n) in enumerate(SLOT):
                for j in range(2):
                    cb = c_ring.take()
                    G.wait([m_y, cb.free])
                    G.queue.append(lambda s=s, j=j, n=n, cb=cb: G.e.indirect_dma_start(
                        out=cb.ap[0:n, :], out_offset=None, in_=y_dram[:, :],
                        in_offset=bass.IndirectOffsetOnAxis(dest.bitcast(I32)[0:n, s, j:j + 1], 0)).then_inc(cb.sem.sem, 16))
                    mk = cb.sem.next()
                    cb.free = [V.stt(h[0:n, s, :], cb.ap[0:n, :], gates[0:n, s, j:j + 1], h[0:n, s, :], ALU.mult, ALU.add,
                                     mk, V.last())]
            dump(f"h{3 + 2 * layer}", h)

        moe(0)

        barrier()
        stage("latent")
        top[0] = base_b2
        NC = KVL + ROPE + QL
        cqT, ckvT, krT = take(3, L), take(2, L), take(L)
        qrT = take(4, L)
        w_uq, w_uk, w_uv = take(3, MH * (NOPE + ROPE)), take(2, MH * NOPE), take(2, MH * VH)
        base_mla = top[0]
        wc = take(KD, NC)
        rope_cs = take(NS, ROPE)
        xn = take(2, D)
        xt = take(2, KD * P)
        rstd, junk = take(NS), take(D)
        ct = [take(NC) for _ in range(2)]
        rs2 = [take(2) for _ in range(2)]
        kr = [take(P) for _ in range(2)]
        rt = [take(ROPE // 2) for _ in range(4)]
        d_lw = dma_sem("latent_w")
        SP.dma(d_lw, wc, io["w_c"])
        SP.dma(d_lw, rope_cs, io["rope"])
        SP.dma(d_lw, w_uq, io["w_uq"])
        SP.dma(d_lw, w_uk, io["w_uk"])
        m_lw = SP.dma(d_lw, w_uv, io["w_uv"])
        for k in range(KD):
            V.ts(wc[:, k, 0:KVL + ROPE], wc[:, k, 0:KVL + ROPE], col("kv_norm", k), None, ALU.mult, None, m_lw)
            V.ts(wc[:, k, KVL + ROPE:], wc[:, k, KVL + ROPE:], col("b_norm", k), None, ALU.mult, None)
        m_wc = V.last()
        for k in range(3):
            G.ts(w_uq[:, k, :], w_uq[:, k, :], col("q_norm", k), None, ALU.mult, None, m_lw)
        for k in range(2):
            G.ts(w_uk[:, k, :], w_uk[:, k, :], col("kv_lat", k), None, ALU.mult, None)
            G.ts(w_uv[:, k, :], w_uv[:, k, :], col("kv_lat", k), None, ALU.mult, None)
        m_wu = G.last()
        m_r = rms(rstd, junk)
        xn_free, xt_free, ct_free = [[], []], [[], []], [[], []]

        def rotate(dst, x, cs, n, tm, rows, *after):
            x1, x2, o1, o2 = x[0], x[1], dst[0], dst[1]
            b = [V.tt(tm[0], x1, cs[0], ALU.mult, after), V.tt(tm[1], x2, cs[1], ALU.mult),
                 V.tt(tm[2], x1, cs[1], ALU.mult), V.tt(tm[3], x2, cs[0], ALU.mult)]
            V.tt(o1, tm[0], tm[1], ALU.subtract, b)
            return V.tt(o2, tm[2], tm[3], ALU.add)

        H2 = ROPE // 2
        for s, (pos, n) in enumerate(SLOT):
            p_ = s % 2
            a = V.ts(xn[:, p_, :], h[:, s, :], rstd[:, s:s + 1], None, ALU.mult, None, m_r, xn_free[p_])
            xtv = xt[:, p_, :].rearrange("p (a b) -> p a b", a=KD)
            cp = []
            for half in range(2):
                bk = psum_ring.take()
                mt = PE.mms([(four(bk.ap)[:, k, 0:n], xn[0:n, p_, P * (4 * half + k):P * (4 * half + k + 1)],
                              ident[0:n, 0:n], None, None) for k in range(4)], a, bk.free)
                bk.free = [(S if half else V).copy(xtv[:, 4 * half:4 * half + 4, 0:n], four(bk.ap)[:, :, 0:n], mt, xt_free[p_])]
                cp.append(bk.free[0])
            xn_free[p_] = [mt]
            c_ = ct[p_]
            for c0, c1 in ((0, KVL + ROPE), (KVL + ROPE, NC)):
                bk = psum_ring.take()
                mt = PE.mms([(bk.ap[0:n, 0:c1 - c0], xtv[:, k, 0:n], wc[:, k, c0:c1], k == 0, k == KD - 1)
                             for k in range(KD)], cp, m_wc, bk.free)
                bk.free = [S.copy(c_[0:n, c0:c1], bk.ap[0:n, 0:c1 - c0], mt, ct_free[p_])]
            xt_free[p_] = [mt]
            a = S.last()
            r2 = rs2[p_]
            b = S.act(junk[0:n, 0:KVL], c_[0:n, 0:KVL], ACT.Square, a, accum=r2[0:n, 0:1])
            b = S.act(junk[0:n, 0:QL], c_[0:n, KVL + ROPE:], ACT.Square, b, accum=r2[0:n, 1:2])
            S.act(r2[0:n, 0:1], r2[0:n, 0:1], ACT.Sqrt, b, bias=eps_rms[0:n, :], scale=1.0 / KVL)
            b = S.act(r2[0:n, 1:2], r2[0:n, 1:2], ACT.Sqrt, bias=eps_rms[0:n, :], scale=1.0 / QL)
            b = V.recip(r2[0:n, :], r2[0:n, :], b)
            V.ts(c_[0:n, 0:KVL], c_[0:n, 0:KVL], r2[0:n, 0:1], None, ALU.mult, None, b)
            m_c = V.ts(c_[0:n, KVL + ROPE:], c_[0:n, KVL + ROPE:], r2[0:n, 1:2], None, ALU.mult, None)
            k_ = kr[p_]
            cs = (rope_cs[0:n, s, 0:H2], rope_cs[0:n, s, H2:])
            a = rotate((k_[0:n, 0:H2], k_[0:n, H2:ROPE]), (c_[0:n, KVL:KVL + H2], c_[0:n, KVL + H2:KVL + ROPE]), cs, n,
                       [r[0:n, :] for r in rt], n, m_c, ct_free[p_])
            a = V.copy(k_[0:n, ROPE:2 * ROPE], k_[0:n, 0:ROPE], a)
            bk = psum_ring.take()
            pv = four(bk.ap)
            srcs = [c_[0:n, 0:P], c_[0:n, P:2 * P], k_[0:n, :]]
            mt = PE.mms([(pv[:, j, 0:n], x_, ident[0:n, 0:n], None, None) for j, x_ in enumerate(srcs)], a, m_c, bk.free)
            S.copy(ckvT[:, :, pos:pos + n], pv[:, 0:2, 0:n], mt)
            bk.free = [S.copy(krT[:, pos:pos + n], pv[:, 2, 0:n])]
            bk = psum_ring.take()
            pv = four(bk.ap)
            mt = PE.mms([(pv[:, j, 0:n], c_[0:n, KVL + ROPE + P * j:KVL + ROPE + P * (j + 1)], ident[0:n, 0:n], None, None)
                         for j in range(3)], bk.free)
            bk.free = [V.copy(cqT[:, :, pos:pos + n], pv[:, 0:3, 0:n], mt)]
            ct_free[p_] = [mt]
        m_lat = [V.last(), S.last()]
        barrier()
        stage("qrope")
        top[0] = base_mla + KD * NC + NS * ROPE
        qt = [take(MH * ROPE) for _ in range(2)]
        qr = [take(MH * ROPE) for _ in range(2)]
        tm = [take(MH * H2) for _ in range(4)]
        qr_free = [[], []]
        for s, (pos, n) in enumerate(SLOT):
            p_ = s % 2
            bk = psum_ring.take()
            mt = PE.mms([(bk.ap[0:n, :], cqT[:, k, pos:pos + n], w_uq[:, k, MH * NOPE:], k == 0, k == 2) for k in range(3)],
                        m_wu, bk.free)
            bk.free = [S.copy(qt[p_][0:n, :], bk.ap[0:n, :], mt, V.last())]

            def halves(t):
                v = t[0:n, :].rearrange("p (h u c) -> p u h c", u=2, c=H2)
                return v[:, 0], v[:, 1]
            cs = (bc_mid(rope_cs[0:n, s, 0:H2], MH), bc_mid(rope_cs[0:n, s, H2:], MH))
            a = rotate(halves(qr[p_]), halves(qt[p_]), cs, n,
                       [t_[0:n, :].rearrange("p (h c) -> p h c", h=MH) for t_ in tm], n, S.last(), qr_free[p_])
            bk = psum_ring.take()
            pv = four(bk.ap)
            mt = PE.mms([(pv[:, j, 0:n], qr[p_][0:n, P * j:P * (j + 1)], ident[0:n, 0:n], None, None) for j in range(4)],
                        a, bk.free)
            qr_free[p_] = [mt]
            bk.free = [S.copy(qrT[:, :, pos:pos + n], pv[:, :, 0:n], mt)]

        barrier()
        stage("mla")
        top[0] = base_mla
        oT = take(MH, L)
        vv = take(NS, 4 * VH)
        qn, kn = [take(L) for _ in range(2)], [take(L) for _ in range(2)]
        Pb = [take(L) for _ in range(2)]
        PTb = [take(NS, P) for _ in range(2)]
        causal = take(P)
        a = G.set(causal, 0.0)
        m_cau = keep(causal, causal, [[-1, P]], 0, 1, ALU.is_ge, NEG, a)
        sm = [[take(1) for _ in range(3)] for _ in range(2)]
        score_ring = Ring([Buf(psum[:, 1536 * i:1536 * (i + 1)]) for i in range(2)])
        side_ring = Ring([Buf(banks[6]), Buf(banks[7])])
        qk_free, p_free, pt_free = [[], []], [[], []], [[], []]
        vv_free = []
        order = [NT] + list(range(NT))
        it = 0
        for hh in range(MH):
            if hh % 4 == 0:
                for s, (pos, n) in enumerate(SLOT):
                    bk = side_ring.take()
                    mt = PE.mms([(bk.ap[0:n, :], ckvT[:, k, pos:pos + n], w_uv[:, k, P * hh:P * (hh + 4)], k == 0, k == 1)
                                 for k in range(2)], bk.free)
                    bk.free = [S.copy(vv[0:n, s, :], bk.ap[0:n, :], mt, vv_free)]
                m_vv = S.last()
            q_, k_ = qn[hh % 2], kn[hh % 2]
            for dst, w_, src, nk in ((q_, w_uq, cqT, 3), (k_, w_uk, ckvT, 2)):
                for c0 in range(0, L, 512):
                    c1 = min(L, c0 + 512)
                    bk = side_ring.take()
                    mt = PE.mms([(bk.ap[:, 0:c1 - c0], w_[:, k, P * hh:P * (hh + 1)], src[:, k, c0:c1], k == 0, k == nk - 1)
                                 for k in range(nk)], bk.free)
                    bk.free = [S.copy(dst[:, c0:c1], bk.ap[:, 0:c1 - c0], mt, qk_free[hh % 2])]
            m_qk = S.last()
            pr = slice(64 * (hh % 2), 64 * (hh % 2) + 64)
            for qi, s in enumerate(order):
                pos, n = SLOT[s]
                kc = pos + n
                pb, ptb, (mx, rsu, rdn) = Pb[it % 2], PTb[it % 2], sm[it % 2]
                sc = score_ring.take()
                prods = []
                for c0 in range(0, kc, 512):
                    c1 = min(kc, c0 + 512)
                    prods += [(sc.ap[0:n, c0:c1], q_[:, pos:pos + n], k_[:, c0:c1], True, False),
                              (sc.ap[0:n, c0:c1], qrT[pr, hh // 2, pos:pos + n], krT[pr, c0:c1], False, True)]
                mt = PE.mms(prods, m_qk, sc.free)
                a = V.tt(sc.ap[0:n, pos:kc], sc.ap[0:n, pos:kc], causal[0:n, 0:n], ALU.add, mt, m_cau)
                a = V.red(mx[0:n, :], sc.ap[0:n, 0:kc], ALU.max, a, p_free[it % 2])
                a = V.ts(mx[0:n, :], mx[0:n, :], -SCALE, None, ALU.mult, None, a)
                a = S.act(pb[0:n, 0:kc], sc.ap[0:n, 0:kc], ACT.Exp, a, p_free[it % 2], bias=mx[0:n, :], scale=SCALE,
                          accum=rsu[0:n, :])
                m_exp = a
                a = V.recip(rdn[0:n, :], rsu[0:n, :], a)
                a = V.ts(pb[0:n, 0:kc], pb[0:n, 0:kc], rdn[0:n, :], None, ALU.mult, None, a)
                keys = order[:qi + 1]
                cp = []
                for j0 in range(0, len(keys), 4):
                    ks_ = keys[j0:j0 + 4]
                    bk = side_ring.take()
                    pv = four(bk.ap)
                    prods = []
                    for j, ks in enumerate(ks_):
                        kp, kn_ = SLOT[ks]
                        prods.append((pv[0:kn_, j, 0:n], pb[0:n, kp:kp + kn_], ident[0:n, 0:n], None, None))
                    mt = PE.mms(prods, a, bk.free)
                    if j0 == 0:
                        S.copy(ptb[0:N_META, 0, 0:n], pv[0:N_META, 0, 0:n], mt, pt_free[it % 2])
                        if len(ks_) > 1:
                            S.copy(ptb[:, 1:len(ks_), 0:n], pv[:, 1:len(ks_), 0:n], mt)
                        bk.free = [S.last()]
                    else:
                        bk.free = [V.copy(ptb[:, j0:j0 + len(ks_), 0:n], pv[:, 0:len(ks_), 0:n], mt, pt_free[it % 2])]
                    cp.append(bk.free[0])
                p_free[it % 2] = [mt]
                ov = sc.ap[:, 1024 + 256:1024 + 256 + n]
                vh = VH * (hh % 4)
                mt = PE.mms([(ov, vv[0:SLOT[ks][1], ks, vh:vh + VH], ptb[0:SLOT[ks][1], j, 0:n], j == 0, j == len(keys) - 1)
                             for j, ks in enumerate(keys)], cp, m_vv, m_exp)
                pt_free[it % 2] = [mt]
                sc.free = [S.copy(oT[:, hh, pos:pos + n], ov, mt)]
                it += 1
            qk_free[hh % 2] = [mt]
            vv_free = [mt]
        dump("oT", oT)
        barrier()
        stage("out2")
        top[0] = base_mla + MH * L
        w_o = take(MH, D)
        m_wo = SP.dma(dma_sem("w_o"), w_o, io["w_o"])
        for s, (pos, n) in enumerate(SLOT):
            for half in range(2):
                bk = psum_ring.take()
                mt = PE.mms([(bk.ap[0:n, :], oT[:, k, pos:pos + n], w_o[:, k, half_cols(half)], k == 0, k == MH - 1)
                             for k in range(MH)], m_wo, bk.free)
                bk.free = [V.tt(h[0:n, s, half_cols(half)], h[0:n, s, half_cols(half)], bk.ap[0:n, :], ALU.add, mt)]
        dump("h4", h)

        moe(1)

        barrier()
        stage("final")
        top[0] = base_b2
        rstd, junk, grow = take(NS), take(D), take(D)
        o_ring = Ring([Buf(take(D), dma_sem(f"out{i}")) for i in range(3)])
        m_g = SP.dma(dma_sem("final_row"), grow, io["rows"][5:6, :].to_broadcast([P, D]))
        m_r = rms(rstd, junk)
        for s in range(NT):
            ob = o_ring.take()
            a = V.stt(ob.ap, h[:, s, :], rstd[:, s:s + 1], grow, ALU.mult, ALU.mult, m_r, m_g, ob.free)
            ob.free = [SP.dma(ob.sem, io["out"][P * s:P * (s + 1), :], ob.ap, a)]
            marks_out.append(ob.free[0])
        SP.wait(marks_out)

        block = ctx.enter_context(nc.Block())

        @block.tensor
        def _(e):
            PE.play()

        @block.vector
        def _(e):
            V.play()

        @block.scalar
        def _(e):
            S.play()

        @block.gpsimd
        def _(e):
            G.play()

        @block.sync
        def _(e):
            SP.play()


def kernel(**inputs):
    import numpy as _np
    import concourse.bacc as _bacc
    from concourse import mybir as _mybir
    from concourse.bass_utils import run_bass_kernel_spmd as _run

    a = {k: _np.asarray(v) for k, v in inputs.items()}

    def ktile(w):
        return _np.ascontiguousarray(w.reshape(-1, P, w.shape[-1]).transpose(1, 0, 2))

    arrays = {"x": a["x"][0], "meta": a["meta_tokens_2"], "sinks": a["attn_sinks"]}
    for name, c0, n in GROUPS:
        arrays["w_in_" + name] = ktile(a["w_in"][0][:, c0:c0 + n])
    arrays["w_out"] = ktile(a["w_out"][0])
    arrays["lru_wa"], arrays["lru_wx"] = a["lru_wa"][0], a["lru_wx"][0]
    arrays["w2a2"] = _np.concatenate([a["rwkv_w2"][0], a["rwkv_a2"][0]], axis=0)

    def cols(v):
        return v.reshape(-1, P).T
    mu = a["rwkv_mu"][0]
    mu_wa = _np.zeros((P, 1), mu.dtype)
    mu_wa[0:HD, 0] = mu[3 * 256:]
    chan = [a["conv_w"][0].reshape(4, 2, P).transpose(2, 1, 0).reshape(P, 8), cols(a["conv_b"]), cols(a["lru_ba"]),
            cols(a["lru_bx"]), cols(a["lru_lambda"]), cols(mu[0:3 * 256]), mu_wa, cols(a["rwkv_w0"]), cols(a["rwkv_a0"]),
            cols(a["rwkv_kk"]), cols(a["rwkv_ka"]), cols(a["rwkv_rk"]), cols(a["rwkv_gn_w"]), cols(a["rwkv_gn_b"]),
            cols(a["a_norm_2"]), cols(a["kv_norm_2"]), cols(a["b_norm_2"]), cols(a["b_q_norm_2"]), cols(a["kv_lat_norm_2"])]
    arrays["chan"] = _np.concatenate(chan, axis=1)
    arrays["rows"] = _np.stack([a["ln_g"][0], a["ln_b"][0], a["a_scale_2"][0], a["ffn_norm_2"][0], a["ffn_norm_2"][1],
                                a["final_norm_2"]])
    arrays["a_w"] = ktile(a["a_w_2"][0].reshape(D, 256))
    arrays["w_router"] = _np.stack([ktile(_np.concatenate([a["router_g_2"][i], a["router_e_2"][i]], axis=1)) for i in range(2)])
    arrays["b_router"] = _np.concatenate([a["router_g_bias_2"], a["router_e_bias_2"]], axis=1)
    gu = _np.concatenate([a["w_gate_2"], a["w_up_2"]], axis=3).reshape(2 * NE, KD, P, 2 * DE).transpose(0, 2, 1, 3)
    dn = a["w_down_2"].reshape(2 * NE, 2, P, D).transpose(0, 2, 1, 3)
    arrays["w_exp"] = _np.concatenate([gu.reshape(2 * NE, P, -1), dn.reshape(2 * NE, P, -1)], axis=2)
    arrays["w_c"] = ktile(_np.concatenate([a["w_dkv_2"], a["b_w_dq_2"][0]], axis=1))
    uq = a["b_w_uq_2"][0]
    arrays["w_uq"] = ktile(_np.concatenate([uq[:, :, :NOPE].reshape(QL, -1), uq[:, :, NOPE:].reshape(QL, -1)], axis=1))
    arrays["w_uk"] = ktile(a["w_uk_2"].reshape(KVL, -1))
    arrays["w_uv"] = ktile(a["w_uv_2"].reshape(KVL, -1))
    arrays["w_o"] = ktile(a["b_w_o_2"][0])
    freq = (_np.float32(10000.0) ** (-_np.arange(0, ROPE, 2, dtype=_np.float32) / _np.float32(ROPE))).astype(_np.float32)
    ang = _np.arange(L, dtype=_np.float32)[:, None] * freq[None, :]
    table = _np.concatenate([_np.cos(ang), _np.sin(ang)], axis=1).astype(_np.float32)
    rope = _np.zeros((P, NS, ROPE), _np.float32)
    for s, (pos, n) in enumerate(SLOT):
        rope[0:n, s] = table[pos:pos + n]
    arrays["rope"] = rope

    nc = _bacc.Bacc("TRN2", target_bir_lowering=False, num_devices=1)
    arrays = {f"in_{k}": _np.ascontiguousarray(v) for k, v in arrays.items()}
    io = {k[3:]: nc.dram_tensor(k, v.shape, _mybir.dt.from_np(v.dtype), kind="ExternalInput").ap() for k, v in arrays.items()}
    io["out"] = nc.dram_tensor("out_0", (T, D), _mybir.dt.float32, kind="ExternalOutput").ap()
    dumps = {k: nc.dram_tensor("dump_" + k, shp, _mybir.dt.float32, kind="ExternalOutput").ap() for k, shp in DUMPS.items()}
    build(nc, io, dumps)
    r = _run(nc, [arrays], core_ids=[0])
    return r.results[0]["out_0"].reshape(1, T, D)
```

```python
from contextlib import ExitStack

import numpy as np

import concourse.bass as bass
from concourse import mybir

F32 = mybir.dt.float32
BF16 = mybir.dt.bfloat16
I32 = mybir.dt.int32
U32 = mybir.dt.uint32
ALU = mybir.AluOpType
ACT = mybir.ActivationFunctionType
AX = mybir.AxisListType

P = 128
D = 1024
KD = D // P
T = 1024
NT = T // P
HD = 64
AH, AKV = 8, 2
C_LRU = 8.0
LN_EPS, GN_EPS, RMS_EPS = 1e-5, 64e-5, 1e-6
ALPHA = 2.0 ** 0.25
EXP_HALF = float(np.exp(-0.5))
CH = 64

N_META = 16
L = T + N_META
NS = NT + 1
WINDOWS = (2, 4, 8, 16)
PADW = max(WINDOWS)
MH, NOPE, ROPE, VH = 8, 128, 64, 128
QL, KVL = 384, 256
SCALE = (NOPE + ROPE) ** -0.5
NEG = -1e30
NG, EPG = 4, 8
NE = NG * EPG
DE = 256
NOV = (2 * L) // P
NBLK = NE + NOV
SLOTS = NBLK * P

SLOT = [(N_META + P * s, P) for s in range(NT)] + [(0, N_META)]

GROUPS = [("q", 0, 512), ("kv", 512, 256), ("ga", 768, 512), ("lru", 1280, 512),
          ("rk", 1792, 512), ("vwa", 2304, 320), ("gc", 2624, 256)]

CHAN = [("conv_w", 8), ("conv_b", 2), ("lru_ba", 2), ("lru_bx", 2), ("lam", 2), ("mu", 6), ("mu_wa", 1),
        ("w0", 2), ("a0", 2), ("k_k", 2), ("k_a", 2), ("r_k", 2), ("gn_w", 2), ("gn_b", 2),
        ("a_norm", 8), ("kv_norm", 8), ("b_norm", 8), ("q_norm", 3), ("kv_lat", 2)]
CHAN_AT, _n = {}, 0
for _name, _w in CHAN:
    CHAN_AT[_name] = _n
    _n += _w
N_CHAN = _n
DUMPS = {}
ROWS = ["ln_g", "ln_b", "a_scale", "ffn0", "ffn1", "final"]


class Mark:

    def __init__(self, sem, value):
        self.sem, self.value = sem, value


class Lane:

    def __init__(self, engine, new_sem, name):
        self.e, self.new_sem, self.name = engine, new_sem, name
        self.queue, self.waited = [], {}
        self.sem, self.count = None, 0

    def stage(self, name):
        if self.count or self.sem is None:
            self.sem = self.new_sem(f"{self.name}_{name}")
        self.count = 0

    def last(self):
        return Mark(self.sem, self.count) if self.count else None

    def wait(self, marks):
        for m in marks:
            if m is None:
                continue
            if isinstance(m, (list, tuple)):
                self.wait(m)
            elif self.waited.get(m.sem, 0) < m.value:
                self.waited[m.sem] = m.value
                self.queue.append(lambda m=m: self.e.wait_ge(m.sem, m.value))

    def do(self, make, *after):
        self.wait(after)
        sem = self.sem
        self.queue.append(lambda: make().then_inc(sem, 1))
        self.count += 1
        return Mark(self.sem, self.count)

    def raw(self, make, *after):
        self.wait(after)
        self.queue.append(make)

    def dma(self, sem, out, in_, *after):
        self.wait(after)
        self.queue.append(lambda: self.e.dma_start(out, in_).then_inc(sem.sem, 16))
        return sem.next()

    def play(self, queue=None):
        for make in (self.queue if queue is None else queue):
            make()


class DmaSem:

    def __init__(self, sem):
        self.sem, self.value = sem, 0

    def next(self):
        self.value += 16
        return Mark(self.sem, self.value)


class Vec(Lane):

    def tt(self, out, a, b, op, *after):
        return self.do(lambda: self.e.tensor_tensor(out, a, b, op), *after)

    def ts(self, out, a, s1, s2, op0, op1, *after):
        if op1 is None:
            return self.do(lambda: self.e.tensor_scalar(out, a, s1, None, op0), *after)
        return self.do(lambda: self.e.tensor_scalar(out, a, s1, s2, op0, op1), *after)

    def stt(self, out, a, s, b, op0, op1, *after):
        return self.do(lambda: self.e.scalar_tensor_tensor(out=out, in0=a, scalar=s, in1=b, op0=op0, op1=op1), *after)

    def copy(self, out, a, *after):
        return self.do(lambda: self.e.tensor_copy(out, a), *after)

    def red(self, out, a, op, *after):
        return self.do(lambda: self.e.tensor_reduce(out, a, AX.X, op), *after)

    def recip(self, out, a, *after):
        return self.do(lambda: self.e.reciprocal(out, a), *after)

    def set(self, out, value, *after):
        return self.do(lambda: self.e.memset(out, value), *after)


class Act(Lane):

    def act(self, out, a, func, *after, bias=0.0, scale=1.0, accum=None):
        if accum is not None:
            return self.do(lambda: self.e.activation(out, a, func, bias=bias, scale=scale, accum_out=accum), *after)
        return self.do(lambda: self.e.activation(out, a, func, bias=bias, scale=scale), *after)

    def copy(self, out, a, *after, scale=1.0):
        return self.do(lambda: self.e.activation(out, a, ACT.Copy, bias=0.0, scale=scale), *after)


class Ten(Lane):

    def mms(self, products, *after):
        self.wait(after)
        sem = self.sem

        def make():
            for i, (out, lhsT, rhs, start, stop) in enumerate(products):
                if start is None:
                    ins = self.e.transpose(out, lhsT, rhs)
                else:
                    ins = self.e.matmul(out, lhsT, rhs, start=start, stop=stop, skip_group_check=True)
                if i == len(products) - 1:
                    ins.then_inc(sem, 1)
        self.queue.append(make)
        self.count += 1
        return Mark(self.sem, self.count)


class Buf:

    def __init__(self, ap, sem=None):
        self.ap, self.free, self.sem = ap, [], sem


class Ring:
    def __init__(self, bufs):
        self.bufs, self.at = bufs, 0

    def take(self):
        b = self.bufs[self.at % len(self.bufs)]
        self.at += 1
        return b


def pipelined(items):
    live = []
    for item in items:
        live.append(item)
        live = [g for g in live if next(g, "done") != "done"]
    while live:
        live = [g for g in live if next(g, "done") != "done"]


def together(*streams):
    live = list(streams)
    while live:
        live = [g for g in live if next(g, "done") != "done"]


def bc_mid(ap, n):
    return ap.unsqueeze(1).to_broadcast([ap.shape[0], n, ap.shape[1]])


def bc_last(ap, n):
    return ap.unsqueeze(2).to_broadcast([ap.shape[0], ap.shape[1], n])


def build(nc, io, dumps):
    ctx = ExitStack()
    with ctx:
        def new_sem(name):
            return ctx.enter_context(nc.semaphore(name))

        def dsem(name):
            return DmaSem(new_sem("dma_" + name))

        PE = Ten(nc.tensor, new_sem, "pe")
        V = Vec(nc.vector, new_sem, "dve")
        G = Vec(nc.gpsimd, new_sem, "pool")
        S = Act(nc.scalar, new_sem, "act")
        SP = Lane(nc.sync, new_sem, "sp")
        lanes = [PE, V, G, S, SP]
        compute = [PE, V, G, S]

        def stage(name):
            for lane in compute:
                lane.stage(name)

        ARENA = 53000
        arena = ctx.enter_context(nc.sbuf_tensor("arena", [P, ARENA], F32))
        psum = ctx.enter_context(nc.psum_tensor("psum", [P, 8 * 512], F32))
        top = [0]

        def take(*dims):
            n = int(np.prod(dims))
            o = top[0]
            top[0] += n + (n % 2)
            assert top[0] <= ARENA, (top[0], dims)
            v = arena[:, o:o + n]
            if len(dims) == 2:
                v = v.rearrange("p (a b) -> p a b", a=dims[0])
            if len(dims) == 3:
                v = v.rearrange("p (a b c) -> p a b c", a=dims[0], b=dims[1])
            return v

        def four(ap):
            return ap.rearrange("p (a b) -> p a b", a=4)

        banks = [psum[:, 512 * i:512 * (i + 1)] for i in range(8)]
        psum_ring = Ring([Buf(b) for b in banks])
        marks_out = []
        xn_dram = nc.dram_tensor("xn_rows", (L, D), F32, kind="Internal").ap()
        y_dram = nc.dram_tensor("expert_rows", (SLOTS, D), F32, kind="Internal").ap()

        def barrier():
            ms = [lane.last() for lane in compute] + [Mark(d.sem, d.value) for d in all_dma if d.value]
            for lane in lanes:
                lane.wait(ms)
            for b in psum_ring.bufs:
                b.free = []

        all_dma = []

        by_name = {}

        def dma_sem(name):
            if name not in by_name:
                by_name[name] = dsem(name)
                all_dma.append(by_name[name])
            return by_name[name]

        def dump(name, ap, *after):
            if dumps is not None and name in dumps:
                after = after or tuple(lane.last() for lane in compute)
                marks_out.append(SP.dma(dma_sem("dump_" + name), dumps[name], ap, *after))

        stage("const")
        ident = take(P)
        chan = take(N_CHAN)
        one_col, zero_col = take(1), take(1)
        eps_ln, eps_gn, eps_rms, eps_kk = take(1), take(1), take(1), take(1)
        ones = take(P)
        pair_ones = take(P)
        G.set(ident, 0.0)
        G.set(ones, 1.0)
        G.set(pair_ones, 1.0)
        G.set(one_col, 1.0)
        G.set(zero_col, 0.0)
        G.set(eps_ln, LN_EPS)
        G.set(eps_gn, GN_EPS)
        G.set(eps_rms, RMS_EPS)
        m = G.set(eps_kk, 1e-12)

        def keep(out, in_, pattern, base, mult, op, fill, *after):
            return G.do(lambda: G.e.affine_select(out=out, in_=in_, pattern=pattern, compare_op=op, fill=fill,
                                                  base=base, channel_multiplier=mult), *after)

        m = keep(ident, ident, [[-1, P]], 0, 1, ALU.not_equal, 1.0, m)

        def same_block(t, n, *after):
            v = t.rearrange("p (b c) -> p b c", c=n)
            a = keep(v, v, [[-n, P // n], [0, n]], 0, 1, ALU.is_ge, 0.0, *after)
            return keep(v, v, [[n, P // n], [0, n]], n - 1, -1, ALU.is_ge, 0.0, a)

        m_const = same_block(pair_ones, HD, m)
        d_chan = dma_sem("chan")
        m_chan = SP.dma(d_chan, chan, io["chan"])

        def col(name, i=0, rows=P):
            c = CHAN_AT[name] + i
            return chan[0:rows, c:c + 1]

        zero_rows = arena[:, ARENA - D:ARENA]
        m_zrows = G.set(zero_rows, 0.0)

        h_at = top[0]
        h = take(NS, D)
        top[0] = h_at
        w_bufs = Ring([Buf(take(KD, 512), dma_sem(f"w_in{i}")) for i in range(2)])
        top[0] = h_at + NS * D
        xT = take(KD, T)
        yT = take(KD, T)
        base_b1 = top[0]

        stage("xT")
        x_bufs = Ring([Buf(take(D), dma_sem(f"x{i}")) for i in range(3)])
        for i in range(NT):
            xb = x_bufs.take()
            m = SP.dma(xb.sem, xb.ap, io["x"][P * i:P * (i + 1), :], xb.free)
            if i == 0:
                w_q = w_bufs.take()
                m_wq = SP.dma(w_q.sem, w_q.ap, io["w_in_q"])
            rd = []
            for half in range(2):
                bk = psum_ring.take()
                pv = bk.ap.rearrange("p (a b) -> p a b", a=4)
                mt = PE.mms([(pv[:, k, :], xb.ap[:, P * (4 * half + k):P * (4 * half + k + 1)], ident, None, None)
                             for k in range(4)], m, m_const, bk.free)
                dst = xT[:, 4 * half:4 * half + 4, P * i:P * (i + 1)]
                bk.free = [(V.copy if half else S.copy)(dst, pv, mt)]
                rd.append(mt)
            xb.free = rd
        m_xT = [V.last(), S.last()]
        top[0] = base_b1

        def load_group(name, width):
            b = w_bufs.take()
            wv = b.ap.rearrange("p a b -> p (a b)")[:, 0:KD * width].rearrange("p (a b) -> p a b", a=KD)
            mk = SP.dma(b.sem, wv, io["w_in_" + name], b.free)
            return b, wv, mk

        def project(w, c0, width, m_w, evac):
            mt = None
            for half in range(2):
                bk = psum_ring.take()
                mt = PE.mms([(bk.ap[0:width, :], w[:, k, c0:c0 + width], xT[:, k, 512 * half:512 * half + 512],
                              k == 0, k == KD - 1) for k in range(KD)], m_w, m_xT, bk.free)
                bk.free = evac(half, bk.ap[0:width, :], mt)
            return mt

        def half_cols(half):
            return slice(512 * half, 512 * half + 512)

        stage("qkv")
        rkv = take(6, T + 2)
        wa = take(T + 2)
        xb = take(2, T + 4)
        base_wa = top[0] - (T + 2) - 2 * (T + 4)
        bonus = take(2, T)
        base_swa = top[0] - 2 * T
        top[0] = base_swa
        qT = take(4, T)
        kd = take(AKV, T)
        v_tok = take(NT, P)
        sig = Ring([Buf(take(512)) for _ in range(2)])
        for mt_i in range(4):
            mt = project(w_q.ap, P * mt_i, P, m_wq,
                         lambda hf, ps, mk, mt_i=mt_i: [S.copy(qT[:, mt_i, half_cols(hf)], ps, mk, scale=HD ** -0.5)])
        w_q.free = [mt]
        wb, w, m_w = load_group("kv", 256)

        def evac_k(hf, ps, mk):
            for kv in range(AKV):
                for dst in range(2):
                    r = V.copy(kd[64 * dst:64 * dst + 64, kv, half_cols(hf)], ps[64 * kv:64 * kv + 64, :], mk)
            return [r]
        project(w, 0, P, m_w, evac_k)
        for g in range(2):
            bk = psum_ring.take()
            pv = bk.ap.rearrange("p (a b) -> p a b", a=4)
            prods = []
            for j in range(4):
                i = 4 * g + j
                prods += [(pv[:, j, :], xT[:, k, P * i:P * (i + 1)], w[:, k, P:2 * P], k == 0, k == KD - 1)
                          for k in range(KD)]
            mt = PE.mms(prods, m_w, m_xT, bk.free)
            bk.free = [S.copy(v_tok[:, 4 * g:4 * g + 4, :], pv, mt)]
        wb.free = [mt]

        def gate(y_at):
            def evac(hf, ps, mk):
                sb = sig.take()
                a = S.act(sb.ap, ps, ACT.Sigmoid, mk, sb.free)
                r = V.tt(yT[:, y_at, half_cols(hf)], ps, sb.ap, ALU.mult, a)
                sb.free = [r]
                return [r]
            return evac

        wb, w, m_w = load_group("ga", 512)
        fill = dma_sem("y_fill")
        for b in range(NE, NBLK):
            m_yfill = SP.dma(fill, y_dram[P * b:P * (b + 1), :], zero_rows, m_zrows)
        for j in range(4):
            mt = project(w, P * j, P, m_w, gate(j))
        wb.free = [mt]
        m_q, m_kvg = S.last(), V.last()

        stage("swa")
        band = take(2, P)
        mk_ = G.set(band, 0.0)
        mk_ = keep(band[:, 0, :], band[:, 0, :], [[1, P]], 0, -1, ALU.is_gt, NEG, mk_)
        m_band = keep(band[:, 1, :], band[:, 1, :], [[-1, P]], 0, 1, ALU.is_ge, NEG, mk_)
        sink_row, sink = take(AH), take(AH)
        m_s = SP.dma(dma_sem("sinks"), sink_row, io["sinks"].to_broadcast([P, AH]))
        ORDER = [0, 2, 1, 3, 4, 6, 5, 7]
        for g in range(2):
            V.copy(sink[:, 4 * g:4 * g + 4].rearrange("p (c b) -> p b c", c=2),
                   sink_row[:, 4 * g:4 * g + 4].rearrange("p (b c) -> p b c", b=2), m_s)
        m_sink = V.last()
        Pm = [take(AH, 2 * P) for _ in range(2)]
        PT = [take(2 * AH, P) for _ in range(2)]
        st = [[take(AH) for _ in range(6)] for _ in range(3)]
        pm_free, pt_free = [[], [], []], [[], []]
        for lane in (V, S):
            lane.wait([m_yfill])
        V.set(xb[:, :, 0:3], 0.0)
        V.set(rkv[:, :, 0:1], 0.0)
        m_pad = V.set(wa[0:64, 0:1], 0.0)

        def window(n):
            pm, pt, (mx, nm, rs, es, den, rden) = Pm[n % 2], PT[n % 2], st[n % 3]
            c0 = 0 if n else P
            k0 = P * (n - 1) + c0
            wd = 2 * P - c0
            for b in range(4):
                bk = psum_ring.take()
                pv = bk.ap.rearrange("p (a b) -> p a b", a=2)
                prods = []
                for j in range(2):
                    hh = ORDER[2 * b + j]
                    pr = slice(64 * (hh % 2), 64 * (hh % 2) + 64)
                    prods.append((pv[:, j, c0:], qT[pr, hh // 2, P * n:P * (n + 1)], kd[pr, hh // 4, k0:k0 + wd], True, True))
                mt = PE.mms(prods, m_q, m_kvg, bk.free)
                a = V.tt(pm[:, 2 * b:2 * b + 2, c0:], pv[:, :, c0:],
                         bc_mid(band.rearrange("p a b -> p (a b)")[:, c0:], 2), ALU.add, mt, m_band, pm_free[n % 2])
                bk.free = [a]
            a = V.red(mx, pm[:, :, c0:], ALU.max, a)
            a = V.tt(mx, mx, sink, ALU.max, a, m_sink)
            a = V.ts(nm, mx, -1.0, None, ALU.mult, None, a)
            e_in = V.tt(es, sink, nm, ALU.add, a)
            for j in range(AH):
                e = S.act(pm[:, j, c0:], pm[:, j, c0:], ACT.Exp, a, bias=nm[:, j:j + 1], accum=rs[:, j:j + 1])
            e = S.act(es, es, ACT.Exp, e_in)
            yield
            a = V.tt(den, rs, es, ALU.add, e)
            a = V.recip(rden, den, a)
            a = V.tt(pm[:, :, c0:], pm[:, :, c0:], bc_last(rden, wd), ALU.mult, a)
            yield
            parts = [0, 1] if n else [1]
            tr = []
            for b in range(4):
                bk = psum_ring.take()
                pv = bk.ap.rearrange("p (a b) -> p a b", a=4)
                prods = []
                for j in range(2):
                    for u in parts:
                        prods.append((pv[:, 2 * j + u, :], pm[:, 2 * b + j, P * u:P * (u + 1)], ident, None, None))
                mt = PE.mms(prods, a, bk.free)
                if n:
                    src, dst = pv, pt[:, 4 * b:4 * b + 4, :]
                else:
                    src, dst = pv[:, 1::2, :], pt[:, 4 * b + 1:4 * b + 4:2, :]
                bk.free = [(S.copy if b % 2 else V.copy)(dst, src, mt, pt_free[n % 2])]
                tr.append(bk.free[0])
            pm_free[n % 2] = [mt]
            yield
            bk = psum_ring.take()
            pv = bk.ap.rearrange("p (a b) -> p a b", a=4)
            prods = []
            for j, hh in enumerate(ORDER):
                pr = slice(64 * (hh % 2), 64 * (hh % 2) + 64)
                for u in parts:
                    prods.append((pv[pr, hh // 2, :], v_tok[:, n - 1 + u, 64 * (hh // 4):64 * (hh // 4) + 64],
                                  pt[:, 2 * j + u, :], u == parts[0], u == 1))
            mt = PE.mms(prods, tr, bk.free)
            pt_free[n % 2] = [mt]
            bk.free = [V.tt(yT[:, 0:4, P * n:P * (n + 1)], pv, yT[:, 0:4, P * n:P * (n + 1)], ALU.mult, mt)]

        def other_projections():
            def keep_in(dst, c0):
                return lambda hf, ps, mk: [S.copy(dst[:, c0 + 512 * hf:c0 + 512 * hf + 512], ps, mk)]
            for name, width, tiles in (
                    ("rk", 512, [(P * j, P, keep_in(rkv[:, j, :], 1)) for j in range(4)]),
                    ("lru", 512, [(P * j, P, keep_in(xb[:, j, :], 3)) for j in range(2)] +
                     [(256 + P * j, P, gate(4 + j)) for j in range(2)]),
                    ("vwa", 320, [(P * j, P, keep_in(rkv[:, 4 + j, :], 1)) for j in range(2)] +
                     [(256, 64, keep_in(wa[0:64, :], 1))]),
                    ("gc", 256, [(P * j, P, gate(6 + j)) for j in range(2)])):
                wb, w, m_w = load_group(name, width)
                for c0, n, evac in tiles:
                    mt = project(w, c0, n, m_w, evac)
                    wb.free = [mt]
                    yield

        fill = other_projections()

        def windows():
            for n in range(NT):
                next(fill, None)
                next(fill, None)
                yield window(n)
        pipelined(windows())
        for _ in fill:
            pass
        dump("ya", yT[:, 0:4, :])

        barrier()
        stage("prep")
        top[0] = base_swa + 2 * T
        low = [h_at]

        def take_low(*dims):
            n = int(np.prod(dims))
            o = low[0]
            low[0] += n + (n % 2)
            assert low[0] <= base_b1 - KD * T
            v = arena[:, o:o + n]
            return v.rearrange("p (a b) -> p a b", a=dims[0]) if len(dims) == 2 else v

        def rg_lru():
            xc, ra, ib, q_, u_ = take(2, T), take(2, T), take(2, T), take(2, T), take(2, T)
            wa_d, wx_d = take(2, P), take(2, P)
            zz = G.set(wa_d, 0.0)
            zz = G.set(wx_d, 0.0)
            d_l = dma_sem("lru_w")
            for dst, name in ((wa_d, "lru_wa"), (wx_d, "lru_wx")):
                for b in range(4):
                    pr = slice(64 * (b % 2), 64 * (b % 2) + 64)
                    m_lw = SP.dma(d_l, dst[pr, b // 2, 64 * (b % 2):64 * (b % 2) + 64], io[name][b], zz)
            lam = chan[:, CHAN_AT["lam"]:CHAN_AT["lam"] + 2]
            neg, ab, e_, s_, s2, ac, cl, ncl = (take(2) for _ in range(8))
            a = V.ts(neg, lam, -1.0, None, ALU.mult, None, m_chan)
            a = V.tt(ab, lam, neg, ALU.max, a)
            a2 = S.act(e_, ab, ACT.Exp, a, scale=-1.0)
            yield
            a = V.ts(s_, e_, 2.0, None, ALU.add, None, a2)
            a = V.recip(s_, s_, a)
            a = V.tt(s_, s_, e_, ALU.mult, a)
            a = V.tt(s2, s_, s_, ALU.mult, a)
            a = V.ts(ac, s2, 1.0 / 19, 1.0 / 17, ALU.mult, ALU.add, a)
            for c in (15, 13, 11, 9, 7, 5, 3, 1):
                a = V.tt(ac, ac, s2, ALU.mult, a)
                a = V.ts(ac, ac, 1.0 / c, None, ALU.add, None, a)
            a = V.tt(ac, ac, s_, ALU.mult, a)
            a = V.ts(ac, ac, 2.0, None, ALU.mult, None, a)
            a = V.ts(neg, neg, 0.0, None, ALU.max, None, a)
            a = V.tt(ac, ac, neg, ALU.add, a)
            a = V.ts(cl, ac, -C_LRU, None, ALU.mult, None, a)
            m_cl = V.ts(ncl, ac, C_LRU, None, ALU.mult, None, a)
            yield
            m_r = []
            for j in range(2):
                a = V.ts(xc[:, j, :], xb[:, j, 0:T], col("conv_w", 4 * j), col("conv_b", j), ALU.mult, ALU.add)
                for t in range(1, 4):
                    a = V.stt(xc[:, j, :], xb[:, j, t:t + T], col("conv_w", 4 * j + t), xc[:, j, :], ALU.mult, ALU.add, a)
                    yield
                for wt, dst, bias in ((wa_d, ra, "lru_ba"), (wx_d, ib, "lru_bx")):
                    for hf in range(2):
                        bk = psum_ring.take()
                        mt = PE.mms([(bk.ap, wt[:, j, :], xc[:, j, half_cols(hf)], True, True)], a, m_lw, bk.free)
                        bk.free = [S.act(dst[:, j, half_cols(hf)], bk.ap, ACT.Sigmoid, mt, bias=col(bias, j))]
                m_r.append(S.last())
                yield
            m_q = []
            for j in range(2):
                th = S.act(q_[:, j, :], ra[:, j, :], ACT.Tanh, m_r[j], m_cl, scale=ncl[:, j:j + 1])
                ea = S.act(ra[:, j, :], ra[:, j, :], ACT.Exp, th, scale=cl[:, j:j + 1])
                g = G.tt(ib[:, j, :], ib[:, j, :], xc[:, j, :], ALU.mult, m_r[j])
                yield
                a = V.tt(u_[:, j, :], ra[:, j, :], ra[:, j, :], ALU.mult, ea)
                m_q.append((V.stt(q_[:, j, :], u_[:, j, :], 1.0, q_[:, j, :], ALU.add, ALU.mult, a, th), g, a))
                yield
            m_sq = [S.act(q_[:, j, :], q_[:, j, :], ACT.Sqrt, m_q[j][0]) for j in range(2)]
            yield
            for j in range(2):
                a = V.tt(u_[:, j, :], ib[:, j, :], q_[:, j, :], ALU.mult, m_q[j][0], m_q[j][1], m_sq[j])
                yield
                a = V.do(lambda j=j: nc.vector.tensor_tensor_scan(xc[:, j, :], ra[:, j, :], u_[:, j, :], 0.0,
                                                                  ALU.mult, ALU.add), a)
                yield
                V.tt(yT[:, 4 + j, :], yT[:, 4 + j, :], xc[:, j, :], ALU.mult, a)
                yield

        R = [rkv[:, j, 1:T + 1] for j in range(6)]
        sgm, av, Lc, Ep, Em, kk = (take_low(2, T) for _ in range(6))
        base_tmp = low[0]
        tmp = [take_low(T) for _ in range(2)]
        w2a2 = take_low(256)
        reset = take_low(T)
        omka = take_low(2)

        def prepare():
            m_w2 = SP.dma(dma_sem("w2a2"), w2a2[0:64, :], io["w2a2"])
            rz = G.set(reset, 1.0)
            m_reset = G.set(reset.rearrange("p (c s) -> p c s", s=CH)[:, :, 0:1], 0.0, rz)
            m_om = V.ts(omka, chan[:, CHAN_AT["k_a"]:CHAN_AT["k_a"] + 2], -1.0, 1.0, ALU.mult, ALU.add)
            a = V.tt(tmp[0][0:64, :], wa[0:64, 0:T], wa[0:64, 1:T + 1], ALU.subtract)
            m_wa = V.stt(wa[0:64, 1:T + 1], tmp[0][0:64, :], col("mu_wa", 0, 64), wa[0:64, 1:T + 1], ALU.mult, ALU.add, a)
            m_th = S.act(wa[0:32, 1:T + 1], wa[0:32, 1:T + 1], ACT.Tanh, m_wa)
            m_sg, m_sh = [], []
            for j in range(2):
                for dst, rows, bias in ((sgm, slice(0, 32), "w0"), (av, slice(32, 64), "a0")):
                    for hf in range(2):
                        bk = psum_ring.take()
                        mt = PE.mms([(bk.ap, w2a2[rows, P * j:P * (j + 1)], wa[rows, 1 + 512 * hf:513 + 512 * hf], True, True)],
                                    m_th, m_w2, bk.free)
                        bk.free = [S.act(dst[:, j, half_cols(hf)], bk.ap, ACT.Sigmoid, mt, bias=col(bias, j))]
                m_sg.append(S.last())
            for j in (2, 3, 0, 1, 4, 5):
                t_ = tmp[j % 2]
                a = V.tt(t_, rkv[:, j, 0:T], R[j], ALU.subtract, V.last())
                yield
                m_sh.append(V.stt(R[j], t_, col("mu", j), R[j], ALU.mult, ALU.add, a))
                yield
            for j in range(2):
                a = V.do(lambda j=j: nc.vector.tensor_tensor_scan(Lc[:, j, :], reset, sgm[:, j, :], 0.0, ALU.mult, ALU.add),
                         m_sg[j], m_reset)
                a_x = G.tt(sgm[:, j, :], Lc[:, j, :], sgm[:, j, :], ALU.subtract, a)
                m_ep = S.act(Ep[:, j, :], Lc[:, j, :], ACT.Exp, a, scale=-EXP_HALF)
                m_em = S.act(Em[:, j, :], Lc[:, j, :], ACT.Exp, a, scale=EXP_HALF)
                m_ex = S.act(sgm[:, j, :], sgm[:, j, :], ACT.Exp, a_x, scale=-EXP_HALF)
                yield
                a = V.ts(kk[:, j, :], R[2 + j], col("k_k", j), None, ALU.mult, None, m_sh)
                sq = S.act(tmp[0], kk[:, j, :], ACT.Square, a, PE.last())
                for hf in range(2):
                    bk = psum_ring.take()
                    mt = PE.mms([(bk.ap, pair_ones, tmp[0][:, half_cols(hf)], True, True)], sq, bk.free)
                    bk.free = [S.act(tmp[1][:, half_cols(hf)], bk.ap, ACT.Sqrt, mt, V.last(), bias=eps_kk)]
                m_s = S.last()
                yield
                a = V.recip(tmp[1], tmp[1], m_s)
                yield
                m_kk = V.tt(kk[:, j, :], kk[:, j, :], tmp[1], ALU.mult, a)
                yield
                a = V.ts(tmp[1], av[:, j, :], col("k_a", j), omka[:, j:j + 1], ALU.mult, ALU.add, m_kk, m_om)
                a = V.tt(R[2 + j], R[2 + j], tmp[1], ALU.mult, a)
                yield
                m_rk = V.stt(tmp[0], R[j], col("r_k", j), R[2 + j], ALU.mult, ALU.mult, a, PE.last())
                for hf in range(2):
                    bk = psum_ring.take()
                    mt = PE.mms([(bk.ap, pair_ones, tmp[0][:, half_cols(hf)], True, True)], m_rk, bk.free)
                    bk.free = [V.tt(bonus[:, j, half_cols(hf)], bk.ap, R[4 + j][:, half_cols(hf)], ALU.mult, mt)]
                yield
                a = V.tt(av[:, j, :], av[:, j, :], kk[:, j, :], ALU.mult, m_kk, a)
                G.tt(R[2 + j], R[2 + j], Em[:, j, :], ALU.mult, m_rk, m_em)
                G.tt(R[j], R[j], Ep[:, j, :], ALU.mult, m_ep)
                yield
                V.tt(av[:, j, :], av[:, j, :], Em[:, j, :], ALU.mult, a, m_em)
                yield
                V.tt(kk[:, j, :], kk[:, j, :], sgm[:, j, :], ALU.mult, m_ex, a)
                yield

        together(prepare(), rg_lru())
        Bf = [av[:, j, :] for j in range(2)]
        Af = [kk[:, j, :] for j in range(2)]
        dump("yb", yT[:, 4:6, :])

        barrier()
        stage("rwkv")
        Kf, Rf, Vf = [R[2], R[3]], [R[0], R[1]], [R[4], R[5]]
        yb = Lc
        areas = [[base_wa, base_swa], [base_tmp, base_b1 - KD * T],
                 [h_at, h_at + 2 * T], [h_at + 8 * T, h_at + 10 * T], [base_swa + 2 * T, ARENA]]

        def take_dead(*dims):
            n = int(np.prod(dims))
            for area in areas:
                if area[0] + n <= area[1]:
                    o = area[0]
                    area[0] += n
                    v = arena[:, o:o + n]
                    return v.rearrange("p (a b) -> p a b", a=dims[0]) if len(dims) == 2 else v
            raise AssertionError(dims)

        NST = 2 * NT + 1
        STt = take_dead(NST, P).rearrange("p c (a v) -> p c a v", a=2)
        m_state = [V.set(STt[:, 0], 0.0)]
        mN, mNT, mC32, mC64, mUp, mUpS = (take_dead(P) for _ in range(6))
        m_a = G.set(mN, -1.0)
        m_a = keep(mN, mN, [[-1, P]], 0, 1, ALU.is_gt, 0.0, m_a)
        m_a = same_block(mN, 16, m_a)
        m_a = G.set(mNT, -1.0, m_a)
        m_a = keep(mNT, mNT, [[1, P]], 0, -1, ALU.is_gt, 0.0, m_a)
        m_a = same_block(mNT, 16, m_a)

        def off_block(t, n, *after):
            hn = n // 2
            a = G.set(t, 1.0, *after)
            v = t.rearrange("p (b u c) -> p b u c", u=2, c=hn)
            a = G.set(v[:, :, 0, :], 0.0, a)
            a = keep(v, v, [[-n, P // n], [0, 2], [0, hn]], 0, 1, ALU.is_ge, 0.0, a)
            return keep(v, v, [[n, P // n], [0, 2], [0, hn]], hn - 1, -1, ALU.is_ge, 0.0, a)

        m_a = off_block(mC32, 32, m_a)
        m_a = off_block(mC64, 64, m_a)
        m_a = G.set(mUp, 1.0, m_a)
        m_a = keep(mUp, mUp, [[1, P]], 0, -1, ALU.is_ge, 0.0, m_a)
        m_a = same_block(mUp, CH, m_a)
        m_a = G.set(mUpS, 1.0, m_a)
        m_a = keep(mUpS, mUpS, [[1, P]], 0, -1, ALU.is_gt, 0.0, m_a)
        m_mask = same_block(mUpS, CH, m_a)
        sets = [dict(tok=take_dead(8, P), mats=[take_dead(4, P) for _ in range(15)], GT=take_dead(2, P),
                     small=[take_dead(4, HD) for _ in range(3)], stg=take_dead(2, HD), free=[m_mask]) for _ in range(2)]

        def heads(ap, par):
            return ap.rearrange("p (j r) c -> p j r c", r=2)[:, :, par, :]

        def mm4(lhs, rhs, *after):
            bk = psum_ring.take()
            pv = four(bk.ap)
            mt = PE.mms([(pv[:, i, :], lhs[:, i, :], rhs[:, i, :], True, True) for i in range(4)], bk.free, *after)
            return bk, pv, mt

        def tile_chunks(i):
            own = sets[i % 2]
            tk = own["tok"]
            N_, NT_, CT32, CT64, AKT, RBT, RKT, PA, PB, PTA, PTB, XTa, XTb, X_, Q_ = own["mats"]
            GT, (AKV_, U0n, SA), stg = own["GT"], own["small"], own["stg"]
            cols = slice(P * i, P * (i + 1))
            free = own["free"]
            for half, srcs in enumerate(((Bf[0], Bf[1], Kf[0], Kf[1]), (Af[0], Af[1], Vf[0], Vf[1]))):
                bk = psum_ring.take()
                mt = PE.mms([(four(bk.ap)[:, j, :], s_[:, cols], ident, None, None) for j, s_ in enumerate(srcs)], bk.free)
                bk.free = [S.copy(tk[:, 4 * half:4 * half + 4, :], four(bk.ap), mt, free)]
            m_tok = S.last()

            def htok(kind, hh):
                return tk[:, 2 * kind + hh // 2, 64 * (hh % 2):64 * (hh % 2) + 64]
            for par in range(2):
                pr = slice(64 * par, 64 * par + 64)
                A_, B_, K_, R_ = ([f[j][pr, cols] for j in range(2)] for f in (Af, Bf, Kf, Rf))
                bk = psum_ring.take()
                pv = four(bk.ap)
                mt = PE.mms([(pv[:, j, :], A_[j], B_[j], True, True) for j in range(2)] +
                            [(pv[:, 2 + j, :], B_[j], A_[j], True, True) for j in range(2)], bk.free)
                V.tt(heads(N_, par), pv[:, 0:2, :], bc_mid(mN, 2), ALU.mult, mt, free)
                V.tt(heads(NT_, par), pv[:, 2:4, :], bc_mid(mNT, 2), ALU.mult)
                V.tt(heads(CT32, par), pv[:, 2:4, :], bc_mid(mC32, 2), ALU.mult)
                m_n = V.tt(heads(CT64, par), pv[:, 2:4, :], bc_mid(mC64, 2), ALU.mult)
                bk.free = [m_n]
            yield
            m_x = V.tt(XTa, NT_, bc_mid(ident, 4), ALU.add, m_n)
            bk, pv, mt = mm4(NT_, N_, m_n)
            m2 = [S.copy(PA, pv, mt)]
            bk.free = m2[:1]
            bk, pv, mt = mm4(N_, NT_)
            m2.append(V.copy(PTA, pv, mt))
            bk.free = m2[1:]
            yield
            for par in range(2):
                pr = slice(64 * par, 64 * par + 64)
                A_, B_, K_, R_ = ([f[j][pr, cols] for j in range(2)] for f in (Af, Bf, Kf, Rf))
                bk = psum_ring.take()
                pv = four(bk.ap)
                mt = PE.mms([(pv[:, j, :], K_[j], A_[j], True, True) for j in range(2)] +
                            [(pv[:, 2 + j, :], B_[j], R_[j], True, True) for j in range(2)], bk.free)
                V.tt(heads(AKT, par), pv[:, 0:2, :], bc_mid(mUpS, 2), ALU.mult, mt)
                bk.free = [V.tt(heads(RBT, par), pv[:, 2:4, :], bc_mid(mUp, 2), ALU.mult)]
            m_ak = V.last()
            yield
            bk, pv, mt = mm4(PA, XTa, m2, m_x)
            m_x = V.tt(XTb, XTa, pv, ALU.add, mt)
            bk.free = [m_x]
            bk, pv, mt = mm4(PTA, PA)
            m4 = [S.copy(PB, pv, mt)]
            bk.free = m4[:1]
            bk, pv, mt = mm4(PA, PTA)
            m4.append(V.copy(PTB, pv, mt))
            bk.free = m4[1:]
            yield
            for par in range(2):
                pr = slice(64 * par, 64 * par + 64)
                K_, R_ = ([f[j][pr, cols] for j in range(2)] for f in (Kf, Rf))
                bk = psum_ring.take()
                pv = four(bk.ap)
                mt = PE.mms([(pv[:, j, :], K_[j], R_[j], True, True) for j in range(2)], bk.free)
                bk.free = [V.tt(heads(RKT, par), pv[:, 0:2, :], bc_mid(mUp, 2), ALU.mult, mt)]
            m_m = V.last()
            bk, pv, mt = mm4(PB, XTb, m4, m_x)
            m_x = V.tt(XTa, XTb, pv, ALU.add, mt)
            bk.free = [m_x]
            bk, pv, mt = mm4(PTB, PB)
            m8 = S.copy(PA, pv, mt)
            bk.free = [m8]
            yield
            bk = psum_ring.take()
            up = bk.ap[:, 0:4 * HD].rearrange("p (a b) -> p a b", a=4)
            mt = PE.mms([(up[:, hh, :], AKT[:, hh, :], htok(3, hh), True, True) for hh in range(4)], m_ak, m_tok, bk.free)
            m_akv = S.copy(AKV_, up, mt)
            bk.free = [m_akv]
            bk, pv, mt = mm4(PA, XTa, m8, m_x)
            m_x = V.tt(XTb, XTa, pv, ALU.add, mt)
            bk.free = [m_x]
            yield
            bk = psum_ring.take()
            mt = PE.mms([(four(bk.ap)[:, j, :], XTb[:, j, :], ident, None, None) for j in range(4)], m_x, bk.free)
            m_xx = S.copy(X_, four(bk.ap), mt)
            bk.free = [m_xx]
            yield
            bk, pv, mt = mm4(CT32, X_, m_xx)
            m_q_ = S.copy(Q_, pv, mt)
            bk.free = [m_q_]
            yield
            bk, pv, mt = mm4(XTb, Q_, m_q_)
            m_pb = V.tt(PB, X_, pv, ALU.subtract, mt)
            bk.free = [m_pb]
            bk, pv, mt = mm4(Q_, XTb)
            m_x = V.tt(XTa, XTb, pv, ALU.subtract, mt)
            bk.free = [m_x]
            yield
            bk, pv, mt = mm4(CT64, PB, m_pb)
            m_q_ = S.copy(Q_, pv, mt)
            bk.free = [m_q_]
            yield
            bk, pv, mt = mm4(Q_, XTa, m_q_, m_x)
            m_x = V.tt(XTb, XTa, pv, ALU.subtract, mt)
            bk.free = [m_x]
            yield
            bk = psum_ring.take()
            gp = bk.ap[:, 0:2 * P].rearrange("p (a b) -> p a b", a=2)
            mt = PE.mms([(gp[64 * (hh % 2):64 * (hh % 2) + 64, hh // 2, :], htok(2, hh), XTb[:, hh, :], True, True)
                         for hh in range(4)], m_x, bk.free)
            m_g = S.copy(GT, gp, mt)
            bk.free = [m_g]
            bk = psum_ring.take()
            up = bk.ap[:, 0:4 * HD].rearrange("p (a b) -> p a b", a=4)
            mt = PE.mms([(up[:, hh, :], XTb[:, hh, :], AKV_[:, hh, :], True, True) for hh in range(4)], m_akv, bk.free)
            m_u = V.ts(U0n, up, -1.0, None, ALU.mult, None, mt)
            bk.free = [m_u]
            yield "state"
            for c in range(2):
                ci = 2 * i + c
                cr = slice(64 * c, 64 * c + 64)
                for par in range(2):
                    pr = slice(64 * par, 64 * par + 64)
                    bk = psum_ring.take()
                    sv = bk.ap[:, 0:2 * HD].rearrange("p (a b) -> p a b", a=2)
                    mt = PE.mms([(sv[cr, j, :], GT[pr, j, cr], STt[pr, ci, j, :], True, True) for j in range(2)],
                                m_state[-1], m_g, bk.free)
                    m_sa = V.tt(heads(SA, par)[cr], heads(U0n, par)[cr], sv[cr], ALU.subtract, mt, m_u)
                    bk.free = [m_sa]
                yield
                bk = psum_ring.take()
                dv = bk.ap[:, 0:2 * HD].rearrange("p (a b) -> p a b", a=2)
                prods = []
                for hh in range(4):
                    o = dv[64 * (hh % 2):64 * (hh % 2) + 64, hh // 2, :]
                    prods += [(o, htok(1, hh)[cr], htok(3, hh)[cr], True, False),
                              (o, htok(0, hh)[cr], SA[cr, hh, :], False, True)]
                mt = PE.mms(prods, m_sa, bk.free)
                a = V.tt(stg, STt[:, ci], dv, ALU.add, mt, m_state[-1])
                bk.free = [a]
                last_col = P * i + 64 * c + 63
                for j in range(2):
                    m_s = V.ts(STt[:, ci + 1, j, :], stg[:, j, :], Ep[:, j, last_col:last_col + 1], None, ALU.mult, None, a)
                m_state.append(m_s)
                yield
            for par in range(2):
                pr = slice(64 * par, 64 * par + 64)
                bk = psum_ring.take()
                yv = bk.ap[:, 0:2 * P].rearrange("p (a b) -> p a b", a=2)
                prods = []
                for j in range(2):
                    hh = 2 * j + par
                    prods += [(yv[pr, j, :], SA[:, hh, :], RBT[:, hh, :], True, False),
                              (yv[pr, j, :], htok(3, hh), RKT[:, hh, :], False, False)]
                    for c in range(2):
                        prods.append((yv[pr, j, 64 * c:64 * c + 64], STt[pr, 2 * i + c, j, :],
                                      Rf[j][pr, P * i + 64 * c:P * i + 64 * c + 64], False, c == 1))
                mt = PE.mms(prods, m_m, m_state[-1], bk.free)
                bk.free = [S.copy(yb[pr, :, cols], yv[pr], mt)]
            m_y = S.last()
            yield
            y2 = yb[:, :, cols]
            sq2, vv2 = (own["mats"][0].rearrange("p a b -> p (a b)")[:, 256 * u:256 * u + 256].rearrange("p (a b) -> p a b", a=2)
                        for u in range(2))
            bk = psum_ring.take()
            pv = bk.ap[:, 0:2 * P].rearrange("p (a b) -> p a b", a=2)
            mt = PE.mms([(pv[:, j, :], pair_ones, y2[:, j, :], True, True) for j in range(2)], m_y, bk.free)
            a = V.stt(y2, pv, -1.0 / HD, y2, ALU.mult, ALU.add, mt)
            bk.free = [a]
            sq = S.act(sq2, y2, ACT.Square, a)
            yield
            bk = psum_ring.take()
            pv = bk.ap[:, 0:2 * P].rearrange("p (a b) -> p a b", a=2)
            mt = PE.mms([(pv[:, j, :], pair_ones, sq2[:, j, :], True, True) for j in range(2)], sq, bk.free)
            b = S.act(vv2, pv, ACT.Sqrt, mt, bias=eps_gn, scale=1.0 / HD)
            bk.free = [b]
            yield
            b = V.recip(vv2, vv2, b)
            b = V.tt(y2, y2, vv2, ALU.mult, a, b)
            for j in range(2):
                c = V.ts(y2[:, j, :], y2[:, j, :], col("gn_w", j), col("gn_b", j), ALU.mult, ALU.add, b)
            c = V.tt(y2, y2, bonus[:, :, cols], ALU.add, c)
            c = V.tt(yT[:, 6:8, cols], yT[:, 6:8, cols], y2, ALU.mult, c)
            own["free"] = [c, mt]

        def two_tiles():
            live, i = [tile_chunks(0)], 1
            while live:
                for g in list(live):
                    said = next(g, "done")
                    if said == "done":
                        live.remove(g)
                    elif said == "state" and i < NT:
                        start = tile_chunks(i)
                        i += 1
                        live.append(start)
        two_tiles()
        dump("yc", yT[:, 6:8, :])

        barrier()
        stage("out1")
        top[0] = base_b1
        wo1 = take(KD, D)
        m_wo = [SP.dma(dma_sem(f"w_out{k}"), wo1[:, k, :], io["w_out"][:, k, :]) for k in range(KD)]
        lng, lnb = take(D), take(D)
        xr = Ring([Buf(take(D), dma_sem(f"xr{i}")) for i in range(2)])
        stats = take(12)
        d_ln = dma_sem("ln")
        SP.dma(d_ln, lng, io["rows"][0:1, :].to_broadcast([P, D]))
        m_ln = SP.dma(d_ln, lnb, io["rows"][1:2, :].to_broadcast([P, D]))
        mvs = [take(2) for _ in range(NT)]
        for g in range(0, NT, 4):
            bks = [[psum_ring.take() for _ in range(2)] for _ in range(4)]
            order = [(k, j) for k in range(KD) for j in range(4)] if g == 0 else [(k, j) for j in range(4) for k in range(KD)]
            for k, j in order:
                for hf in range(2):
                    bk, i = bks[j][hf], g + j
                    bk.mt = PE.mms([(bk.ap, yT[:, k, P * i:P * (i + 1)], wo1[:, k, half_cols(hf)], k == 0, k == KD - 1)],
                                   m_wo[k], bk.free if k == 0 else None)
            for j in range(4):
                i = g + j
                mv = mvs[i]
                xb_ = xr.take()
                m = SP.dma(xb_.sem, xb_.ap, io["x"][P * i:P * (i + 1), :], xb_.free)
                a_ = []
                for hf in range(2):
                    bk = bks[j][hf]
                    bk.free = [V.stt(h[:, i, half_cols(hf)], xb_.ap[:, half_cols(hf)], ALPHA, bk.ap, ALU.mult, ALU.add,
                                     bk.mt, m)]
                    a_.append(V.do(lambda i=i, hf=hf: nc.vector.bn_stats(stats[:, 6 * hf:6 * hf + 6], h[:, i, half_cols(hf)]),
                                   bk.free[0]))
                xb_.free = [V.last()]
                a = V.do(lambda mv=mv: nc.vector.bn_aggr(mv, stats), a_)
                s = S.act(mv[:, 1:2], mv[:, 1:2], ACT.Sqrt, a, bias=eps_ln)
                a = V.recip(mv[:, 1:2], mv[:, 1:2], s)
                a = V.ts(h[:, i, :], h[:, i, :], mv[:, 0:1], mv[:, 1:2], ALU.subtract, ALU.mult, a)
                a = G.tt(h[:, i, :], h[:, i, :], lng, ALU.mult, a, m_ln)
                a = G.tt(h[:, i, :], h[:, i, :], lnb, ALU.add, a)
        z = V.set(h[:, NT, :], 0.0)
        SP.dma(dma_sem("meta"), h[0:N_META, NT, :], io["meta"], z)
        barrier()
        dump("h1", h)
        base_b2 = h_at + NS * D

        def rms(dst_rstd, junk, *after):
            for s in range(NS):
                a = S.act(junk, h[:, s, :], ACT.Square, after, S.last(), accum=dst_rstd[:, s:s + 1])
            a = S.act(dst_rstd, dst_rstd, ACT.Sqrt, a, bias=eps_rms, scale=1.0 / D)
            return V.recip(dst_rstd, dst_rstd, a)

        barrier()
        stage("pool")
        top[0] = base_b2
        hn = take(KD, PADW + L)
        xn = take(3, D)
        rstd, junk = take(NS), take(D)
        sa, sb_ = take(PADW + L), take(PADW + L)
        pooled = take(KD, L)
        a_w = take(KD, 256)
        arow = take(D)
        inv = take(4, PADW)
        edge = take(PADW)
        d_pw = dma_sem("pool_w")
        SP.dma(d_pw, a_w, io["a_w"])
        m_aw = SP.dma(d_pw, arow, io["rows"][2:3, :].to_broadcast([P, D]))
        cnt_i = take(PADW)
        a = G.do(lambda: G.e.iota(cnt_i.bitcast(I32), [[1, PADW]], base=1, channel_multiplier=0))
        a = V.copy(edge, cnt_i.bitcast(I32), a)
        for g, w in enumerate(WINDOWS):
            c = V.ts(inv[:, g, :], edge, float(w), None, ALU.min, None, a)
        m_inv = V.recip(inv, inv, c)
        z = V.set(hn[:, :, 0:PADW], 0.0)
        V.set(sa[:, 0:PADW], 0.0)
        m_z = V.set(sb_[:, 0:PADW], 0.0)
        m_r = rms(rstd, junk)
        xn_free = [[], [], []]
        for s, (pos, n) in enumerate(SLOT):
            xs = xn[:, s % 3, :]
            a = V.ts(xs, h[:, s, :], rstd[:, s:s + 1], None, ALU.mult, None, m_r, xn_free[s % 3])
            for half in range(2):
                bk = psum_ring.take()
                pv = bk.ap.rearrange("p (a b) -> p a b", a=4)
                mt = PE.mms([(pv[:, k, 0:n], xs[0:n, P * (4 * half + k):P * (4 * half + k + 1)], ident[0:n, 0:n], None, None)
                             for k in range(4)], a, bk.free)
                for k in range(4):
                    kk_ = 4 * half + k
                    bk.free = [S.copy(hn[:, kk_, PADW + pos:PADW + pos + n], pv[:, k, 0:n], mt, m_chan,
                                      scale=col("a_norm", kk_))]
            xn_free[s % 3] = [mt]
        m_hn = S.last()
        for k in range(KD):
            g = k // 2
            w = WINDOWS[g]
            src, a, sh = hn[:, k, :], [m_hn, m_z, V.last()], 1
            bufs2 = [sa, sb_]
            while sh < w:
                dst = bufs2[0]
                a = V.tt(dst[:, PADW:], src[:, PADW:], src[:, PADW - sh:PADW + L - sh], ALU.add, a)
                src, sh = dst, 2 * sh
                bufs2.reverse()
            b = V.tt(edge, src[:, PADW:2 * PADW], inv[:, g, :], ALU.mult, a, m_inv)
            V.stt(pooled[:, k, PADW:], src[:, 2 * PADW:], 1.0 / w, hn[:, k, 2 * PADW:], ALU.mult, ALU.subtract)
            V.tt(pooled[:, k, 0:PADW], edge, hn[:, k, PADW:2 * PADW], ALU.subtract, b)
        m_p = V.last()
        for s, (pos, n) in enumerate(SLOT):
            for half in range(2):
                bk = psum_ring.take()
                mt = PE.mms([(bk.ap[0:n, 256 * g:256 * g + 256], pooled[:, 4 * half + 2 * g + u, pos:pos + n],
                              a_w[:, 4 * half + 2 * g + u, :], u == 0, u == 1) for g in range(2) for u in range(2)],
                            m_p, m_aw, bk.free)
                hc = half_cols(half)
                a = V.tt(junk[0:n, hc], bk.ap[0:n, :], arow[0:n, hc], ALU.mult, mt, m_aw, V.last())
                bk.free = [a]
                V.tt(h[0:n, s, hc], h[0:n, s, hc], junk[0:n, hc], ALU.add, a)
        dump("h2", h)

        def moe(layer):
            barrier()
            stage(f"route{layer}")
            top[0] = base_b2
            WF = KD * 2 * DE + 2 * D
            w_ring = Ring([Buf(take(WF), dma_sem(f"we{i}")) for i in range(3)])

            def load_expert(e):
                b = w_ring.take()
                mk = SP.dma(b.sem, b.ap, io["w_exp"][layer * NE + e], b.free)
                return b, mk
            loaded = [load_expert(e) for e in range(3)]
            idx = take(NBLK)
            dest = take(NS, 2)
            gates = take(NS, 2)
            counts = take(32)
            base_route = top[0]
            xg = take(NS, D)
            xgT = take(KD, NS * P)
            rstd, junk = take(NS), xgT.rearrange("p a b -> p (a b)")[:, 0:D]
            grow = take(D)
            wr, br = take(KD, NG + NE), take(NG + NE)
            d_r = dma_sem("router")
            SP.dma(d_r, grow, io["rows"][3 + layer:4 + layer, :].to_broadcast([P, D]))
            SP.dma(d_r, wr, io["w_router"][layer])
            m_rw = SP.dma(d_r, br, io["b_router"][layer:layer + 1, :].to_broadcast([P, NG + NE]))
            io4, io32, io48, tokid = take(NG), take(NE), take(NBLK), take(NS)
            base_e, valid, upper = take(NE), take(NS), take(P)
            io128, tokf = take(P), take(NS)
            ci = take(P)
            a1 = G.do(lambda: G.e.iota(ci.bitcast(I32), [[1, P]], base=0, channel_multiplier=0))
            a2 = G.do(lambda: G.e.iota(tokid.bitcast(I32), [[P, NS]], base=0, channel_multiplier=1))
            G.set(valid, 1.0)
            a3 = G.set(valid[:, NT:NS], 0.0, G.last())
            G.set(valid[0:N_META, NT:NS], 1.0, a3)
            a3 = G.set(upper, 1.0)
            m_up = keep(upper, upper, [[1, P]], 0, -1, ALU.is_gt, 0.0, a3)
            V.copy(io32, ci.bitcast(I32)[:, 0:NE], a1)
            V.copy(io4, ci.bitcast(I32)[:, 0:NG])
            V.copy(io128, ci.bitcast(I32))
            V.copy(io48, ci.bitcast(I32)[:, 0:NBLK])
            c = V.copy(tokf, tokid.bitcast(I32), a2)
            m_tokf = V.tt(tokf, tokf, valid, ALU.mult, c, G.last())
            m_io = V.ts(base_e, io32, float(P), None, ALU.mult, None, V.last())
            m_r = rms(rstd, junk)
            d_x = dma_sem("xn")
            for s, (pos, n) in enumerate(SLOT):
                a = V.stt(xg[:, s, :], h[:, s, :], rstd[:, s:s + 1], grow, ALU.mult, ALU.mult, m_r, m_rw)
                m_xn = SP.dma(d_x, xn_dram[P * s:P * s + n, :], xg[0:n, s, :], a)
                for half in range(2):
                    bk = psum_ring.take()
                    pv = four(bk.ap)
                    mt = PE.mms([(pv[:, k, :], xg[:, s, P * (4 * half + k):P * (4 * half + k + 1)], ident, None, None)
                                 for k in range(4)], a, bk.free)
                    bk.free = [(S if half else V).copy(xgT[:, 4 * half:4 * half + 4, P * s:P * (s + 1)], pv, mt, m_r)]
            m_t = [V.last(), S.last()]
            marks_out.append(m_xn)
            bk = psum_ring.take()
            NR = NG + NE
            pv = bk.ap[:, 0:NS * NR].rearrange("p (a b) -> p a b", a=NS)
            mt = PE.mms([(pv[:, s, :], xgT[:, k, P * s:P * (s + 1)], wr[:, k, :], k == 0, k == KD - 1)
                         for s in range(NS) for k in range(KD)], m_t, m_rw, bk.free)
            lg = take(NS, NR)
            a = V.tt(lg, pv, bc_mid(br, NS), ALU.add, mt, m_rw)
            bk.free = [a]
            gp, m8, i8 = take(NS, 8), take(NS, 8), take(NS, 8)
            b = V.set(gp, NEG)
            b = V.copy(gp[:, :, 0:NG], lg[:, :, 0:NG], a, b)
            for s in range(NS):
                c = V.do(lambda s=s: nc.vector.max(m8[:, s, :], gp[:, s, :]), b)
                V.do(lambda s=s: nc.vector.max_index(i8[:, s, :].bitcast(U32), m8[:, s, :], gp[:, s, :]), c)
            a = V.last()
            eg, wg, gi = take(NS, NG), take(NS), take(NS)
            c = V.tt(eg, lg[:, :, 0:NG], m8[:, :, 0:1].to_broadcast([P, NS, NG]), ALU.subtract, a)
            c = S.act(eg, eg, ACT.Exp, c)
            c = V.red(wg, eg, ALU.add, c)
            c = V.recip(wg, wg, c)
            c = V.copy(gi, i8[:, :, 0:1].rearrange("p a b -> p (a b)").bitcast(U32), c)
            pen = take(NS, NG)
            c = V.tt(pen, bc_mid(io4, NS), bc_last(gi, NG), ALU.is_equal, c, m_io)
            c = V.ts(pen, pen, -NEG, NEG, ALU.mult, ALU.add, c)
            me = take(NS, NE)
            c = V.tt(me.rearrange("p s (g e) -> p s g e", g=NG), lg[:, :, NG:].rearrange("p s (g e) -> p s g e", g=NG),
                     pen.unsqueeze(3).to_broadcast([P, NS, NG, EPG]), ALU.add, c)
            for s in range(NS):
                b = V.do(lambda s=s: nc.vector.max(m8[:, s, :], me[:, s, :]), c)
                V.do(lambda s=s: nc.vector.max_index(i8[:, s, :].bitcast(U32), m8[:, s, :], me[:, s, :]), b)
            a = V.last()
            e1, rr, ei = take(NS), take(NS), take(NS, 2)
            v0, v1 = (m8[:, :, j:j + 1].rearrange("p a b -> p (a b)") for j in range(2))
            c = V.tt(e1, v1, v0, ALU.subtract, a)
            c = S.act(e1, e1, ACT.Exp, c)
            c = V.ts(rr, e1, 1.0, None, ALU.add, None, c)
            c = V.recip(rr, rr, c)
            c = V.tt(rr, rr, wg, ALU.mult, c)
            V.copy(gates[:, :, 0:1], rr.unsqueeze(2), c)
            V.tt(gates[:, :, 1:2], rr.unsqueeze(2), e1.unsqueeze(2), ALU.mult)
            c = V.copy(ei, i8[:, :, 0:2].bitcast(U32))
            oh, both = [take(NS, NE) for _ in range(2)], take(NS, NE)
            for j in range(2):
                b = V.tt(oh[j], bc_mid(io32, NS), ei[:, :, j:j + 1].to_broadcast([P, NS, NE]), ALU.is_equal, c)
                b = V.tt(oh[j], oh[j], bc_last(valid, NE), ALU.mult, b, G.last())
            m_oh = V.tt(both, oh[0], oh[1], ALU.add, b)
            bk = psum_ring.take()
            pv = bk.ap[:, 0:NS * NE].rearrange("p (a b) -> p a b", a=NS)
            prods = []
            for s in range(NS):
                prods += [(pv[:, s, :], ones, both[:, j, :], j == 0, False) for j in range(s)]
                prods.append((pv[:, s, :], upper, both[:, s, :], s == 0, True))
            mt = PE.mms(prods, m_oh, m_up, bk.free)
            rank = take(NS, NE)
            bk.free = [V.copy(rank, pv, mt)]
            bk = psum_ring.take()
            mt = PE.mms([(bk.ap[:, 0:NE], ones, both[:, j, :], j == 0, j == NS - 1) for j in range(NS)], bk.free)
            cnt, nb, cum, dif = (take(NE) for _ in range(4))
            a = V.copy(cnt, bk.ap[:, 0:NE], mt)
            bk.free = [a]
            a = V.ts(nb, cnt, float(P), None, ALU.is_gt, None, a)
            for j in range(2, (L - 1) // P + 1):
                a = V.stt(nb, cnt, float(P * j), nb, ALU.is_gt, ALU.add, a)
            a = V.do(lambda: nc.vector.tensor_tensor_scan(cum, ones[:, 0:NE], nb, 0.0, ALU.mult, ALU.add), a)
            m_cum = a
            a = V.tt(dif, cum, nb, ALU.subtract, a)
            a = V.ts(dif, dif, float(P), float((NE - 1) * P), ALU.mult, ALU.add, a)
            a = V.tt(dif, dif, base_e, ALU.subtract, a)
            over, slot = take(NS, NE), take(NS, NE)
            b = V.ts(over, rank, float(P), None, ALU.is_ge, None, a)
            b = V.tt(over, over, bc_mid(dif, NS), ALU.mult, b)
            c = V.tt(slot, rank, bc_mid(base_e, NS), ALU.add, b)
            c = V.tt(slot, slot, over, ALU.add, c)
            df = take(NS, 2)
            for j in range(2):
                b = V.tt(oh[j], oh[j], slot, ALU.mult, c)
                V.red(df[:, :, j:j + 1], oh[j], ALU.add, b)
            m_dest = V.copy(dest.bitcast(I32), df, V.last())
            ovx, ovs = take(NOV, NE), take(NOV)
            a = V.tt(ovx[0:1], bc_last(io48[0:1, 0:NOV], NE), bc_mid(cum[0:1], NOV), ALU.is_ge, m_cum)
            a = V.red(ovs[0:1], ovx[0:1], ALU.add, a)
            a = V.ts(ovs[0:1], ovs[0:1], float(NE - 1), None, ALU.min, None, a)
            V.copy(counts.bitcast(I32)[0:1, 1:1 + NOV], ovs[0:1], a)
            m_cnt = V.copy(counts.bitcast(I32)[0:1, 0:1], cum[0:1, NE - 1:NE])
            rowi, blki, rowf, blkf = (take(NS, 2) for _ in range(4))
            destf = dest.rearrange("p a b -> p (a b)").bitcast(I32)
            V.ts(rowi.rearrange("p a b -> p (a b)").bitcast(I32), destf, P - 1, None, ALU.bitwise_and, None, m_dest)
            b = V.ts(blki.rearrange("p a b -> p (a b)").bitcast(I32), destf, 7, None, ALU.logical_shift_right, None)
            V.copy(rowf, rowi.bitcast(I32), b)
            b = V.copy(blkf, blki.bitcast(I32))
            dead = xgT.rearrange("p a b -> p (a b)")
            blk1 = [dead[:, NS * NBLK * j:NS * NBLK * (j + 1)].rearrange("p (a b) -> p a b", a=NS) for j in range(2)]
            for j in range(2):
                c = V.tt(blk1[j], bc_mid(io48, NS), blkf[:, :, j:j + 1].to_broadcast([P, NS, NBLK]), ALU.is_equal, b)
                V.tt(blk1[j], blk1[j], bc_last(tokf, NBLK), ALU.mult, c, m_tokf)
            m_blk = V.last()
            bk = psum_ring.take()
            row1 = Ring([Buf(dead[:, 2048 + P * i:2048 + P * (i + 1)]) for i in range(4)])
            for s in range(NS):
                for j in range(2):
                    r1 = row1.take()
                    c = V.ts(r1.ap, io128, rowf[:, s, j:j + 1], None, ALU.is_equal, None, b, r1.free)
                    mt = PE.mms([(bk.ap[:, 0:NBLK], r1.ap, blk1[j][:, s, :], s + j == 0, (s, j) == (NS - 1, 1))],
                                c, m_blk, bk.free)
                    r1.free = [mt]
            bk.free = [V.copy(idx.bitcast(I32), bk.ap[:, 0:NBLK], mt)]
            m_idx = V.last()
            if layer == 0:
                dump("lg", lg)
                dump("slot", slot)
                dump("gates", gates)

            barrier()
            stage(f"experts{layer}")
            top[0] = base_route
            w_ring.bufs.append(Buf(take(WF), dma_sem("we3")))
            loaded.append(load_expert(3))
            xe_ring = Ring([Buf(take(D), dma_sem(f"xe{i}")) for i in range(3)])
            xt_ring = Ring([Buf(take(KD, P)) for _ in range(2)])
            g_ring = Ring([Buf(take(DE)) for _ in range(2)])
            h_ring = Ring([Buf(take(DE)) for _ in range(2)])
            ht_ring = Ring([Buf(take(2, P)) for _ in range(2)])
            y_ring = Ring([Buf(take(D), dma_sem(f"y{i}")) for i in range(3)])

            def gather(block):
                xe = xe_ring.take()
                G.wait([m_idx, m_xn, xe.free])
                sem, ap = xe.sem, xe.ap
                G.queue.append(lambda: G.e.indirect_dma_start(
                    out=ap, out_offset=None, in_=xn_dram[:, :],
                    in_offset=bass.IndirectOffsetOnAxis(idx.bitcast(I32)[:, block:block + 1], 0)).then_inc(sem.sem, 16))
                return xe, sem.next()

            def gate_up(xe, m_xe, w, m_w):
                xt = xt_ring.take()
                cp = []
                for half in range(2):
                    bk = psum_ring.take()
                    mt = PE.mms([(four(bk.ap)[:, k, :], xe.ap[:, P * (4 * half + k):P * (4 * half + k + 1)], ident, None, None)
                                 for k in range(4)], m_xe, bk.free)
                    bk.free = [(S if half else V).copy(xt.ap[:, 4 * half:4 * half + 4, :], four(bk.ap), mt, xt.free)]
                    cp.append(bk.free[0])
                xe.free = [mt]
                wv = w.ap[:, 0:KD * 2 * DE].rearrange("p (a b) -> p a b", a=KD)
                bk = psum_ring.take()
                mt = PE.mms([(bk.ap, xt.ap[:, k, :], wv[:, k, :], k == 0, k == KD - 1) for k in range(KD)], cp, m_w, bk.free)
                xt.free = [mt]
                g, hb = g_ring.take(), h_ring.take()
                a = S.act(g.ap, bk.ap[:, 0:DE], ACT.Sigmoid, mt, g.free)
                a = V.tt(g.ap, bk.ap[:, 0:DE], g.ap, ALU.mult, a)
                a = V.tt(hb.ap, bk.ap[:, DE:2 * DE], g.ap, ALU.mult, a, hb.free)
                bk.free, g.free = [a], [a]
                return hb, a

            def down(hb, m_h, w, block):
                bk = psum_ring.take()
                mt = PE.mms([(four(bk.ap)[:, k, :], hb.ap[:, P * k:P * (k + 1)], ident, None, None) for k in range(2)],
                            m_h, bk.free)
                hb.free = [mt]
                ht = ht_ring.take()
                a = S.copy(ht.ap, four(bk.ap)[:, 0:2, :], mt, ht.free)
                bk.free = [a]
                wv = w.ap[:, KD * 2 * DE:].rearrange("p (a b) -> p a b", a=2)
                y = y_ring.take()
                cp = []
                for half in range(2):
                    bk = psum_ring.take()
                    mt = PE.mms([(bk.ap, ht.ap[:, k, :], wv[:, k, half_cols(half)], k == 0, k == 1) for k in range(2)], a, bk.free)
                    bk.free = [(S if half else V).copy(y.ap[:, half_cols(half)], bk.ap, mt, y.free)]
                    cp.append(bk.free[0])
                ht.free = [mt]
                w.free = [mt]
                y.free = [SP.dma(y.sem, y_dram[P * block:P * (block + 1), :], y.ap, cp)]
                return y.free[0]

            gathered = [gather(0), gather(1)]
            pending = None
            for e in range(NE):
                w, m_w = loaded[e]
                xe, m_xe = gathered[e]
                hb, m_h = gate_up(xe, m_xe, w, m_w)
                if e + 2 < NE:
                    gathered.append(gather(e + 2))
                if pending:
                    down(*pending)
                    if e + 3 < NE:
                        loaded.append(load_expert(e + 3))
                pending = (hb, m_h, w, e)
            down(*pending)
            m_y = [b.free for b in y_ring.bufs]

            barrier()
            loads = {}

            def enter(lane):
                lane.queue.append(lambda: loads.__setitem__(lane, lane.e.value_load(counts.bitcast(I32)[0:1, 0:1],
                                                                                   min_val=0, max_val=NOV)))
            for lane in lanes:
                lane.wait([m_cnt])
                enter(lane)
            stage(f"over{layer}")
            for kind, r in (("rows", xe_ring), ("y", y_ring), ("w", w_ring)):
                del r.bufs[1:]
                r.bufs[0].sem, r.bufs[0].free = dsem(f"over{layer}_{kind}"), []
            for r in (xt_ring, g_ring, h_ring, ht_ring):
                for b in r.bufs:
                    b.free = []
            outer = {lane: (lane.queue, dict(lane.waited)) for lane in lanes}
            for blk in range(NOV):
                for lane in lanes:
                    lane.queue = []
                wb_ = w_ring.take()
                SP.wait(wb_.free)
                sem = wb_.sem

                def load_w(blk=blk, wb_=wb_, sem=sem):
                    ex = SP.e.value_load(counts.bitcast(I32)[0:1, 1 + blk:2 + blk], min_val=0, max_val=NE - 1)
                    SP.e.dma_start(wb_.ap, io["w_exp"][bass.ds(ex + layer * NE, 1)].rearrange("a p n -> (a p) n")).then_inc(sem.sem, 16)
                SP.queue.append(load_w)
                m_w = sem.next()
                xe, m_xe = gather(NE + blk)
                hb, m_h = gate_up(xe, m_xe, wb_, m_w)
                m_yo = down(hb, m_h, wb_, NE + blk)
                S.wait([m_yo])
                for lane in lanes:
                    sub = lane.queue
                    lane.queue = outer[lane][0]

                    def branch(lane=lane, sub=sub, blk=blk):
                        with lane.e.If(loads[lane] > blk):
                            lane.play(sub)
                    lane.queue.append(branch)
            for lane in lanes:
                lane.waited = outer[lane][1]
            stage(f"joined{layer}")
            scr = take(16)
            joined = [V.set(scr[:, 0:2], 0.0), G.set(scr[:, 2:4], 0.0), S.copy(scr[:, 4:6], ident[:, 0:2])]
            joined.append(PE.mms([(banks[0][:, 0:2], ident, ident[:, 0:2], True, True)], joined))
            for lane in lanes:
                lane.wait(joined)
            for b in psum_ring.bufs:
                b.free = []

            c_ring = Ring([Buf(take(D), dma_sem(f"c{i}")) for i in range(4)])
            for s, (pos, n) in enumerate(SLOT):
                for j in range(2):
                    cb = c_ring.take()
                    G.wait([m_y, cb.free])
                    G.queue.append(lambda s=s, j=j, n=n, cb=cb: G.e.indirect_dma_start(
                        out=cb.ap[0:n, :], out_offset=None, in_=y_dram[:, :],
                        in_offset=bass.IndirectOffsetOnAxis(dest.bitcast(I32)[0:n, s, j:j + 1], 0)).then_inc(cb.sem.sem, 16))
                    mk = cb.sem.next()
                    cb.free = [V.stt(h[0:n, s, :], cb.ap[0:n, :], gates[0:n, s, j:j + 1], h[0:n, s, :], ALU.mult, ALU.add,
                                     mk, V.last())]
            dump(f"h{3 + 2 * layer}", h)

        moe(0)

        barrier()
        stage("latent")
        top[0] = base_b2
        NC = KVL + ROPE + QL
        ckvT, krT, qrT = take(2, L), take(L), take(4, L)
        w_uv = take(2, MH * VH)
        base_wo = top[0]
        cqT = take(3, L)
        w_uq, w_uk = take(3, MH * (NOPE + ROPE)), take(2, MH * NOPE)
        w_o = arena[:, base_wo:base_wo + MH * D].rearrange("p (a b) -> p a b", a=MH)
        base_mla = top[0]
        wc = take(KD, NC)
        rope_cs = take(NS, ROPE)
        xn = take(2, D)
        xt = take(2, KD * P)
        rstd, junk = take(NS), take(D)
        ct = [take(NC) for _ in range(2)]
        rs2 = [take(2) for _ in range(2)]
        kr = [take(P) for _ in range(2)]
        rt = [take(ROPE // 2) for _ in range(4)]
        d_lw = dma_sem("latent_w")
        SP.dma(d_lw, wc, io["w_c"])
        SP.dma(d_lw, rope_cs, io["rope"])
        SP.dma(d_lw, w_uq, io["w_uq"])
        SP.dma(d_lw, w_uk, io["w_uk"])
        m_lw = SP.dma(d_lw, w_uv, io["w_uv"])
        for k in range(KD):
            V.ts(wc[:, k, 0:KVL + ROPE], wc[:, k, 0:KVL + ROPE], col("kv_norm", k), None, ALU.mult, None, m_lw)
            V.ts(wc[:, k, KVL + ROPE:], wc[:, k, KVL + ROPE:], col("b_norm", k), None, ALU.mult, None)
        m_wc = V.last()
        for k in range(3):
            G.ts(w_uq[:, k, :], w_uq[:, k, :], col("q_norm", k), None, ALU.mult, None, m_lw)
        for k in range(2):
            G.ts(w_uk[:, k, :], w_uk[:, k, :], col("kv_lat", k), None, ALU.mult, None)
            G.ts(w_uv[:, k, :], w_uv[:, k, :], col("kv_lat", k), None, ALU.mult, None)
        m_wu = G.last()
        m_r = rms(rstd, junk)
        xn_free, xt_free, ct_free = [[], []], [[], []], [[], []]

        def rotate(dst, x, cs, n, tm, rows, *after):
            x1, x2, o1, o2 = x[0], x[1], dst[0], dst[1]
            b = [V.tt(tm[0], x1, cs[0], ALU.mult, after), V.tt(tm[1], x2, cs[1], ALU.mult),
                 V.tt(tm[2], x1, cs[1], ALU.mult), V.tt(tm[3], x2, cs[0], ALU.mult)]
            V.tt(o1, tm[0], tm[1], ALU.subtract, b)
            return V.tt(o2, tm[2], tm[3], ALU.add)

        H2 = ROPE // 2
        for s, (pos, n) in enumerate(SLOT):
            p_ = s % 2
            a = V.ts(xn[:, p_, :], h[:, s, :], rstd[:, s:s + 1], None, ALU.mult, None, m_r, xn_free[p_])
            xtv = xt[:, p_, :].rearrange("p (a b) -> p a b", a=KD)
            cp = []
            for half in range(2):
                bk = psum_ring.take()
                mt = PE.mms([(four(bk.ap)[:, k, 0:n], xn[0:n, p_, P * (4 * half + k):P * (4 * half + k + 1)],
                              ident[0:n, 0:n], None, None) for k in range(4)], a, bk.free)
                bk.free = [(S if half else V).copy(xtv[:, 4 * half:4 * half + 4, 0:n], four(bk.ap)[:, :, 0:n], mt, xt_free[p_])]
                cp.append(bk.free[0])
            xn_free[p_] = [mt]
            c_ = ct[p_]
            for c0, c1 in ((0, KVL + ROPE), (KVL + ROPE, NC)):
                bk = psum_ring.take()
                mt = PE.mms([(bk.ap[0:n, 0:c1 - c0], xtv[:, k, 0:n], wc[:, k, c0:c1], k == 0, k == KD - 1)
                             for k in range(KD)], cp, m_wc, bk.free)
                bk.free = [S.copy(c_[0:n, c0:c1], bk.ap[0:n, 0:c1 - c0], mt, ct_free[p_])]
            xt_free[p_] = [mt]
            a = S.last()
            r2 = rs2[p_]
            b = S.act(junk[0:n, 0:KVL], c_[0:n, 0:KVL], ACT.Square, a, accum=r2[0:n, 0:1])
            b = S.act(junk[0:n, 0:QL], c_[0:n, KVL + ROPE:], ACT.Square, b, accum=r2[0:n, 1:2])
            S.act(r2[0:n, 0:1], r2[0:n, 0:1], ACT.Sqrt, b, bias=eps_rms[0:n, :], scale=1.0 / KVL)
            b = S.act(r2[0:n, 1:2], r2[0:n, 1:2], ACT.Sqrt, bias=eps_rms[0:n, :], scale=1.0 / QL)
            b = V.recip(r2[0:n, :], r2[0:n, :], b)
            V.ts(c_[0:n, 0:KVL], c_[0:n, 0:KVL], r2[0:n, 0:1], None, ALU.mult, None, b)
            m_c = V.ts(c_[0:n, KVL + ROPE:], c_[0:n, KVL + ROPE:], r2[0:n, 1:2], None, ALU.mult, None)
            k_ = kr[p_]
            cs = (rope_cs[0:n, s, 0:H2], rope_cs[0:n, s, H2:])
            a = rotate((k_[0:n, 0:H2], k_[0:n, H2:ROPE]), (c_[0:n, KVL:KVL + H2], c_[0:n, KVL + H2:KVL + ROPE]), cs, n,
                       [r[0:n, :] for r in rt], n, m_c, ct_free[p_])
            a = V.copy(k_[0:n, ROPE:2 * ROPE], k_[0:n, 0:ROPE], a)
            bk = psum_ring.take()
            pv = four(bk.ap)
            srcs = [c_[0:n, 0:P], c_[0:n, P:2 * P], k_[0:n, :]]
            mt = PE.mms([(pv[:, j, 0:n], x_, ident[0:n, 0:n], None, None) for j, x_ in enumerate(srcs)], a, m_c, bk.free)
            S.copy(ckvT[:, :, pos:pos + n], pv[:, 0:2, 0:n], mt)
            bk.free = [S.copy(krT[:, pos:pos + n], pv[:, 2, 0:n])]
            bk = psum_ring.take()
            pv = four(bk.ap)
            mt = PE.mms([(pv[:, j, 0:n], c_[0:n, KVL + ROPE + P * j:KVL + ROPE + P * (j + 1)], ident[0:n, 0:n], None, None)
                         for j in range(3)], bk.free)
            bk.free = [V.copy(cqT[:, :, pos:pos + n], pv[:, 0:3, 0:n], mt)]
            ct_free[p_] = [mt]
        m_lat = [V.last(), S.last()]
        barrier()
        stage("qrope")
        top[0] = base_mla + KD * NC + NS * ROPE
        qt = [take(MH * ROPE) for _ in range(2)]
        qr = [take(MH * ROPE) for _ in range(2)]
        tm = [take(MH * H2) for _ in range(4)]
        qr_free = [[], []]
        for s, (pos, n) in enumerate(SLOT):
            p_ = s % 2
            bk = psum_ring.take()
            mt = PE.mms([(bk.ap[0:n, :], cqT[:, k, pos:pos + n], w_uq[:, k, MH * NOPE:], k == 0, k == 2) for k in range(3)],
                        m_wu, bk.free)
            bk.free = [S.copy(qt[p_][0:n, :], bk.ap[0:n, :], mt, V.last())]

            def halves(t):
                v = t[0:n, :].rearrange("p (h u c) -> p u h c", u=2, c=H2)
                return v[:, 0], v[:, 1]
            cs = (bc_mid(rope_cs[0:n, s, 0:H2], MH), bc_mid(rope_cs[0:n, s, H2:], MH))
            a = rotate(halves(qr[p_]), halves(qt[p_]), cs, n,
                       [t_[0:n, :].rearrange("p (h c) -> p h c", h=MH) for t_ in tm], n, S.last(), qr_free[p_])
            bk = psum_ring.take()
            pv = four(bk.ap)
            mt = PE.mms([(pv[:, j, 0:n], qr[p_][0:n, P * j:P * (j + 1)], ident[0:n, 0:n], None, None) for j in range(4)],
                        a, bk.free)
            qr_free[p_] = [mt]
            bk.free = [S.copy(qrT[:, :, pos:pos + n], pv[:, :, 0:n], mt)]

        barrier()
        stage("mla")
        top[0] = base_mla
        oT = take(MH, L)
        vv = [take(NS, 2 * VH) for _ in range(2)]
        qn, kn = [take(L) for _ in range(2)], [take(L) for _ in range(2)]
        Pb = [take(L) for _ in range(3)]
        PTb = [take(NS, P) for _ in range(2)]
        causal = take(P)
        a = G.set(causal, 0.0)
        m_cau = keep(causal, causal, [[-1, P]], 0, 1, ALU.is_ge, NEG, a)
        sm = [[take(2), take(2), take(1)] for _ in range(4)]
        score_ring = Ring([Buf(psum[:, 1024 * i:1024 * (i + 1)]) for i in range(2)])
        side_ring = Ring([Buf(banks[4 + i]) for i in range(4)])
        qk_free, vv_free = [[], []], [[], []]
        p_free, pt_free = [[], [], []], [[], []]
        m_qk, m_vv = [None] * MH, [None] * (MH // 2)
        order = [NT] + list(range(NT))

        def value_steps(pair):
            def step(s, pos, n):
                bk = side_ring.take()
                mt = PE.mms([(bk.ap[0:n, 0:2 * VH], ckvT[:, k, pos:pos + n], w_uv[:, k, 2 * VH * pair:2 * VH * (pair + 1)],
                              k == 0, k == 1) for k in range(2)], bk.free)
                bk.free = [S.copy(vv[pair % 2][0:n, s, :], bk.ap[0:n, 0:2 * VH], mt, vv_free[pair % 2])]
                m_vv[pair] = S.last()
            return [lambda s=s, pos=pos, n=n: step(s, pos, n) for s, (pos, n) in enumerate(SLOT)]

        def qk_steps(hh):
            def step(dst, w_, src, nk, c0, c1):
                bk = side_ring.take()
                mt = PE.mms([(bk.ap[:, 0:c1 - c0], w_[:, k, P * hh:P * (hh + 1)], src[:, k, c0:c1], k == 0, k == nk - 1)
                             for k in range(nk)], bk.free)
                bk.free = [S.copy(dst[hh % 2][:, c0:c1], bk.ap[:, 0:c1 - c0], mt, qk_free[hh % 2])]
                m_qk[hh] = S.last()
            return [lambda dst=dst, w_=w_, src=src, nk=nk, c0=c0: step(dst, w_, src, nk, c0, min(L, c0 + 512))
                    for dst, w_, src, nk in ((qn, w_uq, cqT, 3), (kn, w_uk, ckvT, 2)) for c0 in range(0, L, 512)]

        def attend(hh, qi, it):
            s = order[qi]
            pos, n = SLOT[s]
            pr = slice(64 * (hh % 2), 64 * (hh % 2) + 64)
            kc = pos + n
            pb, ptb, (mx, rsu, rdn) = Pb[it % 3], PTb[it % 2], sm[it % 4]
            sc = score_ring.take()
            parts = [(sc, 0, min(kc, 1024))]
            if kc > 1024:
                parts.append((side_ring.take(), 1024, kc))
            prods = []
            for buf, p0, p1 in parts:
                for c0 in range(p0, p1, 512):
                    c1 = min(p1, c0 + 512)
                    o = buf.ap[0:n, c0 - p0:c1 - p0]
                    prods += [(o, qn[hh % 2][:, pos:pos + n], kn[hh % 2][:, c0:c1], True, False),
                              (o, qrT[pr, hh // 2, pos:pos + n], krT[pr, c0:c1], False, True)]
            mt = PE.mms(prods, m_qk[hh], [buf.free for buf, _, _ in parts])
            qk_free[hh % 2] = [mt]
            rd = []
            for u, (buf, p0, p1) in enumerate(parts):
                c0 = max(pos, p0)
                o = buf.ap[0:n, c0 - p0:p1 - p0]
                a = V.tt(o, o, causal[0:n, c0 - pos:p1 - pos], ALU.add, mt, m_cau)
                rd.append(V.red(mx[0:n, u:u + 1], buf.ap[0:n, 0:p1 - p0], ALU.max, a))
            a = rd
            if len(parts) > 1:
                a = V.tt(mx[0:n, 0:1], mx[0:n, 0:1], mx[0:n, 1:2], ALU.max, a)
            a = V.ts(mx[0:n, 0:1], mx[0:n, 0:1], -SCALE, None, ALU.mult, None, a)
            for u, (buf, p0, p1) in enumerate(parts):
                e = S.act(pb[0:n, p0:p1], buf.ap[0:n, 0:p1 - p0], ACT.Exp, a, p_free[it % 3], bias=mx[0:n, 0:1], scale=SCALE,
                          accum=rsu[0:n, u:u + 1])
                buf.free = [e]
            yield
            if len(parts) > 1:
                e = V.tt(rsu[0:n, 0:1], rsu[0:n, 0:1], rsu[0:n, 1:2], ALU.add, e)
            a = V.recip(rdn[0:n, :], rsu[0:n, 0:1], e)
            a = V.ts(pb[0:n, 0:kc], pb[0:n, 0:kc], rdn[0:n, :], None, ALU.mult, None, a)
            yield
            keys = order[:qi + 1]
            cp = []
            for j0 in range(0, len(keys), 4):
                ks_ = keys[j0:j0 + 4]
                bk = side_ring.take()
                pv = four(bk.ap)
                prods = []
                for j, ks in enumerate(ks_):
                    kp, kn_ = SLOT[ks]
                    prods.append((pv[0:kn_, j, 0:n], pb[0:n, kp:kp + kn_], ident[0:n, 0:n], None, None))
                mt = PE.mms(prods, a, bk.free)
                if j0 == 0:
                    S.copy(ptb[0:N_META, 0, 0:n], pv[0:N_META, 0, 0:n], mt, pt_free[it % 2])
                    if len(ks_) > 1:
                        S.copy(ptb[:, 1:len(ks_), 0:n], pv[:, 1:len(ks_), 0:n], mt)
                    bk.free = [S.last()]
                else:
                    bk.free = [V.copy(ptb[:, j0:j0 + len(ks_), 0:n], pv[:, 0:len(ks_), 0:n], mt, pt_free[it % 2])]
                cp.append(bk.free[0])
            p_free[it % 3] = [mt]
            yield
            bk = side_ring.take()
            vh = VH * (hh % 2)
            mt = PE.mms([(bk.ap[:, 0:n], vv[hh // 2 % 2][0:SLOT[ks][1], ks, vh:vh + VH], ptb[0:SLOT[ks][1], j, 0:n],
                          j == 0, j == len(keys) - 1) for j, ks in enumerate(keys)], cp, m_vv[hh // 2], bk.free)
            pt_free[it % 2] = [mt]
            vv_free[hh // 2 % 2] = [mt]
            bk.free = [S.copy(oT[:, hh, pos:pos + n], bk.ap[:, 0:n], mt)]

        TURNS = [NS - 1 - i // 2 if i % 2 == 0 else i // 2 for i in range(NS)]

        def heads_in_turn():
            for make in value_steps(0) + qk_steps(0):
                make()
            for hh in range(MH):
                pair = hh // 2
                if hh % 2 == 0 and pair + 1 < MH // 2:
                    values = value_steps(pair + 1)
                nexts = qk_steps(hh + 1) if hh + 1 < MH else []
                for turn, qi in enumerate(TURNS):
                    if nexts:
                        nexts.pop(0)()
                    if values and (hh % 2 or turn >= 4):
                        values.pop(0)()
                    yield attend(hh, qi, NS * hh + turn)
                if hh + 2 == MH:
                    heads_done.append(SP.dma(dma_sem("w_o"), w_o, io["w_o"], PE.last()))
        heads_done = []
        pipelined(heads_in_turn())
        dump("oT", oT)
        barrier()
        stage("out2")
        m_wo = heads_done
        for s, (pos, n) in enumerate(SLOT):
            for half in range(2):
                bk = psum_ring.take()
                mt = PE.mms([(bk.ap[0:n, :], oT[:, k, pos:pos + n], w_o[:, k, half_cols(half)], k == 0, k == MH - 1)
                             for k in range(MH)], m_wo, bk.free)
                bk.free = [V.tt(h[0:n, s, half_cols(half)], h[0:n, s, half_cols(half)], bk.ap[0:n, :], ALU.add, mt)]
        dump("h4", h)

        moe(1)

        barrier()
        stage("final")
        top[0] = base_b2
        rstd, junk, grow = take(NS), take(D), take(D)
        o_ring = Ring([Buf(take(D), dma_sem(f"out{i}")) for i in range(3)])
        m_g = SP.dma(dma_sem("final_row"), grow, io["rows"][5:6, :].to_broadcast([P, D]))
        m_r = rms(rstd, junk)
        for s in range(NT):
            ob = o_ring.take()
            a = V.stt(ob.ap, h[:, s, :], rstd[:, s:s + 1], grow, ALU.mult, ALU.mult, m_r, m_g, ob.free)
            ob.free = [SP.dma(ob.sem, io["out"][P * s:P * (s + 1), :], ob.ap, a)]
            marks_out.append(ob.free[0])
        SP.wait(marks_out)

        block = ctx.enter_context(nc.Block())

        @block.tensor
        def _(e):
            PE.play()

        @block.vector
        def _(e):
            V.play()

        @block.scalar
        def _(e):
            S.play()

        @block.gpsimd
        def _(e):
            G.play()

        @block.sync
        def _(e):
            SP.play()


def kernel(**inputs):
    import numpy as _np
    import concourse.bacc as _bacc
    from concourse import mybir as _mybir
    from concourse.bass_utils import run_bass_kernel_spmd as _run

    a = {k: _np.asarray(v) for k, v in inputs.items()}

    def ktile(w):
        return _np.ascontiguousarray(w.reshape(-1, P, w.shape[-1]).transpose(1, 0, 2))

    arrays = {"x": a["x"][0], "meta": a["meta_tokens_2"], "sinks": a["attn_sinks"]}
    for name, c0, n in GROUPS:
        arrays["w_in_" + name] = ktile(a["w_in"][0][:, c0:c0 + n])
    arrays["w_out"] = ktile(a["w_out"][0])
    arrays["lru_wa"], arrays["lru_wx"] = a["lru_wa"][0], a["lru_wx"][0]
    arrays["w2a2"] = _np.concatenate([a["rwkv_w2"][0], a["rwkv_a2"][0]], axis=0)

    def cols(v):
        return v.reshape(-1, P).T
    mu = a["rwkv_mu"][0]
    mu_wa = _np.zeros((P, 1), mu.dtype)
    mu_wa[0:HD, 0] = mu[3 * 256:]
    chan = [a["conv_w"][0].reshape(4, 2, P).transpose(2, 1, 0).reshape(P, 8), cols(a["conv_b"]), cols(a["lru_ba"]),
            cols(a["lru_bx"]), cols(a["lru_lambda"]), cols(mu[0:3 * 256]), mu_wa, cols(a["rwkv_w0"]), cols(a["rwkv_a0"]),
            cols(a["rwkv_kk"]), cols(a["rwkv_ka"]), cols(a["rwkv_rk"]), cols(a["rwkv_gn_w"]), cols(a["rwkv_gn_b"]),
            cols(a["a_norm_2"]), cols(a["kv_norm_2"]), cols(a["b_norm_2"]), cols(a["b_q_norm_2"]), cols(a["kv_lat_norm_2"])]
    arrays["chan"] = _np.concatenate(chan, axis=1)
    arrays["rows"] = _np.stack([a["ln_g"][0], a["ln_b"][0], a["a_scale_2"][0], a["ffn_norm_2"][0], a["ffn_norm_2"][1],
                                a["final_norm_2"]])
    arrays["a_w"] = ktile(a["a_w_2"][0].reshape(D, 256))
    arrays["w_router"] = _np.stack([ktile(_np.concatenate([a["router_g_2"][i], a["router_e_2"][i]], axis=1)) for i in range(2)])
    arrays["b_router"] = _np.concatenate([a["router_g_bias_2"], a["router_e_bias_2"]], axis=1)
    gu = _np.concatenate([a["w_gate_2"], a["w_up_2"]], axis=3).reshape(2 * NE, KD, P, 2 * DE).transpose(0, 2, 1, 3)
    dn = a["w_down_2"].reshape(2 * NE, 2, P, D).transpose(0, 2, 1, 3)
    arrays["w_exp"] = _np.concatenate([gu.reshape(2 * NE, P, -1), dn.reshape(2 * NE, P, -1)], axis=2)
    arrays["w_c"] = ktile(_np.concatenate([a["w_dkv_2"], a["b_w_dq_2"][0]], axis=1))
    uq = a["b_w_uq_2"][0]
    arrays["w_uq"] = ktile(_np.concatenate([uq[:, :, :NOPE].reshape(QL, -1), uq[:, :, NOPE:].reshape(QL, -1)], axis=1))
    arrays["w_uk"] = ktile(a["w_uk_2"].reshape(KVL, -1))
    arrays["w_uv"] = ktile(a["w_uv_2"].reshape(KVL, -1))
    arrays["w_o"] = ktile(a["b_w_o_2"][0])
    freq = (_np.float32(10000.0) ** (-_np.arange(0, ROPE, 2, dtype=_np.float32) / _np.float32(ROPE))).astype(_np.float32)
    ang = _np.arange(L, dtype=_np.float32)[:, None] * freq[None, :]
    table = _np.concatenate([_np.cos(ang), _np.sin(ang)], axis=1).astype(_np.float32)
    rope = _np.zeros((P, NS, ROPE), _np.float32)
    for s, (pos, n) in enumerate(SLOT):
        rope[0:n, s] = table[pos:pos + n]
    arrays["rope"] = rope

    nc = _bacc.Bacc("TRN2", target_bir_lowering=False, num_devices=1)
    arrays = {f"in_{k}": _np.ascontiguousarray(v) for k, v in arrays.items()}
    io = {k[3:]: nc.dram_tensor(k, v.shape, _mybir.dt.from_np(v.dtype), kind="ExternalInput").ap() for k, v in arrays.items()}
    io["out"] = nc.dram_tensor("out_0", (T, D), _mybir.dt.float32, kind="ExternalOutput").ap()
    dumps = {k: nc.dram_tensor("dump_" + k, shp, _mybir.dt.float32, kind="ExternalOutput").ap() for k, shp in DUMPS.items()}
    build(nc, io, dumps)
    r = _run(nc, [arrays], core_ids=[0])
    return r.results[0]["out_0"].reshape(1, T, D)
```

```python
from contextlib import ExitStack

import numpy as np

import concourse.bass as bass
from concourse import mybir

F32 = mybir.dt.float32
I32 = mybir.dt.int32
U32 = mybir.dt.uint32
ALU = mybir.AluOpType
ACT = mybir.ActivationFunctionType
AX = mybir.AxisListType

P = 128
D = 1024
KD = D // P
T = 1024
NT = T // P
HD = 64
AH, AKV = 8, 2
C_LRU = 8.0
LN_EPS, GN_EPS, RMS_EPS = 1e-5, 64e-5, 1e-6
ALPHA = 2.0 ** 0.25
EXP_HALF = float(np.exp(-0.5))
CH = 64

N_META = 16
L = T + N_META
NS = NT + 1
WINDOWS = (2, 4, 8, 16)
PADW = max(WINDOWS)
MH, NOPE, ROPE, VH = 8, 128, 64, 128
QL, KVL = 384, 256
SCALE = (NOPE + ROPE) ** -0.5
NEG = -1e30
NG, EPG = 4, 8
NE = NG * EPG
DE = 256
NOV = (2 * L) // P
NBLK = NE + NOV
SLOTS = NBLK * P

SLOT = [(N_META + P * s, P) for s in range(NT)] + [(0, N_META)]

GROUPS = [("q", 0, 512), ("kv", 512, 256), ("ga", 768, 512), ("lru", 1280, 512),
          ("rk", 1792, 512), ("vwa", 2304, 320), ("gc", 2624, 256)]

CHAN = [("conv_w", 8), ("conv_b", 2), ("lru_ba", 2), ("lru_bx", 2), ("lam", 2), ("mu", 6), ("mu_wa", 1),
        ("w0", 2), ("a0", 2), ("k_k", 2), ("k_a", 2), ("r_k", 2), ("gn_w", 2), ("gn_b", 2),
        ("a_norm", 8), ("kv_norm", 8), ("b_norm", 8), ("q_norm", 3), ("kv_lat", 2)]
CHAN_AT, _n = {}, 0
for _name, _w in CHAN:
    CHAN_AT[_name] = _n
    _n += _w
N_CHAN = _n


class Mark:

    def __init__(self, sem, value):
        self.sem, self.value = sem, value


class Lane:

    def __init__(self, engine, new_sem, name):
        self.e, self.new_sem, self.name = engine, new_sem, name
        self.queue, self.waited = [], {}
        self.sem, self.count = None, 0

    def stage(self, name):
        if self.count or self.sem is None:
            self.sem = self.new_sem(f"{self.name}_{name}")
        self.count = 0

    def last(self):
        return Mark(self.sem, self.count) if self.count else None

    def wait(self, marks):
        for m in marks:
            if m is None:
                continue
            if isinstance(m, (list, tuple)):
                self.wait(m)
            elif self.waited.get(m.sem, 0) < m.value:
                self.waited[m.sem] = m.value
                self.queue.append(lambda m=m: self.e.wait_ge(m.sem, m.value))

    def do(self, make, *after):
        self.wait(after)
        sem = self.sem
        self.queue.append(lambda: make().then_inc(sem, 1))
        self.count += 1
        return Mark(self.sem, self.count)

    def dma(self, sem, out, in_, *after):
        self.wait(after)
        self.queue.append(lambda: self.e.dma_start(out, in_).then_inc(sem.sem, 16))
        return sem.next()

    def play(self, queue=None):
        for make in (self.queue if queue is None else queue):
            make()


class DmaSem:

    def __init__(self, sem):
        self.sem, self.value = sem, 0

    def next(self):
        self.value += 16
        return Mark(self.sem, self.value)


class Vec(Lane):

    def tt(self, out, a, b, op, *after):
        return self.do(lambda: self.e.tensor_tensor(out, a, b, op), *after)

    def ts(self, out, a, s1, s2, op0, op1, *after):
        if op1 is None:
            return self.do(lambda: self.e.tensor_scalar(out, a, s1, None, op0), *after)
        return self.do(lambda: self.e.tensor_scalar(out, a, s1, s2, op0, op1), *after)

    def stt(self, out, a, s, b, op0, op1, *after):
        return self.do(lambda: self.e.scalar_tensor_tensor(out=out, in0=a, scalar=s, in1=b, op0=op0, op1=op1), *after)

    def copy(self, out, a, *after):
        return self.do(lambda: self.e.tensor_copy(out, a), *after)

    def red(self, out, a, op, *after):
        return self.do(lambda: self.e.tensor_reduce(out, a, AX.X, op), *after)

    def recip(self, out, a, *after):
        return self.do(lambda: self.e.reciprocal(out, a), *after)

    def set(self, out, value, *after):
        return self.do(lambda: self.e.memset(out, value), *after)


class Act(Lane):

    def act(self, out, a, func, *after, bias=0.0, scale=1.0, accum=None):
        if accum is not None:
            return self.do(lambda: self.e.activation(out, a, func, bias=bias, scale=scale, accum_out=accum), *after)
        return self.do(lambda: self.e.activation(out, a, func, bias=bias, scale=scale), *after)

    def copy(self, out, a, *after, scale=1.0):
        return self.do(lambda: self.e.activation(out, a, ACT.Copy, bias=0.0, scale=scale), *after)


class Ten(Lane):

    def mms(self, products, *after):
        self.wait(after)
        sem = self.sem

        def make():
            for i, (out, lhsT, rhs, start, stop) in enumerate(products):
                if start is None:
                    ins = self.e.transpose(out, lhsT, rhs)
                else:
                    ins = self.e.matmul(out, lhsT, rhs, start=start, stop=stop, skip_group_check=True)
                if i == len(products) - 1:
                    ins.then_inc(sem, 1)
        self.queue.append(make)
        self.count += 1
        return Mark(self.sem, self.count)


class Buf:

    def __init__(self, ap, sem=None):
        self.ap, self.free, self.sem = ap, [], sem


class Ring:
    def __init__(self, bufs):
        self.bufs, self.at = bufs, 0

    def take(self):
        b = self.bufs[self.at % len(self.bufs)]
        self.at += 1
        return b


def pipelined(items, between=None):
    live = []
    for item in items:
        live = [g for g in live if next(g, "done") != "done"]
        if between:
            between()
        live.append(item)
        next(item)
    while live:
        live = [g for g in live if next(g, "done") != "done"]


def bc_mid(ap, n):
    return ap.unsqueeze(1).to_broadcast([ap.shape[0], n, ap.shape[1]])


def bc_last(ap, n):
    return ap.unsqueeze(2).to_broadcast([ap.shape[0], ap.shape[1], n])


def build(nc, io):
    ctx = ExitStack()
    with ctx:
        def new_sem(name):
            return ctx.enter_context(nc.semaphore(name))

        def dsem(name):
            return DmaSem(new_sem("dma_" + name))

        PE = Ten(nc.tensor, new_sem, "pe")
        V = Vec(nc.vector, new_sem, "dve")
        G = Vec(nc.gpsimd, new_sem, "pool")
        S = Act(nc.scalar, new_sem, "act")
        SP = Lane(nc.sync, new_sem, "sp")
        lanes = [PE, V, G, S, SP]
        compute = [PE, V, G, S]

        def stage(name):
            for lane in compute:
                lane.stage(name)

        ARENA = 53200
        arena = ctx.enter_context(nc.sbuf_tensor("arena", [P, ARENA], F32))
        psum = ctx.enter_context(nc.psum_tensor("psum", [P, 8 * 512], F32))
        top = [0]

        def take(*dims):
            n = int(np.prod(dims))
            o = top[0]
            top[0] += n + (n % 2)
            assert top[0] <= ARENA, (top[0], dims)
            v = arena[:, o:o + n]
            if len(dims) == 2:
                v = v.rearrange("p (a b) -> p a b", a=dims[0])
            if len(dims) == 3:
                v = v.rearrange("p (a b c) -> p a b c", a=dims[0], b=dims[1])
            return v

        def four(ap):
            return ap.rearrange("p (a b) -> p a b", a=4)

        banks = [psum[:, 512 * i:512 * (i + 1)] for i in range(8)]
        psum_ring = Ring([Buf(b) for b in banks])
        marks_out = []
        xn_dram = nc.dram_tensor("xn_rows", (L, D), F32, kind="Internal").ap()
        y_dram = nc.dram_tensor("expert_rows", (SLOTS, D), F32, kind="Internal").ap()

        def barrier():
            ms = [lane.last() for lane in compute] + [Mark(d.sem, d.value) for d in all_dma if d.value]
            for lane in lanes:
                lane.wait(ms)
            for b in psum_ring.bufs:
                b.free = []

        all_dma = []

        by_name = {}

        def dma_sem(name):
            if name not in by_name:
                by_name[name] = dsem(name)
                all_dma.append(by_name[name])
            return by_name[name]

        stage("const")
        ident = take(P)
        sq_sum = take(NS)
        chan = take(N_CHAN)
        one_col, zero_col = take(1), take(1)
        eps_ln, eps_gn, eps_rms, eps_kk = take(1), take(1), take(1), take(1)
        ones = take(P)
        pair_ones = take(P)
        G.set(ident, 0.0)
        G.set(ones, 1.0)
        G.set(pair_ones, 1.0)
        G.set(one_col, 1.0)
        G.set(zero_col, 0.0)
        G.set(eps_ln, LN_EPS)
        G.set(eps_gn, GN_EPS)
        G.set(eps_rms, RMS_EPS)
        m = G.set(eps_kk, 1e-12)

        def keep(out, in_, pattern, base, mult, op, fill, *after):
            return G.do(lambda: G.e.affine_select(out=out, in_=in_, pattern=pattern, compare_op=op, fill=fill,
                                                  base=base, channel_multiplier=mult), *after)

        m = keep(ident, ident, [[-1, P]], 0, 1, ALU.not_equal, 1.0, m)

        def same_block(t, n, *after):
            v = t.rearrange("p (b c) -> p b c", c=n)
            a = keep(v, v, [[-n, P // n], [0, n]], 0, 1, ALU.is_ge, 0.0, *after)
            return keep(v, v, [[n, P // n], [0, n]], n - 1, -1, ALU.is_ge, 0.0, a)

        m_const = same_block(pair_ones, HD, m)
        d_chan = dma_sem("chan")
        m_chan = SP.dma(d_chan, chan, io["chan"])

        def col(name, i=0, rows=P):
            c = CHAN_AT[name] + i
            return chan[0:rows, c:c + 1]

        zero_rows = arena[:, ARENA - D:ARENA]
        m_zrows = G.set(zero_rows, 0.0)

        h_at = top[0]
        h = take(NS, D)
        top[0] = h_at
        w_bufs = Ring([Buf(take(KD, 512), dma_sem(f"w_in{i}")) for i in range(2)])
        top[0] = h_at + NS * D
        xT = take(KD, T)
        yT = take(KD, T)
        base_b1 = top[0]

        stage("x")
        m_xT = []
        x_bufs = [Buf(take(D), dma_sem(f"x{i}")) for i in range(NT)]
        m_x = []
        w_q = w_bufs.take()
        for i, xb_ in enumerate(x_bufs):
            if i == NT // 2:
                m_wq = SP.dma(w_q.sem, w_q.ap, io["w_in_q"])
            m_x.append(SP.dma(xb_.sem, xb_.ap, io["x"][P * i:P * (i + 1), :]))

        def turn_x(i):
            for half in range(2):
                bk = psum_ring.take()
                pv = bk.ap.rearrange("p (a b) -> p a b", a=4)
                mt = PE.mms([(pv[:, k, :], x_bufs[i].ap[:, P * (4 * half + k):P * (4 * half + k + 1)], ident, None, None)
                             for k in range(4)], m_x[i], m_const, bk.free)
                dst = xT[:, 4 * half:4 * half + 4, P * i:P * (i + 1)]
                bk.free = [(V.copy if half else S.copy)(dst, pv, mt)]
            m_xT.append([V.last(), S.last()])
        top[0] = base_b1

        def load_group(name, width):
            b = w_bufs.take()
            wv = b.ap.rearrange("p a b -> p (a b)")[:, 0:KD * width].rearrange("p (a b) -> p a b", a=KD)
            mk = SP.dma(b.sem, wv, io["w_in_" + name], b.free)
            return b, wv, mk

        all_banks = psum_ring.bufs
        psum_ring.bufs, project_ring = all_banks[:6], Ring(all_banks[6:])

        def project_half(w, c0, width, m_w, half):
            bk = project_ring.take()
            return bk, PE.mms([(bk.ap[0:width, :], w[:, k, c0:c0 + width], xT[:, k, 512 * half:512 * half + 512],
                                k == 0, k == KD - 1) for k in range(KD)], m_w, m_xT[4 * half + 3], bk.free)

        def project_steps(w, c0, width, m_w, evac, wb):
            for half in range(2):
                bk, mt = project_half(w, c0, width, m_w, half)
                wb.free = [mt]
                yield
                bk.free = evac(half, bk.ap[0:width, :], mt)

        def project(*args):
            for _ in project_steps(*args):
                pass

        def half_cols(half):
            return slice(512 * half, 512 * half + 512)

        stage("qkv")
        rkv = take(6, T + 2)
        wa = take(T + 2)
        xb = take(2, T + 4)
        base_wa = top[0] - (T + 2) - 2 * (T + 4)
        bonus = take(2, T)
        base_swa = top[0] - 2 * T
        top[0] = base_swa
        qT = take(4, T)
        kd = take(AKV, T)
        v_tok = take(NT, P)
        sig = Ring([Buf(arena[:, o:o + 512]) for o in (h_at + 2 * KD * 512, h_at + 2 * KD * 512 + 512)])
        assert h_at + 2 * KD * 512 + 1024 <= base_b1 - 2 * KD * T
        for half in range(2):
            for i in range(4 * half, 4 * half + 4):
                turn_x(i)
            for j in range(4):
                bk, mt = project_half(w_q.ap, P * j, P, m_wq, half)
                bk.free = [S.copy(qT[:, j, half_cols(half)], bk.ap, mt, scale=HD ** -0.5)]
                w_q.free = [mt]
        wb, w, m_w = load_group("kv", 256)

        def evac_k(hf, ps, mk):
            for kv in range(AKV):
                for dst in range(2):
                    r = V.copy(kd[64 * dst:64 * dst + 64, kv, half_cols(hf)], ps[64 * kv:64 * kv + 64, :], mk)
            return [r]
        project(w, 0, P, m_w, evac_k, wb)
        for g in range(2):
            bk = psum_ring.take()
            pv = bk.ap.rearrange("p (a b) -> p a b", a=4)
            prods = []
            for j in range(4):
                i = 4 * g + j
                prods += [(pv[:, j, :], xT[:, k, P * i:P * (i + 1)], w[:, k, P:2 * P], k == 0, k == KD - 1)
                          for k in range(KD)]
            mt = PE.mms(prods, m_w, m_xT[-1], bk.free)
            bk.free = [S.copy(v_tok[:, 4 * g:4 * g + 4, :], pv, mt)]
        wb.free = [mt]

        def gate(y_at):
            def evac(hf, ps, mk):
                sb = sig.take()
                a = S.act(sb.ap, ps, ACT.Sigmoid, mk, sb.free)
                r = V.tt(yT[:, y_at, half_cols(hf)], ps, sb.ap, ALU.mult, a)
                sb.free = [r]
                return [r]
            return evac

        wb, w, m_w = load_group("ga", 512)
        fill = dma_sem("y_fill")
        for b in range(NE, NBLK):
            m_yfill = SP.dma(fill, y_dram[P * b:P * (b + 1), :], zero_rows, m_zrows)
        for j in range(4):
            project(w, P * j, P, m_w, gate(j), wb)
        m_q, m_kvg = S.last(), V.last()

        stage("swa")
        band = take(2, P)
        mk_ = G.set(band, 0.0)
        mk_ = keep(band[:, 0, :], band[:, 0, :], [[1, P]], 0, -1, ALU.is_gt, NEG, mk_)
        m_band = keep(band[:, 1, :], band[:, 1, :], [[-1, P]], 0, 1, ALU.is_ge, NEG, mk_)
        sink_row, sink = take(AH), take(AH)
        m_s = SP.dma(dma_sem("sinks"), sink_row, io["sinks"].to_broadcast([P, AH]))
        ORDER = [0, 2, 1, 3, 4, 6, 5, 7]
        for g in range(2):
            V.copy(sink[:, 4 * g:4 * g + 4].rearrange("p (c b) -> p b c", c=2),
                   sink_row[:, 4 * g:4 * g + 4].rearrange("p (b c) -> p b c", b=2), m_s)
        m_sink = V.last()
        Pm = [take(AH, 2 * P) for _ in range(2)]
        PT = [take(2 * AH, P) for _ in range(2)]
        st = [[take(AH) for _ in range(6)] for _ in range(3)]
        pm_free, pt_free = [[], [], []], [[], []]
        for lane in (V, S):
            lane.wait([m_yfill])
        V.set(xb[:, :, 0:3], 0.0)
        V.set(rkv[:, :, 0:1], 0.0)
        V.set(wa[0:64, 0:1], 0.0)

        def window(n):
            pm, pt, (mx, nm, rs, es, den, rden) = Pm[n % 2], PT[n % 2], st[n % 3]
            c0 = 0 if n else P
            k0 = P * (n - 1) + c0
            wd = 2 * P - c0
            for b in range(4):
                bk = psum_ring.take()
                pv = bk.ap.rearrange("p (a b) -> p a b", a=2)
                prods = []
                for j in range(2):
                    hh = ORDER[2 * b + j]
                    pr = slice(64 * (hh % 2), 64 * (hh % 2) + 64)
                    prods.append((pv[:, j, c0:], qT[pr, hh // 2, P * n:P * (n + 1)], kd[pr, hh // 4, k0:k0 + wd], True, True))
                mt = PE.mms(prods, m_q, m_kvg, bk.free)
                a = V.tt(pm[:, 2 * b:2 * b + 2, c0:], pv[:, :, c0:],
                         bc_mid(band.rearrange("p a b -> p (a b)")[:, c0:], 2), ALU.add, mt, m_band, pm_free[n % 2])
                bk.free = [a]
            a = V.red(mx, pm[:, :, c0:], ALU.max, a)
            a = V.tt(mx, mx, sink, ALU.max, a, m_sink)
            a = V.ts(nm, mx, -1.0, None, ALU.mult, None, a)
            e_in = V.tt(es, sink, nm, ALU.add, a)
            for j in range(AH):
                e = S.act(pm[:, j, c0:], pm[:, j, c0:], ACT.Exp, a, bias=nm[:, j:j + 1], accum=rs[:, j:j + 1])
            e = S.act(es, es, ACT.Exp, e_in)
            yield
            a = V.tt(den, rs, es, ALU.add, e)
            a = V.recip(rden, den, a)
            a = V.tt(pm[:, :, c0:], pm[:, :, c0:], bc_last(rden, wd), ALU.mult, a)
            yield
            parts = [0, 1] if n else [1]
            tr = []
            for b in range(4):
                bk = psum_ring.take()
                pv = bk.ap.rearrange("p (a b) -> p a b", a=4)
                prods = []
                for j in range(2):
                    for u in parts:
                        prods.append((pv[:, 2 * j + u, :], pm[:, 2 * b + j, P * u:P * (u + 1)], ident, None, None))
                mt = PE.mms(prods, a, bk.free)
                if n:
                    src, dst = pv, pt[:, 4 * b:4 * b + 4, :]
                else:
                    src, dst = pv[:, 1::2, :], pt[:, 4 * b + 1:4 * b + 4:2, :]
                bk.free = [(S.copy if b % 2 else V.copy)(dst, src, mt, pt_free[n % 2])]
                tr.append(bk.free[0])
            pm_free[n % 2] = [mt]
            yield
            bk = psum_ring.take()
            pv = bk.ap.rearrange("p (a b) -> p a b", a=4)
            prods = []
            for j, hh in enumerate(ORDER):
                pr = slice(64 * (hh % 2), 64 * (hh % 2) + 64)
                for u in parts:
                    prods.append((pv[pr, hh // 2, :], v_tok[:, n - 1 + u, 64 * (hh // 4):64 * (hh // 4) + 64],
                                  pt[:, 2 * j + u, :], u == parts[0], u == 1))
            mt = PE.mms(prods, tr, bk.free)
            pt_free[n % 2] = [mt]
            bk.free = [V.tt(yT[:, 0:4, P * n:P * (n + 1)], pv, yT[:, 0:4, P * n:P * (n + 1)], ALU.mult, mt)]

        def other_projections():
            def keep_in(dst, c0):
                return lambda hf, ps, mk: [S.copy(dst[:, c0 + 512 * hf:c0 + 512 * hf + 512], ps, mk)]
            for name, width, tiles in (
                    ("rk", 512, [(P * j, P, keep_in(rkv[:, j, :], 1)) for j in range(4)]),
                    ("vwa", 320, [(P * j, P, keep_in(rkv[:, 4 + j, :], 1)) for j in range(2)] +
                     [(256, 64, keep_in(wa[0:64, :], 1))]),
                    ("lru", 512, [(P * j, P, keep_in(xb[:, j, :], 3)) for j in range(2)] +
                     [(256 + P * j, P, gate(4 + j)) for j in range(2)]),
                    ("gc", 256, [(P * j, P, gate(6 + j)) for j in range(2)])):
                wb, w, m_w = load_group(name, width)
                for c0, n, evac in tiles:
                    yield from project_steps(w, c0, n, m_w, evac, wb)

        fill = other_projections()

        def windows():
            for n in range(NT):
                next(fill)
                yield window(n)
        pipelined(windows(), lambda: next(fill))

        barrier()
        stage("prep")
        top[0] = base_swa + 2 * T

        def rg_lru():
            xc, ra, ib, q_, u_ = take(2, T), take(2, T), take(2, T), take(2, T), take(2, T)
            wa_d, wx_d = take(2, P), take(2, P)
            zz = G.set(wa_d, 0.0)
            zz = G.set(wx_d, 0.0)
            d_l = dma_sem("lru_w")
            for dst, name in ((wa_d, "lru_wa"), (wx_d, "lru_wx")):
                for b in range(4):
                    pr = slice(64 * (b % 2), 64 * (b % 2) + 64)
                    m_lw = SP.dma(d_l, dst[pr, b // 2, 64 * (b % 2):64 * (b % 2) + 64], io[name][b], zz)
            lam = chan[:, CHAN_AT["lam"]:CHAN_AT["lam"] + 2]
            neg, ab, e_, s_, s2, ac, cl, ncl = (take(2) for _ in range(8))
            a = V.ts(neg, lam, -1.0, None, ALU.mult, None, m_chan)
            a = V.tt(ab, lam, neg, ALU.max, a)
            a2 = S.act(e_, ab, ACT.Exp, a, scale=-1.0)
            yield
            a = V.ts(s_, e_, 2.0, None, ALU.add, None, a2)
            a = V.recip(s_, s_, a)
            a = V.tt(s_, s_, e_, ALU.mult, a)
            a = V.tt(s2, s_, s_, ALU.mult, a)
            a = V.ts(ac, s2, 1.0 / 19, 1.0 / 17, ALU.mult, ALU.add, a)
            for c in (15, 13, 11, 9, 7, 5, 3, 1):
                a = V.tt(ac, ac, s2, ALU.mult, a)
                a = V.ts(ac, ac, 1.0 / c, None, ALU.add, None, a)
            a = V.tt(ac, ac, s_, ALU.mult, a)
            a = V.ts(ac, ac, 2.0, None, ALU.mult, None, a)
            a = V.ts(neg, neg, 0.0, None, ALU.max, None, a)
            a = V.tt(ac, ac, neg, ALU.add, a)
            a = V.ts(cl, ac, -C_LRU, None, ALU.mult, None, a)
            m_cl = V.ts(ncl, ac, C_LRU, None, ALU.mult, None, a)
            yield
            m_r = []
            for j in range(2):
                a = V.ts(xc[:, j, :], xb[:, j, 0:T], col("conv_w", 4 * j), col("conv_b", j), ALU.mult, ALU.add)
                for t in range(1, 4):
                    a = V.stt(xc[:, j, :], xb[:, j, t:t + T], col("conv_w", 4 * j + t), xc[:, j, :], ALU.mult, ALU.add, a)
                    yield
                for wt, dst, bias in ((wa_d, ra, "lru_ba"), (wx_d, ib, "lru_bx")):
                    for hf in range(2):
                        bk = psum_ring.take()
                        mt = PE.mms([(bk.ap, wt[:, j, :], xc[:, j, half_cols(hf)], True, True)], a, m_lw, bk.free)
                        bk.free = [S.act(dst[:, j, half_cols(hf)], bk.ap, ACT.Sigmoid, mt, bias=col(bias, j))]
                m_r.append(S.last())
                yield
            m_q = []
            for j in range(2):
                th = S.act(q_[:, j, :], ra[:, j, :], ACT.Tanh, m_r[j], m_cl, scale=ncl[:, j:j + 1])
                ea = S.act(ra[:, j, :], ra[:, j, :], ACT.Exp, th, scale=cl[:, j:j + 1])
                g = G.tt(ib[:, j, :], ib[:, j, :], xc[:, j, :], ALU.mult, m_r[j])
                yield
                a = V.tt(u_[:, j, :], ra[:, j, :], ra[:, j, :], ALU.mult, ea)
                m_q.append((V.stt(q_[:, j, :], u_[:, j, :], 1.0, q_[:, j, :], ALU.add, ALU.mult, a, th), g, a))
                yield
            m_sq = [S.act(q_[:, j, :], q_[:, j, :], ACT.Sqrt, m_q[j][0]) for j in range(2)]
            yield
            for j in range(2):
                a = V.tt(u_[:, j, :], ib[:, j, :], q_[:, j, :], ALU.mult, m_q[j][0], m_q[j][1], m_sq[j])
                yield
                a = V.do(lambda j=j: nc.vector.tensor_tensor_scan(xc[:, j, :], ra[:, j, :], u_[:, j, :], 0.0,
                                                                  ALU.mult, ALU.add), a)
                yield
                V.tt(yT[:, 4 + j, :], yT[:, 4 + j, :], xc[:, j, :], ALU.mult, a)
                yield

        R = [rkv[:, j, 1:T + 1] for j in range(6)]
        av, Lc, Ep, kk = (take(2, T) for _ in range(4))
        base_tmp = top[0]
        sgm, Em = take(2, T), take(2, T)
        tmp = [take(T) for _ in range(2)]
        w2a2 = take(256)
        omka = take(2)
        reset = take(T)
        G.wait([m_yfill])

        def prepare():
            m_w2 = SP.dma(dma_sem("w2a2"), w2a2[0:64, :], io["w2a2"])
            rz = G.set(reset, 1.0)
            m_reset = G.set(reset.rearrange("p (c s) -> p c s", s=CH)[:, :, 0:1], 0.0, rz)
            m_om = V.ts(omka, chan[:, CHAN_AT["k_a"]:CHAN_AT["k_a"] + 2], -1.0, 1.0, ALU.mult, ALU.add)
            a = V.tt(tmp[0][0:64, :], wa[0:64, 0:T], wa[0:64, 1:T + 1], ALU.subtract)
            m_wa = V.stt(wa[0:64, 1:T + 1], tmp[0][0:64, :], col("mu_wa", 0, 64), wa[0:64, 1:T + 1], ALU.mult, ALU.add, a)
            m_th = S.act(wa[0:32, 1:T + 1], wa[0:32, 1:T + 1], ACT.Tanh, m_wa)
            m_sg, m_sh = [], []
            for j in range(2):
                for dst, rows, bias in ((sgm, slice(0, 32), "w0"), (av, slice(32, 64), "a0")):
                    for hf in range(2):
                        bk = psum_ring.take()
                        mt = PE.mms([(bk.ap, w2a2[rows, P * j:P * (j + 1)], wa[rows, 1 + 512 * hf:513 + 512 * hf], True, True)],
                                    m_th, m_w2, bk.free)
                        bk.free = [S.act(dst[:, j, half_cols(hf)], bk.ap, ACT.Sigmoid, mt, bias=col(bias, j))]
                m_sg.append(S.last())
            for j in (2, 3, 0, 1, 4, 5):
                t_ = tmp[j % 2]
                a = V.tt(t_, rkv[:, j, 0:T], R[j], ALU.subtract, V.last())
                yield
                m_sh.append(V.stt(R[j], t_, col("mu", j), R[j], ALU.mult, ALU.add, a))
                yield
            for j in range(2):
                a = V.do(lambda j=j: nc.vector.tensor_tensor_scan(Lc[:, j, :], reset, sgm[:, j, :], 0.0, ALU.mult, ALU.add),
                         m_sg[j], m_reset)
                a_x = G.tt(sgm[:, j, :], Lc[:, j, :], sgm[:, j, :], ALU.subtract, a)
                m_ep = S.act(Ep[:, j, :], Lc[:, j, :], ACT.Exp, a, scale=-EXP_HALF)
                m_em = S.act(Em[:, j, :], Lc[:, j, :], ACT.Exp, a, scale=EXP_HALF)
                m_ex = S.act(sgm[:, j, :], sgm[:, j, :], ACT.Exp, a_x, scale=-EXP_HALF)
                yield
                a = V.ts(kk[:, j, :], R[2 + j], col("k_k", j), None, ALU.mult, None, m_sh)
                sq = S.act(tmp[0], kk[:, j, :], ACT.Square, a, PE.last())
                for hf in range(2):
                    bk = psum_ring.take()
                    mt = PE.mms([(bk.ap, pair_ones, tmp[0][:, half_cols(hf)], True, True)], sq, bk.free)
                    bk.free = [S.act(tmp[1][:, half_cols(hf)], bk.ap, ACT.Sqrt, mt, V.last(), bias=eps_kk)]
                m_s = S.last()
                yield
                a = V.recip(tmp[1], tmp[1], m_s)
                yield
                m_kk = V.tt(kk[:, j, :], kk[:, j, :], tmp[1], ALU.mult, a)
                yield
                a = V.ts(tmp[1], av[:, j, :], col("k_a", j), omka[:, j:j + 1], ALU.mult, ALU.add, m_kk, m_om)
                a = V.tt(R[2 + j], R[2 + j], tmp[1], ALU.mult, a)
                yield
                m_rk = V.stt(tmp[0], R[j], col("r_k", j), R[2 + j], ALU.mult, ALU.mult, a, PE.last())
                for hf in range(2):
                    bk = psum_ring.take()
                    mt = PE.mms([(bk.ap, pair_ones, tmp[0][:, half_cols(hf)], True, True)], m_rk, bk.free)
                    bk.free = [V.tt(bonus[:, j, half_cols(hf)], bk.ap, R[4 + j][:, half_cols(hf)], ALU.mult, mt)]
                yield
                a = V.tt(av[:, j, :], av[:, j, :], kk[:, j, :], ALU.mult, m_kk, a)
                G.tt(R[2 + j], R[2 + j], Em[:, j, :], ALU.mult, m_rk, m_em)
                G.tt(R[j], R[j], Ep[:, j, :], ALU.mult, m_ep)
                yield
                V.tt(av[:, j, :], av[:, j, :], Em[:, j, :], ALU.mult, a, m_em)
                yield
                V.tt(kk[:, j, :], kk[:, j, :], sgm[:, j, :], ALU.mult, m_ex, a)
                yield

        for turn, _ in enumerate(prepare()):
            if turn % 3 == 0:
                next(fill, None)
        for _ in fill:
            pass
        psum_ring.bufs = all_banks

        barrier()
        stage("rwkv")
        Bf = [av[:, j, :] for j in range(2)]
        Af = [kk[:, j, :] for j in range(2)]
        Kf, Rf, Vf = [R[2], R[3]], [R[0], R[1]], [R[4], R[5]]
        top[0] = h_at
        lru_steps = rg_lru()
        next(lru_steps)
        end_lru = top[0]
        yb = Lc
        areas = [[base_wa, base_wa + T + 2], [base_tmp, ARENA], [end_lru, base_b1 - KD * T]]

        def take_dead(*dims):
            n = int(np.prod(dims))
            for area in areas:
                if area[0] + n <= area[1]:
                    o = area[0]
                    area[0] += n
                    v = arena[:, o:o + n]
                    return v.rearrange("p (a b) -> p a b", a=dims[0]) if len(dims) == 2 else v
            raise AssertionError(dims)

        NST = 2 * NT + 1
        STt = take_dead(NST, P).rearrange("p c (a v) -> p c a v", a=2)
        m_state = [V.set(STt[:, 0], 0.0)]
        mN, mNT, mC32, mC64, mUp, mUpS = (take_dead(P) for _ in range(6))
        m_a = G.set(mN, -1.0)
        m_a = keep(mN, mN, [[-1, P]], 0, 1, ALU.is_gt, 0.0, m_a)
        m_a = same_block(mN, 16, m_a)
        m_a = G.set(mNT, -1.0, m_a)
        m_a = keep(mNT, mNT, [[1, P]], 0, -1, ALU.is_gt, 0.0, m_a)
        m_a = same_block(mNT, 16, m_a)

        def off_block(t, n, *after):
            hn = n // 2
            a = G.set(t, 1.0, *after)
            v = t.rearrange("p (b u c) -> p b u c", u=2, c=hn)
            a = G.set(v[:, :, 0, :], 0.0, a)
            a = keep(v, v, [[-n, P // n], [0, 2], [0, hn]], 0, 1, ALU.is_ge, 0.0, a)
            return keep(v, v, [[n, P // n], [0, 2], [0, hn]], hn - 1, -1, ALU.is_ge, 0.0, a)

        m_a = off_block(mC32, 32, m_a)
        m_a = off_block(mC64, 64, m_a)
        m_a = G.set(mUp, 1.0, m_a)
        m_a = keep(mUp, mUp, [[1, P]], 0, -1, ALU.is_ge, 0.0, m_a)
        m_a = same_block(mUp, CH, m_a)
        m_a = G.set(mUpS, 1.0, m_a)
        m_a = keep(mUpS, mUpS, [[1, P]], 0, -1, ALU.is_gt, 0.0, m_a)
        m_mask = same_block(mUpS, CH, m_a)

        def tile_set(*free):
            return dict(tok=take_dead(8, P), mats=[take_dead(4, P) for _ in range(15)], GT=take_dead(2, P),
                        small=[take_dead(4, HD) for _ in range(3)], stg=take_dead(2, HD), free=list(free))
        sets = [tile_set(m_mask)]

        def heads(ap, par):
            return ap.rearrange("p (j r) c -> p j r c", r=2)[:, :, par, :]

        def mm4(lhs, rhs, *after):
            bk = psum_ring.take()
            pv = four(bk.ap)
            mt = PE.mms([(pv[:, i, :], lhs[:, i, :], rhs[:, i, :], True, True) for i in range(4)], bk.free, *after)
            return bk, pv, mt

        def tile_chunks(i):
            own = sets[i % 2]
            tk = own["tok"]
            N_, NT_, CT32, CT64, AKT, RBT, RKT, PA, PB, PTA, PTB, XTa, XTb, X_, Q_ = own["mats"]
            GT, (AKV_, U0n, SA), stg = own["GT"], own["small"], own["stg"]
            cols = slice(P * i, P * (i + 1))
            free = own["free"]
            for half, srcs in enumerate(((Bf[0], Bf[1], Kf[0], Kf[1]), (Af[0], Af[1], Vf[0], Vf[1]))):
                bk = psum_ring.take()
                mt = PE.mms([(four(bk.ap)[:, j, :], s_[:, cols], ident, None, None) for j, s_ in enumerate(srcs)], bk.free)
                bk.free = [S.copy(tk[:, 4 * half:4 * half + 4, :], four(bk.ap), mt, free)]
            m_tok = S.last()

            def htok(kind, hh):
                return tk[:, 2 * kind + hh // 2, 64 * (hh % 2):64 * (hh % 2) + 64]
            for par in range(2):
                pr = slice(64 * par, 64 * par + 64)
                A_, B_, K_, R_ = ([f[j][pr, cols] for j in range(2)] for f in (Af, Bf, Kf, Rf))
                bk = psum_ring.take()
                pv = four(bk.ap)
                mt = PE.mms([(pv[:, j, :], A_[j], B_[j], True, True) for j in range(2)] +
                            [(pv[:, 2 + j, :], B_[j], A_[j], True, True) for j in range(2)], bk.free)
                V.tt(heads(N_, par), pv[:, 0:2, :], bc_mid(mN, 2), ALU.mult, mt, free)
                V.tt(heads(NT_, par), pv[:, 2:4, :], bc_mid(mNT, 2), ALU.mult)
                V.tt(heads(CT32, par), pv[:, 2:4, :], bc_mid(mC32, 2), ALU.mult)
                m_n = V.tt(heads(CT64, par), pv[:, 2:4, :], bc_mid(mC64, 2), ALU.mult)
                bk.free = [m_n]
            yield
            m_x = V.tt(XTa, NT_, bc_mid(ident, 4), ALU.add, m_n)
            bk, pv, mt = mm4(NT_, N_, m_n)
            m2 = [S.copy(PA, pv, mt)]
            bk.free = m2[:1]
            bk, pv, mt = mm4(N_, NT_)
            m2.append(V.copy(PTA, pv, mt))
            bk.free = m2[1:]
            yield
            for par in range(2):
                pr = slice(64 * par, 64 * par + 64)
                A_, B_, K_, R_ = ([f[j][pr, cols] for j in range(2)] for f in (Af, Bf, Kf, Rf))
                bk = psum_ring.take()
                pv = four(bk.ap)
                mt = PE.mms([(pv[:, j, :], K_[j], A_[j], True, True) for j in range(2)] +
                            [(pv[:, 2 + j, :], B_[j], R_[j], True, True) for j in range(2)], bk.free)
                V.tt(heads(AKT, par), pv[:, 0:2, :], bc_mid(mUpS, 2), ALU.mult, mt)
                bk.free = [V.tt(heads(RBT, par), pv[:, 2:4, :], bc_mid(mUp, 2), ALU.mult)]
            m_ak = V.last()
            yield
            bk, pv, mt = mm4(PA, XTa, m2, m_x)
            m_x = V.tt(XTb, XTa, pv, ALU.add, mt)
            bk.free = [m_x]
            bk, pv, mt = mm4(PTA, PA)
            m4 = [S.copy(PB, pv, mt)]
            bk.free = m4[:1]
            bk, pv, mt = mm4(PA, PTA)
            m4.append(V.copy(PTB, pv, mt))
            bk.free = m4[1:]
            yield
            for par in range(2):
                pr = slice(64 * par, 64 * par + 64)
                K_, R_ = ([f[j][pr, cols] for j in range(2)] for f in (Kf, Rf))
                bk = psum_ring.take()
                pv = four(bk.ap)
                mt = PE.mms([(pv[:, j, :], K_[j], R_[j], True, True) for j in range(2)], bk.free)
                bk.free = [V.tt(heads(RKT, par), pv[:, 0:2, :], bc_mid(mUp, 2), ALU.mult, mt)]
            m_m = V.last()
            bk, pv, mt = mm4(PB, XTb, m4, m_x)
            m_x = V.tt(XTa, XTb, pv, ALU.add, mt)
            bk.free = [m_x]
            bk, pv, mt = mm4(PTB, PB)
            m8 = S.copy(PA, pv, mt)
            bk.free = [m8]
            yield
            bk = psum_ring.take()
            up = bk.ap[:, 0:4 * HD].rearrange("p (a b) -> p a b", a=4)
            mt = PE.mms([(up[:, hh, :], AKT[:, hh, :], htok(3, hh), True, True) for hh in range(4)], m_ak, m_tok, bk.free)
            m_akv = S.copy(AKV_, up, mt)
            bk.free = [m_akv]
            bk, pv, mt = mm4(PA, XTa, m8, m_x)
            m_x = V.tt(XTb, XTa, pv, ALU.add, mt)
            bk.free = [m_x]
            yield
            bk = psum_ring.take()
            mt = PE.mms([(four(bk.ap)[:, j, :], XTb[:, j, :], ident, None, None) for j in range(4)], m_x, bk.free)
            m_xx = S.copy(X_, four(bk.ap), mt)
            bk.free = [m_xx]
            yield
            bk, pv, mt = mm4(CT32, X_, m_xx)
            m_q_ = S.copy(Q_, pv, mt)
            bk.free = [m_q_]
            yield
            bk, pv, mt = mm4(XTb, Q_, m_q_)
            m_pb = V.tt(PB, X_, pv, ALU.subtract, mt)
            bk.free = [m_pb]
            bk, pv, mt = mm4(Q_, XTb)
            m_x = V.tt(XTa, XTb, pv, ALU.subtract, mt)
            bk.free = [m_x]
            yield
            bk, pv, mt = mm4(CT64, PB, m_pb)
            m_q_ = S.copy(Q_, pv, mt)
            bk.free = [m_q_]
            yield "half way"
            bk, pv, mt = mm4(Q_, XTa, m_q_, m_x)
            m_x = V.tt(XTb, XTa, pv, ALU.subtract, mt)
            bk.free = [m_x]
            yield
            bk = psum_ring.take()
            gp = bk.ap[:, 0:2 * P].rearrange("p (a b) -> p a b", a=2)
            mt = PE.mms([(gp[64 * (hh % 2):64 * (hh % 2) + 64, hh // 2, :], htok(2, hh), XTb[:, hh, :], True, True)
                         for hh in range(4)], m_x, bk.free)
            m_g = S.copy(GT, gp, mt)
            bk.free = [m_g]
            bk = psum_ring.take()
            up = bk.ap[:, 0:4 * HD].rearrange("p (a b) -> p a b", a=4)
            mt = PE.mms([(up[:, hh, :], XTb[:, hh, :], AKV_[:, hh, :], True, True) for hh in range(4)], m_akv, bk.free)
            m_u = V.ts(U0n, up, -1.0, None, ALU.mult, None, mt)
            bk.free = [m_u]
            yield
            for c in range(2):
                ci = 2 * i + c
                cr = slice(64 * c, 64 * c + 64)
                for par in range(2):
                    pr = slice(64 * par, 64 * par + 64)
                    bk = psum_ring.take()
                    sv = bk.ap[:, 0:2 * HD].rearrange("p (a b) -> p a b", a=2)
                    mt = PE.mms([(sv[cr, j, :], GT[pr, j, cr], STt[pr, ci, j, :], True, True) for j in range(2)],
                                m_state[-1], m_g, bk.free)
                    m_sa = V.tt(heads(SA, par)[cr], heads(U0n, par)[cr], sv[cr], ALU.subtract, mt, m_u)
                    bk.free = [m_sa]
                yield
                bk = psum_ring.take()
                dv = bk.ap[:, 0:2 * HD].rearrange("p (a b) -> p a b", a=2)
                prods = []
                for hh in range(4):
                    o = dv[64 * (hh % 2):64 * (hh % 2) + 64, hh // 2, :]
                    prods += [(o, htok(1, hh)[cr], htok(3, hh)[cr], True, False),
                              (o, htok(0, hh)[cr], SA[cr, hh, :], False, True)]
                mt = PE.mms(prods, m_sa, bk.free)
                a = V.tt(stg, STt[:, ci], dv, ALU.add, mt, m_state[-1])
                bk.free = [a]
                last_col = P * i + 64 * c + 63
                for j in range(2):
                    m_s = V.ts(STt[:, ci + 1, j, :], stg[:, j, :], Ep[:, j, last_col:last_col + 1], None, ALU.mult, None, a)
                m_state.append(m_s)
                yield
            for par in range(2):
                pr = slice(64 * par, 64 * par + 64)
                bk = psum_ring.take()
                yv = bk.ap[:, 0:2 * P].rearrange("p (a b) -> p a b", a=2)
                prods = []
                for j in range(2):
                    hh = 2 * j + par
                    prods += [(yv[pr, j, :], SA[:, hh, :], RBT[:, hh, :], True, False),
                              (yv[pr, j, :], htok(3, hh), RKT[:, hh, :], False, False)]
                    for c in range(2):
                        prods.append((yv[pr, j, 64 * c:64 * c + 64], STt[pr, 2 * i + c, j, :],
                                      Rf[j][pr, P * i + 64 * c:P * i + 64 * c + 64], False, c == 1))
                mt = PE.mms(prods, m_m, m_state[-1], bk.free)
                bk.free = [S.copy(yb[pr, :, cols], yv[pr], mt)]
            m_y = S.last()
            yield
            y2 = yb[:, :, cols]
            sq2, vv2 = (own["mats"][0].rearrange("p a b -> p (a b)")[:, 256 * u:256 * u + 256].rearrange("p (a b) -> p a b", a=2)
                        for u in range(2))
            bk = psum_ring.take()
            pv = bk.ap[:, 0:2 * P].rearrange("p (a b) -> p a b", a=2)
            mt = PE.mms([(pv[:, j, :], pair_ones, y2[:, j, :], True, True) for j in range(2)], m_y, bk.free)
            a = V.stt(y2, pv, -1.0 / HD, y2, ALU.mult, ALU.add, mt)
            bk.free = [a]
            sq = S.act(sq2, y2, ACT.Square, a)
            yield
            bk = psum_ring.take()
            pv = bk.ap[:, 0:2 * P].rearrange("p (a b) -> p a b", a=2)
            mt = PE.mms([(pv[:, j, :], pair_ones, sq2[:, j, :], True, True) for j in range(2)], sq, bk.free)
            b = S.act(vv2, pv, ACT.Sqrt, mt, bias=eps_gn, scale=1.0 / HD)
            bk.free = [b]
            yield
            b = V.recip(vv2, vv2, b)
            b = V.tt(y2, y2, vv2, ALU.mult, a, b)
            for j in range(2):
                c = V.ts(y2[:, j, :], y2[:, j, :], col("gn_w", j), col("gn_b", j), ALU.mult, ALU.add, b)
            c = V.tt(y2, y2, bonus[:, :, cols], ALU.add, c)
            c = V.tt(yT[:, 6:8, cols], yT[:, 6:8, cols], y2, ALU.mult, c)
            own["free"] = [c, mt]

        def two_tiles():
            live, i, done = [(0, tile_chunks(0))], 1, set()
            while live:
                for n, g in list(live):
                    said = next(g, "done")
                    if n == 0 and len(sets) == 1:
                        for _ in range(2):
                            next(lru_steps, None)
                    if said == "done":
                        live.remove((n, g))
                        done.add(n)
                    elif said == "half way" and i < NT:
                        assert i < 2 or i - 2 in done
                        if len(sets) == 1:
                            for _ in lru_steps:
                                pass
                            areas.extend([[h_at, end_lru], [base_wa + T + 2, base_swa]])
                            sets.append(tile_set(*(lane.last() for lane in compute)))
                        live.append((i, tile_chunks(i)))
                        i += 1
        two_tiles()

        barrier()
        stage("out1")
        top[0] = base_b1
        wo1 = take(KD, D)
        m_wo = [SP.dma(dma_sem(f"w_out{k}"), wo1[:, k, :], io["w_out"][:, k, :]) for k in range(KD)]
        lng, lnb = take(D), take(D)
        xr = Ring([Buf(take(D), dma_sem(f"xr{i}")) for i in range(2)])
        stats = take(12)
        d_ln = dma_sem("ln")
        SP.dma(d_ln, lng, io["rows"][0:1, :].to_broadcast([P, D]))
        m_ln = SP.dma(d_ln, lnb, io["rows"][1:2, :].to_broadcast([P, D]))
        z = V.set(h[:, NT, :], 0.0)
        m_meta = SP.dma(dma_sem("meta"), h[0:N_META, NT, :], io["meta"], z)
        mvs = [take(2) for _ in range(NT)]
        junk = take(D)

        def square_sum(s, junk, *after):
            return S.act(junk, h[:, s, :], ACT.Square, after, S.last(), accum=sq_sum[:, s:s + 1])

        square_sum(NT, junk, m_meta)
        n_g = len(WINDOWS)
        base_bands = ARENA - NS * D - n_g * (P + 2 * PADW) - PADW
        assert top[0] <= base_bands
        scratch_top, top[0] = top[0], base_bands
        bands, tails, first, step_i = take(n_g, P), take(n_g, PADW), take(n_g, N_META), take(PADW)
        top[0] = scratch_top
        a_i = G.do(lambda: G.e.iota(step_i.bitcast(I32), [[1, PADW]], base=1, channel_multiplier=0))
        a_i = G.copy(step_i, step_i.bitcast(I32), a_i)
        for g, w in enumerate(WINDOWS):
            a = G.set(tails[:, g, :], 1.0 / w)
            for rows, base in ((slice(96, P), 96 - P), (slice(0, N_META), -N_META)):
                v = tails[rows, g, :]
                a = keep(v, v, [[-1, PADW]], base + w, 1, ALU.is_gt, 0.0, a)
            a = G.set(bands[:, g, :], 1.0 / w)
            v = bands[:, g, :]
            a = keep(v, v, [[1, P]], 0, -1, ALU.is_ge, 0.0, a)
            a = keep(v, v, [[-1, P]], w, 1, ALU.is_gt, 0.0, a)
            G.tt(v, v, ident, ALU.subtract, a)
            v = first[0:N_META, g, :]
            a = G.ts(v, step_i[0:N_META, :], float(w), None, ALU.min, None, a_i)
            a = V.recip(v, v, a)
            a = keep(v, v, [[1, N_META]], 0, -1, ALU.is_ge, 0.0, a)
            a = keep(v, v, [[-1, N_META]], w, 1, ALU.is_gt, 0.0, a)
            G.tt(v, v, ident[0:N_META, 0:N_META], ALU.subtract, a)
        m_bands = G.last()
        for g in range(0, NT, 4):
            bks = [[psum_ring.take() for _ in range(2)] for _ in range(4)]
            order = [(k, j) for k in range(KD) for j in range(4)] if g == 0 else [(k, j) for j in range(4) for k in range(KD)]
            for k, j in order:
                for hf in range(2):
                    bk, i = bks[j][hf], g + j
                    bk.mt = PE.mms([(bk.ap, yT[:, k, P * i:P * (i + 1)], wo1[:, k, half_cols(hf)], k == 0, k == KD - 1)],
                                   m_wo[k], bk.free if k == 0 else None)
            for j in range(4):
                i = g + j
                mv = mvs[i]
                xb_ = xr.take()
                m = SP.dma(xb_.sem, xb_.ap, io["x"][P * i:P * (i + 1), :], xb_.free)
                a_ = []
                for hf in range(2):
                    bk = bks[j][hf]
                    bk.free = [V.stt(h[:, i, half_cols(hf)], xb_.ap[:, half_cols(hf)], ALPHA, bk.ap, ALU.mult, ALU.add,
                                     bk.mt, m)]
                    a_.append(V.do(lambda i=i, hf=hf: nc.vector.bn_stats(stats[:, 6 * hf:6 * hf + 6], h[:, i, half_cols(hf)]),
                                   bk.free[0]))
                xb_.free = [V.last()]
                a = V.do(lambda mv=mv: nc.vector.bn_aggr(mv, stats), a_)
                s = S.act(mv[:, 1:2], mv[:, 1:2], ACT.Sqrt, a, bias=eps_ln)
                a = V.recip(mv[:, 1:2], mv[:, 1:2], s)
                a = V.ts(h[:, i, :], h[:, i, :], mv[:, 0:1], mv[:, 1:2], ALU.subtract, ALU.mult, a)
                L_ = V if i == NT - 1 else G
                a = L_.tt(h[:, i, :], h[:, i, :], lng, ALU.mult, a, m_ln)
                a = L_.tt(h[:, i, :], h[:, i, :], lnb, ALU.add, a)
                square_sum(i, junk, a)
        barrier()
        top[0] = h_at + NS * D
        idx = take(NBLK)
        dest = take(NS, 2)
        gates = take(NS, 2)
        counts = take(32)
        rstd = take(NS)
        scr = take(16)
        base_b2 = top[0]

        def rms(slots=slice(0, NS)):
            r = rstd[:, slots]
            a = S.act(r, sq_sum[:, slots], ACT.Sqrt, S.last(), bias=eps_rms, scale=1.0 / D)
            return V.recip(r, r, a)

        barrier()
        stage("pool")
        top[0] = base_b2
        xn = Ring([Buf(take(D)) for _ in range(4)])
        junk = take(D)
        pooled = Ring([Buf(take(KD, P)) for _ in range(3)])
        a_w = take(KD, 256)
        arow = take(D)
        scaled = Ring([Buf(take(D)) for _ in range(2)])
        assert top[0] <= base_bands
        d_pw = dma_sem("pool_w")
        SP.dma(d_pw, a_w, io["a_w"])
        m_aw = SP.dma(d_pw, arow, io["rows"][2:3, :].to_broadcast([P, D]))
        m_r = rms()

        rows_of = {}

        def pool_slot(s, prev):
            pos, n = SLOT[s]
            xb_ = rows_of[s] = xn.take()
            xs = xb_.ap
            m_x = V.ts(xs, h[:, s, :], rstd[:, s:s + 1], None, ALU.mult, None, m_r, xb_.free)
            xb_.free = []
            yield
            pl = pooled.take()
            cp = []
            for half in range(2):
                bk = psum_ring.take()
                pv = four(bk.ap)
                prods = []
                for j in range(4):
                    k = 4 * half + j
                    g, fs = k // 2, slice(P * k, P * (k + 1))
                    if prev is None:
                        prods.append((pv[:, j, 0:n], xs[0:n, fs], first[0:n, g, :], True, True))
                        continue
                    before = rows_of[prev].ap
                    rows = slice(0, N_META) if prev == NT else slice(96, P)
                    prods += [(pv[:, j, :], xs[:, fs], bands[:, g, :], True, False),
                              (pv[:, j, 0:PADW], before[rows, fs], tails[rows, g, :], False, True)]
                mt = PE.mms(prods, m_x, m_bands, bk.free)
                for j in range(4):
                    k = 4 * half + j
                    if half:
                        r = V.ts(pl.ap[:, k, 0:n], pv[:, j, 0:n], col("a_norm", k), None, ALU.mult, None, mt, pl.free)
                    else:
                        r = S.copy(pl.ap[:, k, 0:n], pv[:, j, 0:n], mt, pl.free, scale=col("a_norm", k))
                bk.free = [r]
                cp.append(r)
            xb_.free = xb_.free + [mt]
            if prev is not None:
                rows_of[prev].free = [mt]
            yield
            sb_ = scaled.take()
            for half in range(2):
                bk = psum_ring.take()
                mt = PE.mms([(bk.ap[0:n, 256 * g:256 * g + 256], pl.ap[:, 4 * half + 2 * g + u, 0:n],
                              a_w[:, 4 * half + 2 * g + u, :], u == 0, u == 1) for g in range(2) for u in range(2)],
                            cp, m_aw, bk.free)
                hc = half_cols(half)
                a = V.tt(sb_.ap[0:n, hc], bk.ap[0:n, :], arow[0:n, hc], ALU.mult, mt, m_aw, sb_.free)
                bk.free = [a]
                a = G.tt(h[0:n, s, hc], h[0:n, s, hc], sb_.ap[0:n, hc], ALU.add, a)
            sb_.free = [a]
            pl.free = [mt]
            square_sum(s, junk, a)
        by_position = [NT] + list(range(NT))

        WF = KD * 2 * DE + 2 * D
        NC = KVL + ROPE + QL
        top[0] = base_b2
        w_uv = take(2, MH * VH)
        base_wo = top[0]
        w_uq = take(3, MH * (NOPE + ROPE))
        top_uq = top[0]
        w_uk = take(2, MH * NOPE)
        cqT = take(3, L)
        w_o = arena[:, base_wo:base_wo + MH * D].rearrange("p (a b) -> p a b", a=MH)
        assert base_wo + MH * D <= top[0]
        base_wc = top[0]
        wc, rope_cs = take(KD, NC), take(NS, ROPE)
        end_wc = top[0]
        assert end_wc <= base_b2 + 3 * WF
        ckvT, krT, qrT = take(2, L), take(L), take(4, L)
        base_mla = top[0]
        base_route = base_b2 + 3 * WF

        def weights_at(i):
            return arena[:, base_b2 + WF * i:base_b2 + WF * (i + 1)]

        def moe(layer, finish, load_ahead=None):
            w_ring = Ring([Buf(weights_at(i), dma_sem(f"we{i}")) for i in range(3)])

            def load_expert(e):
                b = w_ring.take()
                mk = SP.dma(b.sem, b.ap, io["w_exp"][layer * NE + e], b.free)
                return b, mk
            top[0] = base_route
            xg = Ring([Buf(take(D), dma_sem(f"xn{i}")) for i in range(3)])
            grow = take(D)
            lgT, lg = take(NS * P), take(NS, NG + NE)
            wr, br = take(KD, NG + NE), take(NG + NE)
            d_r = dma_sem("router")
            SP.dma(d_r, grow, io["rows"][3 + layer:4 + layer, :].to_broadcast([P, D]))
            SP.dma(d_r, wr, io["w_router"][layer])
            m_rw = SP.dma(d_r, br, io["b_router"][layer:layer + 1, :].to_broadcast([P, NG + NE]))
            io4, io32, io48, tokid = take(NG), take(NE), take(NBLK), take(NS)
            base_e, valid, upper = take(NE), take(NS), take(P)
            io128, tokf = take(P), take(NS)
            ci = take(P)
            a1 = G.do(lambda: G.e.iota(ci.bitcast(I32), [[1, P]], base=0, channel_multiplier=0))
            a2 = G.do(lambda: G.e.iota(tokid.bitcast(I32), [[P, NS]], base=0, channel_multiplier=1))
            G.set(valid, 1.0)
            a3 = G.set(valid[:, NT:NS], 0.0, G.last())
            G.set(valid[0:N_META, NT:NS], 1.0, a3)
            a3 = G.set(upper, 1.0)
            m_up = keep(upper, upper, [[1, P]], 0, -1, ALU.is_gt, 0.0, a3)
            V.copy(io32, ci.bitcast(I32)[:, 0:NE], a1)
            V.copy(io4, ci.bitcast(I32)[:, 0:NG])
            V.copy(io128, ci.bitcast(I32))
            V.copy(io48, ci.bitcast(I32)[:, 0:NBLK])
            c = V.copy(tokf, tokid.bitcast(I32), a2)
            m_tokf = V.tt(tokf, tokf, valid, ALU.mult, c, G.last())
            full = take(NE)
            V.ts(full, io32, float(P), float(P), ALU.mult, ALU.add, V.last())
            m_io = V.ts(base_e, io32, float(P), None, ALU.mult, None, V.last())
            assert top[0] <= base_mla
            top[0] = ARENA - NS * D
            xgT = take(KD, NS * P)
            NR = NG + NE
            done_rows, done_t, done_l = [], [], []

            def route_slot(s):
                pos, n = SLOT[s]
                yield from finish(s)
                yield
                m_r = rms(slice(s, s + 1))
                xs = xg.take()
                a = V.stt(xs.ap, h[:, s, :], rstd[:, s:s + 1], grow, ALU.mult, ALU.mult, m_r, m_rw, xs.free)
                done_rows.append(SP.dma(xs.sem, xn_dram[P * s:P * s + n, :], xs.ap[0:n, :], a))
                yield
                for half in range(2):
                    bk = psum_ring.take()
                    pv = four(bk.ap)
                    mt = PE.mms([(pv[:, k, :], xs.ap[:, P * (4 * half + k):P * (4 * half + k + 1)], ident, None, None)
                                 for k in range(4)], a, bk.free)
                    bk.free = [S.copy(xgT[:, 4 * half:4 * half + 4, P * s:P * (s + 1)], pv, mt)]
                xs.free = [mt, done_rows[-1]]
                done_t.append(S.last())
                yield
                if s % 4 == 3 or s == NT:
                    s0 = s - s % 4
                    cols = slice(P * s0, P * (s + 1))
                    bk = psum_ring.take()
                    mt = PE.mms([(bk.ap[0:NR, 0:P * (s + 1 - s0)], wr[:, k, :], xgT[:, k, cols], k == 0, k == KD - 1)
                                 for k in range(KD)], done_t[-1], m_rw, bk.free)
                    c = S.copy(lgT[0:NR, cols], bk.ap[0:NR, 0:P * (s + 1 - s0)], mt)
                    bk.free = [c]
                    bk = psum_ring.take()
                    pv = bk.ap[:, 0:NR * (s + 1 - s0)].rearrange("p (a b) -> p a b", b=NR)
                    mt = PE.mms([(pv[:, j - s0, :], lgT[0:NR, P * j:P * (j + 1)], ident[0:NR, 0:NR], None, None)
                                 for j in range(s0, s + 1)], c, bk.free)
                    c = V.tt(lg[:, s0:s + 1, :], pv, bc_mid(br, s + 1 - s0), ALU.add, mt, m_rw)
                    bk.free = [c]
                    done_l.append(c)
            pipelined(route_slot(s) for s in by_position)
            m_xn = done_rows[-3:]
            for b in w_ring.bufs:
                b.free = [lane.last() for lane in compute]
            loaded = [load_expert(e) for e in range(3)]
            stage(f"route{layer}")
            top[0] = base_mla
            marks_out.append(m_xn)
            a = done_l
            gp, m8, i8 = take(NS, 8), take(NS, 8), take(NS, 8)

            def largest(x, *after):
                found = [V.do(lambda s=s: nc.vector.max(m8[:, s, :], x[:, s, :]), after) for s in range(NS)]
                for s in range(NS):
                    V.do(lambda s=s: nc.vector.max_index(i8[:, s, :].bitcast(U32), m8[:, s, :], x[:, s, :]), found[s])
            b = V.set(gp, NEG)
            b = V.copy(gp[:, :, 0:NG], lg[:, :, 0:NG], a, b)
            largest(gp, b)
            a = V.last()
            eg, wg, gi = take(NS, NG), take(NS), take(NS)
            c = V.tt(eg, lg[:, :, 0:NG], m8[:, :, 0:1].to_broadcast([P, NS, NG]), ALU.subtract, a)
            c = S.act(eg, eg, ACT.Exp, c)
            c = V.red(wg, eg, ALU.add, c)
            c = V.recip(wg, wg, c)
            c = V.copy(gi, i8[:, :, 0:1].rearrange("p a b -> p (a b)").bitcast(U32), c)
            pen = take(NS, NG)
            c = V.tt(pen, bc_mid(io4, NS), bc_last(gi, NG), ALU.is_equal, c, m_io)
            c = V.ts(pen, pen, -NEG, NEG, ALU.mult, ALU.add, c)
            me = take(NS, NE)
            c = V.tt(me.rearrange("p s (g e) -> p s g e", g=NG), lg[:, :, NG:].rearrange("p s (g e) -> p s g e", g=NG),
                     pen.unsqueeze(3).to_broadcast([P, NS, NG, EPG]), ALU.add, c)
            largest(me, c)
            a = V.last()
            e1, rr, ei = take(NS), take(NS), take(NS, 2)
            v0, v1 = (m8[:, :, j:j + 1].rearrange("p a b -> p (a b)") for j in range(2))
            c = V.tt(e1, v1, v0, ALU.subtract, a)
            c = S.act(e1, e1, ACT.Exp, c)
            c = V.ts(rr, e1, 1.0, None, ALU.add, None, c)
            c = V.recip(rr, rr, c)
            c = V.tt(rr, rr, wg, ALU.mult, c)
            V.copy(gates[:, :, 0:1], rr.unsqueeze(2), c)
            V.tt(gates[:, :, 1:2], rr.unsqueeze(2), e1.unsqueeze(2), ALU.mult)
            c = V.copy(ei, i8[:, :, 0:2].bitcast(U32))
            oh, both, before = [take(NS, NE) for _ in range(2)], take(NS, NE), take(NS + 1, NE)
            for j in range(2):
                b = V.tt(oh[j], bc_mid(io32, NS), ei[:, :, j:j + 1].to_broadcast([P, NS, NE]), ALU.is_equal, c)
                b = V.tt(oh[j], oh[j], bc_last(valid, NE), ALU.mult, b, G.last())
            m_oh = V.tt(both, oh[0], oh[1], ALU.add, b)
            z = V.set(before[:, 0, :], 0.0)
            for s in range(NS):
                z = V.tt(before[:, s + 1, :], before[:, s, :], both[:, s, :], ALU.add, z, m_oh)
            bk = psum_ring.take()
            flat = [t.rearrange("p a b -> p (a b)")[:, 0:NS * NE] for t in (both, before)]
            mt = PE.mms([(bk.ap[:, 0:NS * NE], upper, flat[0], True, False),
                         (bk.ap[:, 0:NS * NE], ones, flat[1], False, True)], z, m_up, bk.free)
            rank, over, slot = (lgT[:, NS * NE * j:NS * NE * (j + 1)].rearrange("p (a b) -> p a b", a=NS) for j in range(3))
            bk.free = [V.copy(rank, bk.ap[:, 0:NS * NE].rearrange("p (a b) -> p a b", a=NS), mt)]
            bk = psum_ring.take()
            mt = PE.mms([(bk.ap[:, 0:NE], ones, before[:, NS, :], True, True)], bk.free)
            cnt, nb, cum, dif = (take(NE) for _ in range(4))
            a = V.copy(cnt, bk.ap[:, 0:NE], mt)
            bk.free = [a]
            n_more = (L - 1) // P
            more = take(NE, n_more)
            a = V.tt(more, bc_last(cnt, n_more), bc_mid(full[:, 0:n_more], NE), ALU.is_gt, a, m_io)
            a = V.red(nb, more, ALU.add, a)
            a = V.do(lambda: nc.vector.tensor_tensor_scan(cum, ones[:, 0:NE], nb, 0.0, ALU.mult, ALU.add), a)
            m_cum = a
            a = V.tt(dif, cum, nb, ALU.subtract, a)
            a = V.ts(dif, dif, float(P), float((NE - 1) * P), ALU.mult, ALU.add, a)
            a = V.tt(dif, dif, base_e, ALU.subtract, a)
            b = V.ts(over, rank, float(P), None, ALU.is_ge, None, a)
            b = V.tt(over, over, bc_mid(dif, NS), ALU.mult, b)
            c = V.tt(slot, rank, bc_mid(base_e, NS), ALU.add, b)
            c = V.tt(slot, slot, over, ALU.add, c)
            df = take(NS, 2)
            for j in range(2):
                b = V.tt(oh[j], oh[j], slot, ALU.mult, c)
                V.red(df[:, :, j:j + 1], oh[j], ALU.add, b)
            m_dest = V.copy(dest.bitcast(I32), df, V.last())
            ovx, ovs = take(NOV, NE), take(NOV)
            a = V.tt(ovx[0:1], bc_last(io48[0:1, 0:NOV], NE), bc_mid(cum[0:1], NOV), ALU.is_ge, m_cum)
            a = V.red(ovs[0:1], ovx[0:1], ALU.add, a)
            a = V.ts(ovs[0:1], ovs[0:1], float(NE - 1), None, ALU.min, None, a)
            V.copy(counts.bitcast(I32)[0:1, 1:1 + NOV], ovs[0:1], a)
            m_cnt = V.copy(counts.bitcast(I32)[0:1, 0:1], cum[0:1, NE - 1:NE])
            rowi, blki, rowf, blkf = (take(NS, 2) for _ in range(4))
            destf = dest.rearrange("p a b -> p (a b)").bitcast(I32)
            V.ts(rowi.rearrange("p a b -> p (a b)").bitcast(I32), destf, P - 1, None, ALU.bitwise_and, None, m_dest)
            b = V.ts(blki.rearrange("p a b -> p (a b)").bitcast(I32), destf, 7, None, ALU.logical_shift_right, None)
            V.copy(rowf, rowi.bitcast(I32), b)
            b = V.copy(blkf, blki.bitcast(I32))
            dead = xgT.rearrange("p a b -> p (a b)")
            blk1 = [dead[:, NS * NBLK * j:NS * NBLK * (j + 1)].rearrange("p (a b) -> p a b", a=NS) for j in range(2)]
            for j in range(2):
                c = V.tt(blk1[j], bc_mid(io48, NS), blkf[:, :, j:j + 1].to_broadcast([P, NS, NBLK]), ALU.is_equal, b)
                V.tt(blk1[j], blk1[j], bc_last(tokf, NBLK), ALU.mult, c, m_tokf)
            m_blk = V.last()
            bk = psum_ring.take()
            row1 = Ring([Buf(dead[:, 2048 + P * i:2048 + P * (i + 1)]) for i in range(2 * NS)])
            for s in range(NS):
                for j in range(2):
                    r1 = row1.take()
                    c = V.ts(r1.ap, io128, rowf[:, s, j:j + 1], None, ALU.is_equal, None, b, r1.free)
                    mt = PE.mms([(bk.ap[:, 0:NBLK], r1.ap, blk1[j][:, s, :], s + j == 0, (s, j) == (NS - 1, 1))],
                                c, m_blk, bk.free)
                    r1.free = [mt]
            bk.free = [V.copy(idx.bitcast(I32), bk.ap[:, 0:NBLK], mt)]
            m_idx = V.last()

            barrier()
            stage(f"experts{layer}")
            top[0] = base_route
            w_ring.bufs.append(Buf(take(WF), dma_sem("we3")))
            xe_ring = Ring([Buf(take(D), dma_sem(f"xe{i}")) for i in range(3)])
            xt_ring = Ring([Buf(take(KD, P)) for _ in range(2)])
            g_ring = Ring([Buf(take(DE)) for _ in range(2)])
            h_ring = Ring([Buf(take(DE)) for _ in range(2)])
            ht_ring = Ring([Buf(take(2, P)) for _ in range(2)])
            y_ring = Ring([Buf(take(D), dma_sem(f"y{i}")) for i in range(3)])

            def gather(block):
                xe = xe_ring.take()
                G.wait([m_idx, m_xn, xe.free])
                sem, ap = xe.sem, xe.ap
                G.queue.append(lambda: G.e.indirect_dma_start(
                    out=ap, out_offset=None, in_=xn_dram[:, :],
                    in_offset=bass.IndirectOffsetOnAxis(idx.bitcast(I32)[:, block:block + 1], 0)).then_inc(sem.sem, 16))
                return xe, sem.next()

            def turn_rows(xe, m_xe):
                xt = xt_ring.take()
                cp = []
                for half in range(2):
                    bk = psum_ring.take()
                    mt = PE.mms([(four(bk.ap)[:, k, :], xe.ap[:, P * (4 * half + k):P * (4 * half + k + 1)], ident, None, None)
                                 for k in range(4)], m_xe, bk.free)
                    bk.free = [(S if half else V).copy(xt.ap[:, 4 * half:4 * half + 4, :], four(bk.ap), mt, xt.free)]
                    cp.append(bk.free[0])
                xe.free = [mt]
                return xt, cp

            def gate_up(xt, cp, w, m_w):
                wv = w.ap[:, 0:KD * 2 * DE].rearrange("p (a b) -> p a b", a=KD)
                bk = psum_ring.take()
                mt = PE.mms([(bk.ap, xt.ap[:, k, :], wv[:, k, :], k == 0, k == KD - 1) for k in range(KD)], cp, m_w, bk.free)
                xt.free = [mt]
                g, hb = g_ring.take(), h_ring.take()
                a = S.act(g.ap, bk.ap[:, 0:DE], ACT.Sigmoid, mt, g.free)
                a = V.tt(g.ap, bk.ap[:, 0:DE], g.ap, ALU.mult, a)
                a = V.tt(hb.ap, bk.ap[:, DE:2 * DE], g.ap, ALU.mult, a, hb.free)
                bk.free, g.free = [a], [a]
                return hb, a

            def turn_hidden(hb, m_h):
                bk = psum_ring.take()
                mt = PE.mms([(four(bk.ap)[:, k, :], hb.ap[:, P * k:P * (k + 1)], ident, None, None) for k in range(2)],
                            m_h, bk.free)
                hb.free = [mt]
                ht = ht_ring.take()
                a = S.copy(ht.ap, four(bk.ap)[:, 0:2, :], mt, ht.free)
                bk.free = [a]
                return ht, a

            def down(ht, a, w, block):
                wv = w.ap[:, KD * 2 * DE:].rearrange("p (a b) -> p a b", a=2)
                y = y_ring.take()
                cp = []
                for half in range(2):
                    bk = psum_ring.take()
                    mt = PE.mms([(bk.ap, ht.ap[:, k, :], wv[:, k, half_cols(half)], k == 0, k == 1) for k in range(2)], a, bk.free)
                    bk.free = [(S if half else V).copy(y.ap[:, half_cols(half)], bk.ap, mt, y.free)]
                    cp.append(bk.free[0])
                ht.free = [mt]
                w.free = [mt]
                y.free = [SP.dma(y.sem, y_dram[P * block:P * (block + 1), :], y.ap, cp)]
                return y.free[0]

            gathered = [gather(0), gather(1)]
            SP.wait([m_xe for _, m_xe in gathered])
            loaded.append(load_expert(3))
            turned = turn_rows(*gathered[0])
            last_block = None
            for e in range(NE):
                w, m_w = loaded[e]
                hb, m_h = gate_up(*turned, w, m_w)
                if last_block:
                    ht = turn_hidden(*last_block[0:2])
                if e + 2 < NE:
                    gathered.append(gather(e + 2))
                if e + 1 < NE:
                    turned = turn_rows(*gathered[e + 1])
                if last_block:
                    down(*ht, *last_block[2:])
                    if e + 3 < NE:
                        loaded.append(load_expert(e + 3))
                    if load_ahead:
                        load_ahead(e - 1)
                last_block = (hb, m_h, w, e)
            down(*turn_hidden(*last_block[0:2]), *last_block[2:])
            m_y = [b.free for b in y_ring.bufs]

            barrier()
            loads = {}

            def enter(lane):
                lane.queue.append(lambda: loads.__setitem__(lane, lane.e.value_load(counts.bitcast(I32)[0:1, 0:1],
                                                                                   min_val=0, max_val=NOV)))
            for lane in lanes:
                lane.wait([m_cnt])
                enter(lane)
            stage(f"over{layer}")
            for kind, r in (("rows", xe_ring), ("y", y_ring), ("w", w_ring)):
                del r.bufs[:-1]
                r.bufs[0].sem, r.bufs[0].free = dsem(f"over{layer}_{kind}"), []
            for r in (xt_ring, g_ring, h_ring, ht_ring):
                for b in r.bufs:
                    b.free = []
            outer = {lane: (lane.queue, dict(lane.waited)) for lane in lanes}
            for blk in range(NOV):
                for lane in lanes:
                    lane.queue = []
                wb_ = w_ring.take()
                SP.wait(wb_.free)
                sem = wb_.sem

                def load_w(blk=blk, wb_=wb_, sem=sem):
                    ex = SP.e.value_load(counts.bitcast(I32)[0:1, 1 + blk:2 + blk], min_val=0, max_val=NE - 1)
                    SP.e.dma_start(wb_.ap, io["w_exp"][bass.ds(ex + layer * NE, 1)].rearrange("a p n -> (a p) n")).then_inc(sem.sem, 16)
                SP.queue.append(load_w)
                m_w = sem.next()
                xe, m_xe = gather(NE + blk)
                hb, m_h = gate_up(*turn_rows(xe, m_xe), wb_, m_w)
                m_yo = down(*turn_hidden(hb, m_h), wb_, NE + blk)
                S.wait([m_yo])
                for lane in lanes:
                    sub = lane.queue
                    lane.queue = outer[lane][0]

                    def branch(lane=lane, sub=sub, blk=blk):
                        with lane.e.If(loads[lane] > blk):
                            lane.play(sub)
                    lane.queue.append(branch)
            for lane in lanes:
                lane.waited = outer[lane][1]
            stage(f"joined{layer}")
            SP.dma(dma_sem("sp_joined"), scr[:, 8:10], io["chan"][:, 0:2])
            joined = [V.set(scr[:, 0:2], 0.0), G.set(scr[:, 2:4], 0.0), S.copy(scr[:, 4:6], ident[:, 0:2])]
            joined.append(PE.mms([(banks[0][:, 0:2], ident, ident[:, 0:2], True, True)], joined))
            for lane in lanes:
                lane.wait(joined)
            for b in psum_ring.bufs:
                b.free = []


            def combiner(c_ring, junk):
                def combine(s):
                    pos, n = SLOT[s]
                    for j in range(2):
                        cb = c_ring.take()
                        G.wait([m_y, cb.free])
                        G.queue.append(lambda s=s, j=j, n=n, cb=cb: G.e.indirect_dma_start(
                            out=cb.ap[0:n, :], out_offset=None, in_=y_dram[:, :],
                            in_offset=bass.IndirectOffsetOnAxis(dest.bitcast(I32)[0:n, s, j:j + 1], 0)
                        ).then_inc(cb.sem.sem, 16))
                        mk = cb.sem.next()
                        cb.free = [V.stt(h[0:n, s, :], cb.ap[0:n, :], gates[0:n, s, j:j + 1], h[0:n, s, :], ALU.mult,
                                         ALU.add, mk, V.last())]
                    return square_sum(s, junk, V.last())
                return combine
            return combiner

        d_lc, d_lu = dsem("latent_c"), dsem("latent_u")

        def load_latent(e):
            if e == NE - 3:
                assert top_uq <= base_b2 + 2 * WF
                SP.dma(d_lu, w_uv, io["w_uv"], PE.last())
                SP.dma(d_lu, w_uq, io["w_uq"])
            if e == NE - 2:
                SP.dma(d_lu, w_uk, io["w_uk"], PE.last())
                SP.dma(d_lc, wc, io["w_c"])
                SP.dma(d_lc, rope_cs, io["rope"])

        def scale_latent():
            m_lc, m_lu = Mark(d_lc.sem, d_lc.value), Mark(d_lu.sem, d_lu.value)
            for k in range(KD):
                S.copy(wc[:, k, 0:KVL + ROPE], wc[:, k, 0:KVL + ROPE], m_lc, scale=col("kv_norm", k))
                S.copy(wc[:, k, KVL + ROPE:], wc[:, k, KVL + ROPE:], scale=col("b_norm", k))
            m_c = S.last()
            for k in range(3):
                V.ts(w_uq[:, k, :], w_uq[:, k, :], col("q_norm", k), None, ALU.mult, None, m_lu)
            for w_ in (w_uk, w_uv):
                for k in range(2):
                    V.ts(w_[:, k, :], w_[:, k, :], col("kv_lat", k), None, ALU.mult, None)
            return m_c, V.last()

        combiner = moe(0, lambda s: pool_slot(s, by_position[by_position.index(s) - 1] if s != NT else None), load_latent)

        stage("latent")
        top[0] = base_mla
        H2 = ROPE // 2
        sets = [dict(xn=take(D), xt=take(KD, P), c=take(NC), rs=take(2), kr=take(P), rt=[take(H2) for _ in range(4)],
                     qt=take(MH * ROPE), qr=take(MH * ROPE), tm=[take(MH * H2) for _ in range(4)]) for _ in range(2)]
        for own in sets:
            own["free"] = {k: [] for k in own}
        junk = take(D)
        m_w, m_wu = scale_latent()
        combine = combiner(Ring([Buf(take(D), dma_sem(f"c{i}")) for i in range(4)]), junk)

        def rotate(dst, x, cs, tm, *after):
            x1, x2, o1, o2 = x[0], x[1], dst[0], dst[1]
            b = [V.tt(tm[0], x1, cs[0], ALU.mult, after), V.tt(tm[1], x2, cs[1], ALU.mult),
                 V.tt(tm[2], x1, cs[1], ALU.mult), V.tt(tm[3], x2, cs[0], ALU.mult)]
            V.tt(o1, tm[0], tm[1], ALU.subtract, b)
            return V.tt(o2, tm[2], tm[3], ALU.add)

        def latent_slot(s):
            pos, n = SLOT[s]
            own = sets[s % 2]
            free = own["free"]
            idn = ident[0:n, 0:n]
            xs, xtv, c_, r2, k_ = own["xn"], own["xt"], own["c"], own["rs"], own["kr"]
            combine(s)
            yield
            m_r = rms(slice(s, s + 1))
            a = V.ts(xs, h[:, s, :], rstd[:, s:s + 1], None, ALU.mult, None, m_r, free["xn"])
            yield
            cp = []
            for half in range(2):
                bk = psum_ring.take()
                mt = PE.mms([(four(bk.ap)[:, k, 0:n], xs[0:n, P * (4 * half + k):P * (4 * half + k + 1)], idn, None, None)
                             for k in range(4)], a, bk.free)
                bk.free = [(S if half else V).copy(xtv[:, 4 * half:4 * half + 4, 0:n], four(bk.ap)[:, :, 0:n], mt, free["xt"])]
                cp.append(bk.free[0])
            free["xn"] = [mt]
            yield
            for c0, c1 in ((KVL + ROPE, NC), (0, KVL + ROPE)):
                bk = psum_ring.take()
                mt = PE.mms([(bk.ap[0:n, 0:c1 - c0], xtv[:, k, 0:n], wc[:, k, c0:c1], k == 0, k == KD - 1)
                             for k in range(KD)], cp, m_w, bk.free)
                bk.free = [S.copy(c_[0:n, c0:c1], bk.ap[0:n, 0:c1 - c0], mt, free["c"])]
            free["xt"] = [mt]
            a = S.last()
            b = S.act(junk[0:n, 0:KVL], c_[0:n, 0:KVL], ACT.Square, a, accum=r2[0:n, 0:1])
            b = S.act(junk[0:n, 0:QL], c_[0:n, KVL + ROPE:], ACT.Square, b, accum=r2[0:n, 1:2])
            S.act(r2[0:n, 0:1], r2[0:n, 0:1], ACT.Sqrt, b, bias=eps_rms[0:n, :], scale=1.0 / KVL)
            b = S.act(r2[0:n, 1:2], r2[0:n, 1:2], ACT.Sqrt, bias=eps_rms[0:n, :], scale=1.0 / QL)
            yield
            b = V.recip(r2[0:n, :], r2[0:n, :], b)
            V.ts(c_[0:n, 0:KVL], c_[0:n, 0:KVL], r2[0:n, 0:1], None, ALU.mult, None, b)
            m_c = V.ts(c_[0:n, KVL + ROPE:], c_[0:n, KVL + ROPE:], r2[0:n, 1:2], None, ALU.mult, None)
            cs = (rope_cs[0:n, s, 0:H2], rope_cs[0:n, s, H2:])
            a = rotate((k_[0:n, 0:H2], k_[0:n, H2:ROPE]), (c_[0:n, KVL:KVL + H2], c_[0:n, KVL + H2:KVL + ROPE]), cs,
                       [r[0:n, :] for r in own["rt"]], m_c, free["kr"])
            m_k = V.copy(k_[0:n, ROPE:2 * ROPE], k_[0:n, 0:ROPE], a)
            yield
            bk = psum_ring.take()
            mt = PE.mms([(four(bk.ap)[:, j, 0:n], c_[0:n, KVL + ROPE + P * j:KVL + ROPE + P * (j + 1)], idn, None, None)
                         for j in range(3)], m_c, bk.free)
            m_cq = V.copy(cqT[:, :, pos:pos + n], four(bk.ap)[:, 0:3, 0:n], mt)
            bk.free = [m_cq]
            bk = psum_ring.take()
            pv = four(bk.ap)
            srcs = [c_[0:n, 0:P], c_[0:n, P:2 * P], k_[0:n, :]]
            mt = PE.mms([(pv[:, j, 0:n], x_, idn, None, None) for j, x_ in enumerate(srcs)], m_k, bk.free)
            S.copy(ckvT[:, :, pos:pos + n], pv[:, 0:2, 0:n], mt)
            bk.free = [S.copy(krT[:, pos:pos + n], pv[:, 2, 0:n])]
            free["c"], free["kr"] = [mt], [mt]
            yield
            bk = psum_ring.take()
            mt = PE.mms([(bk.ap[0:n, :], cqT[:, k, pos:pos + n], w_uq[:, k, MH * NOPE:], k == 0, k == 2) for k in range(3)],
                        m_cq, m_wu, bk.free)
            m_qt = S.copy(own["qt"][0:n, :], bk.ap[0:n, :], mt, free["qt"])
            bk.free = [m_qt]
            yield

            def halves(t):
                v = t[0:n, :].rearrange("p (h u c) -> p u h c", u=2, c=H2)
                return v[:, 0], v[:, 1]
            cs = (bc_mid(rope_cs[0:n, s, 0:H2], MH), bc_mid(rope_cs[0:n, s, H2:], MH))
            a = rotate(halves(own["qr"]), halves(own["qt"]), cs,
                       [t_[0:n, :].rearrange("p (h c) -> p h c", h=MH) for t_ in own["tm"]], m_qt, free["qr"])
            free["qt"] = [a]
            yield
            bk = psum_ring.take()
            pv = four(bk.ap)
            mt = PE.mms([(pv[:, j, 0:n], own["qr"][0:n, P * j:P * (j + 1)], idn, None, None) for j in range(4)], a, bk.free)
            free["qr"] = [mt]
            bk.free = [S.copy(qrT[:, :, pos:pos + n], pv[:, :, 0:n], mt)]
        pipelined(latent_slot(s) for s in range(NS))

        barrier()
        stage("mla")
        top[0] = base_wc
        vv = [take(NS, 2 * VH) for _ in range(2)]
        Pb = [take(L)]
        assert top[0] <= end_wc
        top[0] = base_mla
        oT = take(MH, L)
        qn, kn = [take(L) for _ in range(2)], [take(L) for _ in range(2)]
        Pb += [take(L) for _ in range(2)]
        PTb = [take(NS, P) for _ in range(2)]
        causal = take(P)
        a = G.set(causal, 0.0)
        m_cau = keep(causal, causal, [[-1, P]], 0, 1, ALU.is_ge, NEG, a)
        sm = [[take(2), take(2), take(1)] for _ in range(4)]
        score_ring = Ring([Buf(psum[:, 1024 * i:1024 * (i + 1)]) for i in range(2)])
        side_ring = Ring([Buf(banks[4 + i]) for i in range(4)])
        qk_free, vv_free = [[], []], [[], []]
        p_free, pt_free = [[], [], []], [[], []]
        m_qk, m_vv = [None] * MH, [None] * (MH // 2)
        order = [NT] + list(range(NT))

        def value_steps(pair):
            def step(s, pos, n):
                bk = side_ring.take()
                mt = PE.mms([(bk.ap[0:n, 0:2 * VH], ckvT[:, k, pos:pos + n], w_uv[:, k, 2 * VH * pair:2 * VH * (pair + 1)],
                              k == 0, k == 1) for k in range(2)], bk.free)
                bk.free = [S.copy(vv[pair % 2][0:n, s, :], bk.ap[0:n, 0:2 * VH], mt, vv_free[pair % 2])]
                m_vv[pair] = S.last()
            return [lambda s=s, pos=pos, n=n: step(s, pos, n) for s, (pos, n) in enumerate(SLOT)]

        def qk_steps(hh):
            def step(dst, w_, src, nk, c0, c1):
                bk = side_ring.take()
                mt = PE.mms([(bk.ap[:, 0:c1 - c0], w_[:, k, P * hh:P * (hh + 1)], src[:, k, c0:c1], k == 0, k == nk - 1)
                             for k in range(nk)], bk.free)
                bk.free = [S.copy(dst[hh % 2][:, c0:c1], bk.ap[:, 0:c1 - c0], mt, qk_free[hh % 2])]
                m_qk[hh] = S.last()
            return [lambda dst=dst, w_=w_, src=src, nk=nk, c0=c0: step(dst, w_, src, nk, c0, min(L, c0 + 512))
                    for dst, w_, src, nk in ((qn, w_uq, cqT, 3), (kn, w_uk, ckvT, 2)) for c0 in range(0, L, 512)]

        def attend(hh, qi, it):
            s = order[qi]
            pos, n = SLOT[s]
            pr = slice(64 * (hh % 2), 64 * (hh % 2) + 64)
            kc = pos + n
            pb, ptb, (mx, rsu, rdn) = Pb[it % 3], PTb[it % 2], sm[it % 4]
            sc = score_ring.take()
            parts = [(sc, 0, min(kc, 1024))]
            if kc > 1024:
                parts.append((side_ring.take(), 1024, kc))
            prods = []
            for buf, p0, p1 in parts:
                for c0 in range(p0, p1, 512):
                    c1 = min(p1, c0 + 512)
                    o = buf.ap[0:n, c0 - p0:c1 - p0]
                    prods += [(o, qn[hh % 2][:, pos:pos + n], kn[hh % 2][:, c0:c1], True, False),
                              (o, qrT[pr, hh // 2, pos:pos + n], krT[pr, c0:c1], False, True)]
            mt = PE.mms(prods, m_qk[hh], [buf.free for buf, _, _ in parts])
            qk_free[hh % 2] = [mt]
            rd = []
            for u, (buf, p0, p1) in enumerate(parts):
                c0 = max(pos, p0)
                o = buf.ap[0:n, c0 - p0:p1 - p0]
                a = V.tt(o, o, causal[0:n, c0 - pos:p1 - pos], ALU.add, mt, m_cau)
                rd.append(V.red(mx[0:n, u:u + 1], buf.ap[0:n, 0:p1 - p0], ALU.max, a))
            a = rd
            if len(parts) > 1:
                a = V.tt(mx[0:n, 0:1], mx[0:n, 0:1], mx[0:n, 1:2], ALU.max, a)
            a = V.ts(mx[0:n, 0:1], mx[0:n, 0:1], -SCALE, None, ALU.mult, None, a)
            for u, (buf, p0, p1) in enumerate(parts):
                e = S.act(pb[0:n, p0:p1], buf.ap[0:n, 0:p1 - p0], ACT.Exp, a, p_free[it % 3], bias=mx[0:n, 0:1], scale=SCALE,
                          accum=rsu[0:n, u:u + 1])
                buf.free = [e]
            yield
            if len(parts) > 1:
                e = V.tt(rsu[0:n, 0:1], rsu[0:n, 0:1], rsu[0:n, 1:2], ALU.add, e)
            a = V.recip(rdn[0:n, :], rsu[0:n, 0:1], e)
            a = V.ts(pb[0:n, 0:kc], pb[0:n, 0:kc], rdn[0:n, :], None, ALU.mult, None, a)
            yield
            keys = order[:qi + 1]
            cp = []
            for j0 in range(0, len(keys), 4):
                ks_ = keys[j0:j0 + 4]
                bk = side_ring.take()
                pv = four(bk.ap)
                prods = []
                for j, ks in enumerate(ks_):
                    kp, kn_ = SLOT[ks]
                    prods.append((pv[0:kn_, j, 0:n], pb[0:n, kp:kp + kn_], ident[0:n, 0:n], None, None))
                mt = PE.mms(prods, a, bk.free)
                if j0 == 0:
                    S.copy(ptb[0:N_META, 0, 0:n], pv[0:N_META, 0, 0:n], mt, pt_free[it % 2])
                    if len(ks_) > 1:
                        S.copy(ptb[:, 1:len(ks_), 0:n], pv[:, 1:len(ks_), 0:n], mt)
                    bk.free = [S.last()]
                else:
                    bk.free = [V.copy(ptb[:, j0:j0 + len(ks_), 0:n], pv[:, 0:len(ks_), 0:n], mt, pt_free[it % 2])]
                cp.append(bk.free[0])
            p_free[it % 3] = [mt]
            yield
            bk = side_ring.take()
            vh = VH * (hh % 2)
            mt = PE.mms([(bk.ap[:, 0:n], vv[hh // 2 % 2][0:SLOT[ks][1], ks, vh:vh + VH], ptb[0:SLOT[ks][1], j, 0:n],
                          j == 0, j == len(keys) - 1) for j, ks in enumerate(keys)], cp, m_vv[hh // 2], bk.free)
            pt_free[it % 2] = [mt]
            vv_free[hh // 2 % 2] = [mt]
            bk.free = [S.copy(oT[:, hh, pos:pos + n], bk.ap[:, 0:n], mt)]

        TURNS = [NS - 1 - i // 2 if i % 2 == 0 else i // 2 for i in range(NS)]

        def heads_in_turn():
            for make in value_steps(0) + qk_steps(0):
                make()
            for hh in range(MH):
                pair = hh // 2
                if hh % 2 == 0 and pair + 1 < MH // 2:
                    values = value_steps(pair + 1)
                nexts = qk_steps(hh + 1) if hh + 1 < MH else []
                for turn, qi in enumerate(TURNS):
                    if nexts:
                        nexts.pop(0)()
                    if values and (hh % 2 or turn >= 4):
                        values.pop(0)()
                    yield attend(hh, qi, NS * hh + turn)
                if hh + 2 == MH:
                    heads_done.append(SP.dma(dma_sem("w_o"), w_o, io["w_o"], PE.last()))
        heads_done = []
        pipelined(heads_in_turn())
        barrier()
        stage("out2")
        m_wo = heads_done
        top[0] = base_b2
        junk = take(D)
        assert top[0] <= base_wo

        def attended(s):
            pos, n = SLOT[s]
            for half in range(2):
                bk = psum_ring.take()
                mt = PE.mms([(bk.ap[0:n, :], oT[:, k, pos:pos + n], w_o[:, k, half_cols(half)], k == 0, k == MH - 1)
                             for k in range(MH)], m_wo, bk.free)
                bk.free = [V.tt(h[0:n, s, half_cols(half)], h[0:n, s, half_cols(half)], bk.ap[0:n, :], ALU.add, mt)]
            square_sum(s, junk, V.last())
            yield

        combiner = moe(1, attended)

        stage("final")
        top[0] = base_b2
        junk, grow = take(D), take(D)
        combine = combiner(Ring([Buf(take(D), dma_sem(f"c{i}")) for i in range(8)]), junk)
        o_ring = Ring([Buf(take(D), dma_sem(f"out{i}")) for i in range(3)])
        m_g = SP.dma(dma_sem("final_row"), grow, io["rows"][5:6, :].to_broadcast([P, D]))

        def final_slot(s):
            combine(s)
            yield
            yield
            m_r = rms(slice(s, s + 1))
            ob = o_ring.take()
            a = V.stt(ob.ap, h[:, s, :], rstd[:, s:s + 1], grow, ALU.mult, ALU.mult, m_r, m_g, ob.free)
            ob.free = [SP.dma(ob.sem, io["out"][P * s:P * (s + 1), :], ob.ap, a)]
            marks_out.append(ob.free[0])
        pipelined(final_slot(s) for s in range(NT))
        SP.wait(marks_out)

        block = ctx.enter_context(nc.Block())

        @block.tensor
        def _(e):
            PE.play()

        @block.vector
        def _(e):
            V.play()

        @block.scalar
        def _(e):
            S.play()

        @block.gpsimd
        def _(e):
            G.play()

        @block.sync
        def _(e):
            SP.play()


def kernel(**inputs):
    import numpy as _np
    import concourse.bacc as _bacc
    from concourse import mybir as _mybir
    from concourse.bass_utils import run_bass_kernel_spmd as _run

    a = {k: _np.asarray(v) for k, v in inputs.items()}

    def ktile(w):
        return _np.ascontiguousarray(w.reshape(-1, P, w.shape[-1]).transpose(1, 0, 2))

    arrays = {"x": a["x"][0], "meta": a["meta_tokens_2"], "sinks": a["attn_sinks"]}
    for name, c0, n in GROUPS:
        arrays["w_in_" + name] = ktile(a["w_in"][0][:, c0:c0 + n])
    arrays["w_out"] = ktile(a["w_out"][0])
    arrays["lru_wa"], arrays["lru_wx"] = a["lru_wa"][0], a["lru_wx"][0]
    arrays["w2a2"] = _np.concatenate([a["rwkv_w2"][0], a["rwkv_a2"][0]], axis=0)

    def cols(v):
        return v.reshape(-1, P).T
    mu = a["rwkv_mu"][0]
    mu_wa = _np.zeros((P, 1), mu.dtype)
    mu_wa[0:HD, 0] = mu[3 * 256:]
    chan = [a["conv_w"][0].reshape(4, 2, P).transpose(2, 1, 0).reshape(P, 8), cols(a["conv_b"]), cols(a["lru_ba"]),
            cols(a["lru_bx"]), cols(a["lru_lambda"]), cols(mu[0:3 * 256]), mu_wa, cols(a["rwkv_w0"]), cols(a["rwkv_a0"]),
            cols(a["rwkv_kk"]), cols(a["rwkv_ka"]), cols(a["rwkv_rk"]), cols(a["rwkv_gn_w"]), cols(a["rwkv_gn_b"]),
            cols(a["a_norm_2"]), cols(a["kv_norm_2"]), cols(a["b_norm_2"]), cols(a["b_q_norm_2"]), cols(a["kv_lat_norm_2"])]
    arrays["chan"] = _np.concatenate(chan, axis=1)
    arrays["rows"] = _np.stack([a["ln_g"][0], a["ln_b"][0], a["a_scale_2"][0], a["ffn_norm_2"][0], a["ffn_norm_2"][1],
                                a["final_norm_2"]])
    arrays["a_w"] = ktile(a["a_w_2"][0].reshape(D, 256))
    arrays["w_router"] = _np.stack([ktile(_np.concatenate([a["router_g_2"][i], a["router_e_2"][i]], axis=1)) for i in range(2)])
    arrays["b_router"] = _np.concatenate([a["router_g_bias_2"], a["router_e_bias_2"]], axis=1)
    gu = _np.concatenate([a["w_gate_2"], a["w_up_2"]], axis=3).reshape(2 * NE, KD, P, 2 * DE).transpose(0, 2, 1, 3)
    dn = a["w_down_2"].reshape(2 * NE, 2, P, D).transpose(0, 2, 1, 3)
    arrays["w_exp"] = _np.concatenate([gu.reshape(2 * NE, P, -1), dn.reshape(2 * NE, P, -1)], axis=2)
    arrays["w_c"] = ktile(_np.concatenate([a["w_dkv_2"], a["b_w_dq_2"][0]], axis=1))
    uq = a["b_w_uq_2"][0]
    arrays["w_uq"] = ktile(_np.concatenate([uq[:, :, :NOPE].reshape(QL, -1), uq[:, :, NOPE:].reshape(QL, -1)], axis=1))
    arrays["w_uk"] = ktile(a["w_uk_2"].reshape(KVL, -1))
    arrays["w_uv"] = ktile(a["w_uv_2"].reshape(KVL, -1))
    arrays["w_o"] = ktile(a["b_w_o_2"][0])
    freq = (_np.float32(10000.0) ** (-_np.arange(0, ROPE, 2, dtype=_np.float32) / _np.float32(ROPE))).astype(_np.float32)
    ang = _np.arange(L, dtype=_np.float32)[:, None] * freq[None, :]
    table = _np.concatenate([_np.cos(ang), _np.sin(ang)], axis=1).astype(_np.float32)
    rope = _np.zeros((P, NS, ROPE), _np.float32)
    for s, (pos, n) in enumerate(SLOT):
        rope[0:n, s] = table[pos:pos + n]
    arrays["rope"] = rope

    nc = _bacc.Bacc("TRN2", target_bir_lowering=False, num_devices=1)
    arrays = {f"in_{k}": _np.ascontiguousarray(v) for k, v in arrays.items()}
    io = {k[3:]: nc.dram_tensor(k, v.shape, _mybir.dt.from_np(v.dtype), kind="ExternalInput").ap() for k, v in arrays.items()}
    io["out"] = nc.dram_tensor("out_0", (T, D), _mybir.dt.float32, kind="ExternalOutput").ap()
    build(nc, io)
    r = _run(nc, [arrays], core_ids=[0])
    return r.results[0]["out_0"].reshape(1, T, D)
```
